# Optimizing a Trainium2 kernel written in Bass

```python
import jax, jax.numpy as jnp
from jax import lax
import numpy as np

D_MODEL = 1024
BATCH = 1
SEQ = 256
DEPTH = 2
DEC_BATCH = 1
DEC_SEQ = 32
PAST_LEN = 256

CHUNK = 64
A_CHUNK = 128
A_WIDTH = D_MODEL // 2
A_GROUPS = 4
A_GROUP_DIM = A_WIDTH // A_GROUPS
B_HEAD_DIM = 64
B_HEADS = D_MODEL // 128
B_WIDTH = B_HEADS * B_HEAD_DIM
B_PREV_CHUNKS = 8
B_REACH = B_PREV_CHUNKS * CHUNK
REL_CLIP = 128
C_WIDTH = D_MODEL // 2
CONV_WIDTH = 3
N_BRANCH = 3
BRANCH_WIDTH = D_MODEL // 2
IN_COLS = 2 * A_WIDTH + 3 * B_WIDTH + 3 * C_WIDTH + N_BRANCH * D_MODEL
D_FF = ((8 * D_MODEL // 3 + 255) // 256) * 256
N_EXPERTS = 8
TOP_K = 2
D_FF_EXPERT = 7 * D_MODEL // 2
EPS = 1e-6
NEG_INF = -1e30

kernel_name = 'hybrid_stream_encoder_step'

def rmsnorm(x, g):
    x32 = x.astype(jnp.float32)
    y = x32 * lax.rsqrt(jnp.mean(x32 * x32, axis=-1, keepdims=True) + EPS)
    return (y * g.astype(jnp.float32)).astype(x.dtype)

def project(h, w_in):
    z = jnp.einsum('btd,dc->btc', h, w_in)
    sizes = [A_WIDTH, A_WIDTH, B_WIDTH, B_WIDTH, B_WIDTH, C_WIDTH, C_WIDTH, C_WIDTH]
    offsets = [int(o) for o in np.cumsum(sizes)]
    return jnp.split(z, offsets, axis=-1)

def gmlp_mix(u, v, ws, bs):
    b, L, _ = u.shape
    lc = min(L, A_CHUNK)
    n = L // lc
    pos = np.arange(lc)
    mask = (pos[None, :] // CHUNK) <= (pos[:, None] // CHUNK)
    w = jnp.where(mask[None], ws[:, :lc, :lc], 0)
    v5 = v.reshape(b, n, lc, A_GROUPS, A_GROUP_DIM)
    mixed = jnp.einsum('gij,bnjgd->bnigd', w, v5) + jnp.transpose(bs[:, :lc])[None, None, :, :, None]
    return u * mixed.reshape(b, L, A_WIDTH)

def rel_bias(table, n_q, n_k, offset):
    dist = offset + jnp.arange(n_q)[:, None] - jnp.arange(n_k)[None, :]
    idx = jnp.clip(dist, -REL_CLIP, REL_CLIP) + REL_CLIP
    return jnp.take(table, idx, axis=1).astype(jnp.float32)

def attend(q, k, v, bias, valid=None):
    s = jnp.einsum('bqhd,bkhd->bhqk', q, k).astype(jnp.float32) * (B_HEAD_DIM ** -0.5) + bias[None]
    if valid is not None:
        s = jnp.where(valid, s, NEG_INF)
    p = jax.nn.softmax(s, axis=-1)
    return jnp.einsum('bhqk,bkhd->bqhd', p.astype(v.dtype), v)

def band_attention(q, k, v, table):
    b, s, hh, dh = q.shape
    nc = s // CHUNK
    band = B_REACH + CHUNK
    kp = jnp.pad(k, ((0, 0), (B_REACH, 0), (0, 0), (0, 0)))
    vp = jnp.pad(v, ((0, 0), (B_REACH, 0), (0, 0), (0, 0)))
    bias = rel_bias(table, CHUNK, band, B_REACH)
    qc = jnp.moveaxis(q.reshape(b, nc, CHUNK, hh, dh), 1, 0)

    def one_chunk(args):
        c, qb = args
        start = c * CHUNK
        kb = lax.dynamic_slice_in_dim(kp, start, band, axis=1)
        vb = lax.dynamic_slice_in_dim(vp, start, band, axis=1)
        valid = (start - B_REACH + jnp.arange(band)) >= 0
        return attend(qb, kb, vb, bias, valid[None, None, None, :])

    out = lax.map(one_chunk, (jnp.arange(nc), qc))
    return jnp.moveaxis(out, 0, 1).reshape(b, s, hh, dh)

def causal_conv(zp, w, L):
    y = zp[:, 0:L] * w[0]
    for t in range(1, CONV_WIDTH):
        y = y + zp[:, t:t + L] * w[t]
    return y

def merge(a, bo, c, gates, w_branch, w_out):
    b, L, _ = a.shape
    br = jnp.stack([a, bo, c], axis=-2)
    p = jnp.einsum('blnw,nwd->blnd', br, w_branch)
    g = jax.nn.sigmoid(gates.reshape(b, L, N_BRANCH, D_MODEL))
    m = jnp.sum(g * p, axis=-2)
    return jnp.einsum('bld,de->ble', m, w_out)

def mixer_prompt(h, w_in, g_v, ws, bs, table, conv_w, w_branch, w_out):
    b, s, _ = h.shape
    ua, va, q, k, v, cin, gb, gc, gates = project(h, w_in)
    vn = rmsnorm(jax.nn.gelu(va), g_v)
    a_out = gmlp_mix(jax.nn.gelu(ua), vn, ws, bs)
    q = q.reshape(b, s, B_HEADS, B_HEAD_DIM)
    k = k.reshape(b, s, B_HEADS, B_HEAD_DIM)
    v = v.reshape(b, s, B_HEADS, B_HEAD_DIM)
    b_out = band_attention(q, k, v, table).reshape(b, s, B_WIDTH)
    zp = jnp.pad(gc * cin, ((0, 0), (CONV_WIDTH - 1, 0), (0, 0)))
    c_out = gb * causal_conv(zp, conv_w, s)
    y = merge(a_out, b_out, c_out, gates, w_branch, w_out)
    keep = min(B_REACH, s)
    return y, k[:, s - keep:], v[:, s - keep:], zp[:, -(CONV_WIDTH - 1):]

def mixer_sample(h, ck, cv, cs, w_in, g_v, ws, bs, table, conv_w, w_branch, w_out):
    b, t, _ = h.shape
    ua, va, q, k, v, cin, gb, gc, gates = project(h, w_in)
    vn = rmsnorm(jax.nn.gelu(va), g_v)
    a_out = gmlp_mix(jax.nn.gelu(ua), vn, ws, bs)
    q = q.reshape(b, t, B_HEADS, B_HEAD_DIM)
    k = k.reshape(b, t, B_HEADS, B_HEAD_DIM)
    v = v.reshape(b, t, B_HEADS, B_HEAD_DIM)
    keep = ck.shape[1]
    kk = jnp.concatenate([ck, k], axis=1)
    vv = jnp.concatenate([cv, v], axis=1)
    bias = rel_bias(table, t, keep + t, keep)
    b_out = attend(q, kk, vv, bias).reshape(b, t, B_WIDTH)
    zp = jnp.concatenate([cs, gc * cin], axis=1)
    c_out = gb * causal_conv(zp, conv_w, t)
    y = merge(a_out, b_out, c_out, gates, w_branch, w_out)
    return y, k, v, zp[:, -(CONV_WIDTH - 1):], vn

def swiglu(h, w1, w3, w2):
    a = jnp.einsum('...d,df->...f', h, w1)
    g = jnp.einsum('...d,df->...f', h, w3)
    return jnp.einsum('...f,fd->...d', jax.nn.silu(a) * g, w2)

def moe(h, w_router, b_router, w1, w3, w2):
    logits = jnp.einsum('...d,de->...e', h, w_router).astype(jnp.float32) + b_router.astype(jnp.float32)
    top_v, top_i = lax.top_k(logits, TOP_K)
    top_w = jax.nn.softmax(top_v, axis=-1)
    combine = jnp.einsum('...k,...ke->...e', top_w, jax.nn.one_hot(top_i, N_EXPERTS, dtype=jnp.float32))
    y = None
    for e in range(N_EXPERTS):
        term = combine[..., e:e + 1].astype(h.dtype) * swiglu(h, w1[e], w3[e], w2[e])
        y = term if y is None else y + term
    return y

def setup_inputs(seed: int = 0) -> dict:
    key = jax.random.key(seed)
    ks = jax.random.split(key, 24)
    nrm = jax.random.normal
    f32 = jnp.float32
    d = D_MODEL
    keep = min(B_REACH, PAST_LEN)
    n_dense = (DEPTH + 1) // 2
    n_moe = DEPTH // 2
    return {
        'x_prompt': nrm(ks[0], (BATCH, SEQ, d), f32),
        'x_sample': nrm(ks[1], (DEC_BATCH, DEC_SEQ, d), f32),
        'cache_attn_k': nrm(ks[2], (DEPTH, DEC_BATCH, keep, B_HEADS, B_HEAD_DIM), f32),
        'cache_attn_v': nrm(ks[3], (DEPTH, DEC_BATCH, keep, B_HEADS, B_HEAD_DIM), f32),
        'state_conv': nrm(ks[4], (DEPTH, DEC_BATCH, CONV_WIDTH - 1, C_WIDTH), f32),
        'norm_mix_g': 1.0 + 0.05 * nrm(ks[5], (DEPTH, d), f32),
        'w_in': nrm(ks[6], (DEPTH, d, IN_COLS), f32) * d ** -0.5,
        'gmlp_norm_g': 1.0 + 0.05 * nrm(ks[7], (DEPTH, A_WIDTH), f32),
        'gmlp_ws': nrm(ks[8], (DEPTH, A_GROUPS, A_CHUNK, A_CHUNK), f32) * (0.5 * A_CHUNK ** -0.5),
        'gmlp_bs': 1.0 + 0.1 * nrm(ks[9], (DEPTH, A_GROUPS, A_CHUNK), f32),
        'attn_rel_bias': 0.5 * nrm(ks[10], (DEPTH, B_HEADS, 2 * REL_CLIP + 1), f32),
        'conv_w': nrm(ks[11], (DEPTH, CONV_WIDTH, C_WIDTH), f32) * CONV_WIDTH ** -0.5,
        'w_branch': nrm(ks[12], (DEPTH, N_BRANCH, BRANCH_WIDTH, d), f32) * BRANCH_WIDTH ** -0.5,
        'w_out': nrm(ks[13], (DEPTH, d, d), f32) * d ** -0.5,
        'norm_ffn_g': 1.0 + 0.05 * nrm(ks[14], (DEPTH, d), f32),
        'ffn_w1': nrm(ks[15], (n_dense, d, D_FF), f32) * d ** -0.5,
        'ffn_w3': nrm(ks[16], (n_dense, d, D_FF), f32) * d ** -0.5,
        'ffn_w2': nrm(ks[17], (n_dense, D_FF, d), f32) * D_FF ** -0.5,
        'moe_router': nrm(ks[18], (n_moe, d, N_EXPERTS), f32) * d ** -0.5,
        'moe_router_b': 0.01 * nrm(ks[19], (n_moe, N_EXPERTS), f32),
        'moe_w1': nrm(ks[20], (n_moe, N_EXPERTS, d, D_FF_EXPERT), f32) * d ** -0.5,
        'moe_w3': nrm(ks[21], (n_moe, N_EXPERTS, d, D_FF_EXPERT), f32) * d ** -0.5,
        'moe_w2': nrm(ks[22], (n_moe, N_EXPERTS, D_FF_EXPERT, d), f32) * D_FF_EXPERT ** -0.5,
        'final_norm_g': 1.0 + 0.05 * nrm(ks[23], (d,), f32),
    }

def reference(x_prompt, x_sample, cache_attn_k, cache_attn_v, state_conv, norm_mix_g, w_in,
              gmlp_norm_g, gmlp_ws, gmlp_bs, attn_rel_bias, conv_w, w_branch, w_out, norm_ffn_g,
              ffn_w1, ffn_w3, ffn_w2, moe_router, moe_router_b, moe_w1, moe_w3, moe_w2, final_norm_g):
    xp, xs = x_prompt, x_sample
    pk, pv, pc, sk, sv, sc, sg = [], [], [], [], [], [], []
    for l in range(DEPTH):
        yp, k_p, v_p, c_p = mixer_prompt(rmsnorm(xp, norm_mix_g[l]), w_in[l], gmlp_norm_g[l], gmlp_ws[l],
                                         gmlp_bs[l], attn_rel_bias[l], conv_w[l], w_branch[l], w_out[l])
        ys, k_s, v_s, c_s, g_s = mixer_sample(rmsnorm(xs, norm_mix_g[l]), cache_attn_k[l], cache_attn_v[l],
                                              state_conv[l], w_in[l], gmlp_norm_g[l], gmlp_ws[l], gmlp_bs[l],
                                              attn_rel_bias[l], conv_w[l], w_branch[l], w_out[l])
        xp = xp + yp
        xs = xs + ys
        hp = rmsnorm(xp, norm_ffn_g[l])
        hs = rmsnorm(xs, norm_ffn_g[l])
        i = l // 2
        if l % 2 == 0:
            xp = xp + swiglu(hp, ffn_w1[i], ffn_w3[i], ffn_w2[i])
            xs = xs + swiglu(hs, ffn_w1[i], ffn_w3[i], ffn_w2[i])
        else:
            xp = xp + moe(hp, moe_router[i], moe_router_b[i], moe_w1[i], moe_w3[i], moe_w2[i])
            xs = xs + moe(hs, moe_router[i], moe_router_b[i], moe_w1[i], moe_w3[i], moe_w2[i])
        pk.append(k_p); pv.append(v_p); pc.append(c_p)
        sk.append(k_s); sv.append(v_s); sc.append(c_s); sg.append(g_s)
    y_prompt = rmsnorm(xp, final_norm_g)
    y_sample = rmsnorm(xs, final_norm_g)
    prompt_attn_k = jnp.stack(pk)
    prompt_attn_v = jnp.stack(pv)
    prompt_conv_state = jnp.stack(pc)
    sample_attn_k = jnp.stack(sk)
    sample_attn_v = jnp.stack(sv)
    sample_conv_state = jnp.stack(sc)
    sample_gmlp_v = jnp.stack(sg)
    return (y_prompt, y_sample, prompt_attn_k, prompt_attn_v, prompt_conv_state,
            sample_attn_k, sample_attn_v, sample_conv_state, sample_gmlp_v)


_drawn_inputs = setup_inputs


def setup_inputs(seed=0):
    import zlib

    import numpy as np

    out = dict(_drawn_inputs(seed))
    spreads = {}
    factors = {}
    for name, (base, spread) in spreads.items():
        noise = np.random.default_rng([zlib.crc32(name.encode()), seed]).standard_normal(out[name].shape)
        drawn = base * np.exp(spread * noise) if base else spread * noise
        out[name] = __import__('jax').numpy.asarray(drawn.astype(out[name].dtype))
    for name, factor in factors.items():
        out[name] = (out[name] * factor).astype(out[name].dtype)
    return out
```

```python
import numpy as np
import concourse.bass as bass
from concourse import mybir
from contextlib import ExitStack

P = 128
D = 1024
DT = D // P
SEQ, DEC = 256, 32
TOK = SEQ + DEC
TILES = [(0, 128), (128, 128), (256, 32)]
HALF = D // 2
BT = HALF // P
HEADS, DH = 8, 64
CHUNK = 64
PAST = 256
CLIP = 128
TAB = 2 * CLIP + 1
IN_COLS = 7 * D
FF = 2816
EXPERTS = 8
FFE = 3584
SLOT = 96
ST = TOK // SLOT
EPS = 1e-6
MASKED = -1e30
SCALE = DH ** -0.5

RING = 6
UNIT = 256
KB = UNIT // P
PAIRS = FFE // UNIT // 2
BIAS_W = 384
EXT = 512

VEC_MIX, VEC_FFN, VEC_FIN, VEC_CONV, VEC_STATE = 0, 16, 32, 40, 64
VECS = 80


def mixer_matrices(l):
    names = []
    for seg, n in (("ua", 2), ("va", 2), ("q", 2), ("k", 2), ("v", 2), ("cin", 2), ("gc", 2), ("gb", 2),
                   ("gate", 12)):
        names += [(seg, l, i) for i in range(n)]
    names += [("branch", l, h, b) for h in range(2) for b in range(3)]
    names += [("out", l, i) for i in range(4)]
    return names


SEGMENT = {"ua": 0, "va": 1, "q": 2, "k": 3, "v": 4, "cin": 5, "gb": 6, "gc": 7, "gate": 8}


def weight_stream():
    names = mixer_matrices(0)
    for u in range(FF // UNIT):
        names += [("w1", u), ("w3", u), ("w2", u)]
    names += mixer_matrices(1)
    return {n: i for i, n in enumerate(names)}


STREAM = weight_stream()
LEAD = len(STREAM)
SHIFT = -LEAD % RING


def slot_of(i):
    return (i + SHIFT) % RING


def loads_of(i):
    first = (slot_of(i) - SHIFT) % RING
    return (i - first) // RING + 1


def mixer_groups(l):
    g = [("norm", 2 * l)]
    g += [("ua", l, j) for j in range(BT)]
    g += [("va", l, h, n) for h in range(2) for n in range(3)]
    g += [("q", l, j) for j in range(BT)] + [("k", l, j) for j in range(BT)]
    g += [("v", l, h, n) for h in range(2) for n in range(3)]
    g += [("s", l, h) for h in range(HEADS)] + [("s2", l, r) for r in range(2)]
    g += [(s, l, j) for s in ("cin", "gc", "gb") for j in range(BT)]
    g += [("mixed", l, j) for j in range(BT)]
    g += [("gate", l, j) for j in range(24)]
    g += [("pt2", l, r) for r in range(2)]
    for b in range(BT):
        g += [("pt", l, 2 * b), ("pt", l, 2 * b + 1), ("pv", l, b)]
    g += [("branch", l, h, b, j) for h in range(2) for b in range(3) for j in range(4)]
    g += [("out", l, j) for j in range(DT)]
    g += [("norm", 2 * l + 1)]
    return g


def unit_groups(u):
    return [(s, u, b) for b in range(KB) for s in ("a", "g")] + [("y", u, j) for j in range(DT)]


class Groups:

    def __init__(self):
        self.at, self.total, self.last = {}, 0, [[] for _ in range(8)]

    def add(self, names, first_bank=0):
        for i, n in enumerate(names):
            b = (first_bank + i) % 8
            self.at[n] = (b, self.total, list(self.last[b]))
            self.last[b] = [(n, "same")]
            self.total += 1

    def close_loop(self, names, turns, back, end):
        for b in range(8):
            inside = [n for n in names if self.at[n][0] == b]
            if inside:
                self.at[inside[0]][2].append((inside[-1], back))
                self.last[b] = [(inside[-1], end)]
        self.total += (turns - 1) * len(names)


def number_groups():
    g = Groups()
    g.add(mixer_groups(0))
    for u in range(FF // UNIT):
        g.add(unit_groups(("dense", u)), 0 if u % 2 == 0 else 4)
    g.add(mixer_groups(1))
    g.add([("logits",), ("counts",)] + [("htok", n, h) for n in range(3) for h in range(2)])
    start = g.total
    g.add([("gather", j) for j in range(DT)] + [("dwt", s) for s in range(ST)])
    pair = [n for u in range(2) for n in unit_groups(("moe", u))]
    g.add(pair)
    g.close_loop(pair, PAIRS, "last_pair", "end_of_pairs")
    g.add([("ytok", s, h) for s in range(ST) for h in range(2)] + [("scatter", j) for j in range(DT)])
    per_expert = g.total - start
    turn = [n for n in g.at if g.at[n][1] >= start]
    before_loop = g.total
    for b in range(8):
        inside = [n for n in turn if g.at[n][0] == b]
        g.at[inside[0]][2].append((inside[-1], "last_expert"))
        g.last[b] = [(inside[-1], "end_of_experts")]
    g.total = before_loop + (EXPERTS - 1) * per_expert
    g.add([("norm", 4)])
    return g.at, len(pair), per_expert


GROUP, PER_PAIR, PER_EXPERT = number_groups()


class Turns:

    def __init__(self):
        self.e = self.i = None

    def value(self, base, per_expert, per_pair):
        v = base
        if self.e is not None and per_expert:
            v = self.e * per_expert + v
        if self.i is not None and per_pair:
            v = self.i * per_pair + v
        return v

    def full(self, name):
        return self.value(GROUP[name][1] + 1, PER_EXPERT, PER_PAIR)


def last_uses():
    uses = []
    for n in STREAM:
        kind = n[0]
        if kind in ("va", "v"):
            uses.append((kind, n[1], n[2], 2))
        elif kind == "branch":
            uses.append(("branch", n[1], n[2], n[3], 3))
        elif kind in ("w1", "w3", "w2"):
            uses.append({"w1": ("a", ("dense", n[1]), KB - 1), "w3": ("g", ("dense", n[1]), KB - 1),
                         "w2": ("y", ("dense", n[1]), DT - 1)}[kind])
        else:
            uses.append((kind, n[1], 2 * n[2] + 1))
    return uses


LAST_USE = last_uses()
DENSE_UNITS = FF // UNIT
MIXER_SUMS = 2 * DT


def encoder(nc, x_t, vecs, w_in, cache_k_t, cache_v, ws_t, bs, g_v, bias_rev, w_branch, w_out,
            w1, w3, w2, router, router_b, e_w1, e_w3, e_w2, y_t, k_t, v_rows, z_state, vn_rows):
    f32, i32 = mybir.dt.float32, mybir.dt.int32
    ALU, ACT, AX = mybir.AluOpType, mybir.ActivationFunctionType, mybir.AxisListType
    ctx = ExitStack()
    with ctx:
        def sb(name, shape, dt=f32):
            return ctx.enter_context(nc.sbuf_tensor(name, shape, dt))

        def sem(name):
            return ctx.enter_context(nc.semaphore(name))

        bias_ext = nc.dram_tensor("bias_ext", [2, P, HEADS * EXT], f32).ap()

        ring = [sb(f"ring{i}", [P, 2048]) for i in range(RING)]
        x = sb("x", [P, DT, TOK])
        h = sb("h", [P, DT, TOK])
        rms = sb("rms", [P, TOK])
        rstd = sb("rstd", [P, TOK])
        eps = sb("eps", [P, 1])
        vec = sb("vec", [P, VECS])
        mean_w = sb("mean_w", [P, P])
        ident = sb("ident", [P, P])
        ones = sb("ones", [P, P])
        before = sb("before", [P, P])
        slot_id = sb("slot_id", [P, TOK])
        rank = sb("rank", [P, 3, EXPERTS])
        valid = sb("valid", [P, 3])
        vg = sb("vg", [P, 3, HALF])
        vsq = sb("vsq", [P, 3])
        vrs = sb("vrs", [P, 3])
        u_t = sb("u_t", [P, BT, TOK])
        q_t = sb("q_t", [P, BT, TOK])
        key_t = sb("key_t", [P, BT, TOK])
        v_tok = sb("v_tok", [P, 3, HALF])
        ck_t = sb("ck_t", [P, BT, PAST])
        cv = sb("cv", [P, 2, HALF])
        wst = sb("wst", [P, BT, P])
        bsb = sb("bsb", [P, BT, P])
        gvb = sb("gvb", [P, HALF])
        bias = sb("bias", [P, HEADS, BIAS_W])
        bias2 = sb("bias2", [P, 2, TOK])
        prob = sb("prob", [P, HEADS, BIAS_W])
        prob2 = sb("prob2", [P, 2, TOK])
        top = sb("top", [P, 2 * HEADS + 2])
        total = sb("total", [P, 2 * HEADS + 2])
        part = sb("part", [P, 2 * HEADS + 2])
        pt = sb("pt", [P, 2, BIAS_W])
        pt2 = sb("pt2", [P, 2, 3, P])
        z = sb("z", [P, BT, TOK + 4])
        gate = sb("gate", [P, 24, TOK])
        a_t = sb("a_t", [P, BT, TOK])
        b_t = sb("b_t", [P, BT, TOK])
        c_t = sb("c_t", [P, BT, TOK])
        tmp = sb("tmp", [P, 2, TOK + 4])
        silu = sb("silu", [P, 2 * KB, TOK])
        hid = sb("hid", [P, 2 * KB, TOK])
        rw = sb("rw", [P, DT, EXPERTS])
        rb = sb("rb", [P, EXPERTS])
        count = sb("count", [1, EXPERTS], i32)
        sq = gate[:, 0:DT, :]
        m_t = q_t, key_t
        ext = gate[:, :, :].rearrange("p a b -> p (a b)")[:, 0:HEADS * EXT].rearrange("p (h c) -> p h c", h=HEADS)
        gate_flat = gate[:, :, :].rearrange("p a b -> p (a b)")
        h_tok = gate_flat[:, 2304:2304 + 3 * D].rearrange("p (n d) -> p n d", n=3)
        bias_flat = bias[:, :, :].rearrange("p a b -> p (a b)")
        y_tok = bias_flat[:, 0:3 * D].rearrange("p (n d) -> p n d", n=3)
        prob_flat = prob[:, :, :].rearrange("p a b -> p (a b)")
        he = prob_flat[:, 0:DT * TOK].rearrange("p (a b) -> p a b", a=DT)
        spread = a_t[:, 0:3, :]
        wspread = b_t[:, 0:3, :]
        wspread_t = c_t[:, 0:3, :]
        y_sum = gate_flat[:, 0:DT * TOK].rearrange("p (a b) -> p a b", a=DT)
        rt = u_t[:, 0, 0:288].rearrange("p (a n e) -> p a n e", a=12, n=3)
        rs = u_t[:, 1, 0:24].rearrange("p (a n) -> p a n", a=8)
        psum = ctx.enter_context(nc.psum_tensor("psum", [P, 8, 512], f32))

        slot_loaded = [sem(f"slot_loaded{i}") for i in range(RING)]
        bank_full = sem("bank_full")
        x_in = sem("x_in")
        vec_in = sem("vec_in")
        made = sem("made")
        dve_step = sem("dve_step")
        rms_ready = sem("rms_ready")
        rstd_ready = sem("rstd_ready")
        vrms_ready = sem("vrms_ready")
        vg_ready = sem("vg_ready")
        score_ready = sem("score_ready")
        gc_read = sem("gc_read")
        mixed_read = sem("mixed_read")
        branch_read = sem("branch_read")
        logits_read = sem("logits_read")
        sum_ready = sem("sum_ready")
        rows_stored = sem("rows_stored")
        keys_stored = sem("keys_stored")
        values_stored = sem("values_stored")
        state_stored = sem("state_stored")
        pool_step = sem("pool_step")
        zeroed = sem("zeroed")
        squared = sem("squared")
        h_ready = sem("h_ready")
        layer_in = [sem(f"layer_in{i}") for i in range(6)]
        ext_loaded = sem("ext_loaded")
        ext_ready = sem("ext_ready")
        ext_stored = sem("ext_stored")
        bias_loaded = sem("bias_loaded")
        bias2_loaded = sem("bias2_loaded")
        bias_masked = sem("bias_masked")
        mix_masked = sem("mix_masked")
        u_ready = sem("u_ready")
        vsq_ready = sem("vsq_ready")
        vn_ready = sem("vn_ready")
        qk_ready = sem("qk_ready")
        v_ready = sem("v_ready")
        top_ready = sem("top_ready")
        exp_ready = sem("exp_ready")
        prob_ready = sem("prob_ready")
        pt_ready = sem("pt_ready")
        pt2_ready = sem("pt2_ready")
        cin_ready = sem("cin_ready")
        z_ready = sem("z_ready")
        gate_ready = sem("gate_ready")
        a_ready = sem("a_ready")
        b_ready = sem("b_ready")
        c_ready = sem("c_ready")
        m_ready = sem("m_ready")
        x_ready = sem("x_ready")
        silu_ready = sem("silu_ready")
        hid_ready = sem("hid_ready")
        mask_ready = sem("mask_ready")
        gap_ready = sem("gap_ready")
        gap_exp = sem("gap_exp")
        count_ready = sem("count_ready")
        htok_ready = sem("htok_ready")
        spread_ready = sem("spread_ready")
        he_ready = sem("he_ready")
        spread_t_ready = sem("spread_t_ready")
        ytok_ready = sem("ytok_ready")
        y_out = sem("y_out")
        out_done = sem("out_done")
        NORM_OF_LAYER = (0, 2)

        def bank(name, rows=P, cols=TOK, row0=0):
            return psum[row0:row0 + rows, GROUP[name][0], 0:cols]

        def reader(name):
            kind, at = name[0], name[1:]
            if kind in ("a", "g", "y"):
                (part, u), j = at
                n, ready = {"a": (KB, silu_ready), "g": (KB, hid_ready), "y": (DT, sum_ready)}[kind]
                if part == "dense":
                    return ready, n * u + j + 1, 0, 0
                return ready, n * (DENSE_UNITS + u) + j + 1, 2 * n * PAIRS, 2 * n
            if kind == "branch":
                l, hf, b, j = at
                return branch_read, 24 * l + 12 * hf + 4 * b + j + 1, 0, 0
            if kind in ("va", "v"):
                l, hf, n = at
                return {"va": vg_ready, "v": v_ready}[kind], 6 * l + 3 * hf + n + 1, 0, 0
            if kind == "ytok":
                return ytok_ready, 2 * at[0] + at[1] + 1, 2 * ST, 0
            if kind == "htok":
                return htok_ready, 2 * at[0] + at[1] + 1, 0, 0
            once = {"gather": (he_ready, DT, 0), "dwt": (spread_t_ready, ST, 0), "scatter": (x_ready, DT, MIXER_SUMS)}
            if kind in once:
                ready, n, base = once[kind]
                return ready, base + at[0] + 1, n, 0
            if kind in ("logits", "counts"):
                return {"logits": logits_read, "counts": count_ready}[kind], 1, 0, 0
            if kind == "norm":
                return rms_ready, at[0] + 1, 0, 0
            ready, per_layer, first = {
                "ua": (u_ready, BT, 0), "q": (qk_ready, 2 * BT, 0), "k": (qk_ready, 2 * BT, BT),
                "s": (score_ready, HEADS + 2, 0), "s2": (score_ready, HEADS + 2, HEADS),
                "cin": (cin_ready, BT, 0), "gc": (gc_read, BT, 0), "gb": (c_ready, BT, 0),
                "mixed": (mixed_read, BT, 0), "gate": (gate_ready, 24, 0), "pt2": (pt2_ready, 2, 0),
                "pt": (pt_ready, HEADS, 0), "pv": (b_ready, BT, 0), "out": (x_ready, DT, 0)}[kind]
            return ready, per_layer * at[0] + first + at[1] + 1, 0, 0

        block = ctx.enter_context(nc.Block())

        @block.sync
        def _(sp):
            def load(i, dst, src):
                if i >= RING:
                    sp.wait_ge(bank_full, GROUP[LAST_USE[i - RING]][1] + 1)
                sp.dma_start(dst, src).then_inc(slot_loaded[slot_of(i)], 16)

            def tall(s, c=256):
                return ring[s][:, :].rearrange("p (k c) -> p k c", c=c)

            def mixer(l):
                for n in mixer_matrices(l):
                    i = STREAM[n]
                    s = slot_of(i)
                    if n[0] == "branch":
                        _, _, half, b = n
                        src = w_branch[l, b, :, half * 512:(half + 1) * 512]
                        load(i, tall(s, 512), src.rearrange("(k p) c -> p k c", p=P))
                    elif n[0] == "out":
                        load(i, tall(s), w_out[l, :, n[2] * 256:(n[2] + 1) * 256].rearrange("(k p) c -> p k c", p=P))
                    else:
                        c = SEGMENT[n[0]] * 512 + n[2] * 256
                        load(i, tall(s), w_in[l, :, c:c + 256].rearrange("(k p) c -> p k c", p=P))

            mixer(0)
            for u in range(FF // UNIT):
                for k, w in enumerate((w1, w3)):
                    i = STREAM[("w1", u)] + k
                    load(i, tall(slot_of(i)), w[:, u * UNIT:(u + 1) * UNIT].rearrange("(k p) c -> p k c", p=P))
                i = STREAM[("w2", u)]
                load(i, tall(slot_of(i), D), w2[u * UNIT:(u + 1) * UNIT, :].rearrange("(k p) c -> p k c", p=P))
            mixer(1)

            def expert_pair(e, i, used):
                for u in range(2):
                    for k in range(3):
                        s = 3 * u + k
                        used(u, k)
                        cols = bass.ds(i * (2 * UNIT) + u * UNIT, UNIT)
                        if k < 2:
                            src = (e_w1, e_w3)[k][bass.ds(e, 1), :, cols]
                            sp.dma_start(tall(s), src.rearrange("o (k p) c -> p (o k) c", p=P)).then_inc(slot_loaded[s], 16)
                        else:
                            src = e_w2[bass.ds(e, 1), cols, :]
                            sp.dma_start(tall(s, D), src.rearrange("o (k p) c -> p (o k) c", p=P)).then_inc(slot_loaded[s], 16)

            def pair_use(u, k):
                return GROUP[(("a", ("moe", u), KB - 1), ("g", ("moe", u), KB - 1), ("y", ("moe", u), DT - 1))[k]][1] + 1

            def other_pairs(e):
                with sp.Fori(1, PAIRS) as i:
                    expert_pair(e, i, lambda u, k: sp.wait_ge(
                        bank_full, e * PER_EXPERT + i * PER_PAIR + (pair_use(u, k) - PER_PAIR)))

            expert_pair(0, 0, lambda u, k: sp.wait_ge(bank_full, GROUP[LAST_USE[LEAD - RING + 3 * u + k]][1] + 1))
            with sp.Fori(0, EXPERTS - 1) as e:
                other_pairs(e)
                expert_pair(e + 1, 0, lambda u, k: sp.wait_ge(
                    bank_full, e * PER_EXPERT + (pair_use(u, k) + (PAIRS - 1) * PER_PAIR)))
            other_pairs(EXPERTS - 1)

        @block.gpsimd
        def _(pool):
            nc.gpsimd.memset(ident[:, :], 0.0).then_inc(pool_step, 1)
            nc.gpsimd.memset(ones[:, :], 1.0).then_inc(pool_step, 1)
            nc.gpsimd.memset(before[:, :], 1.0).then_inc(pool_step, 1)
            nc.gpsimd.iota(slot_id[:, :], pattern=[[1, TOK]], base=0, channel_multiplier=0,
                           allow_small_or_imprecise_dtypes=True).then_inc(made, 1)
            nc.gpsimd.iota(rank[:, :, :], pattern=[[0, 3], [-1, EXPERTS]], base=EXPERTS, channel_multiplier=0,
                           allow_small_or_imprecise_dtypes=True).then_inc(made, 1)
            pool.wait_ge(pool_step, 3)
            nc.gpsimd.affine_select(out=ident[:, :], in_=ident[:, :], compare_op=ALU.not_equal, fill=1.0,
                                    base=0, pattern=[[-1, P]], channel_multiplier=1).then_inc(made, 1)
            nc.gpsimd.affine_select(out=before[:, :], in_=before[:, :], compare_op=ALU.is_gt, fill=0.0,
                                    base=0, pattern=[[1, P]], channel_multiplier=-1).then_inc(made, 1)

            def layer_inputs(l):
                if l:
                    pool.wait_ge(a_ready, BT)
                    pool.wait_ge(b_ready, BT)
                pool.dma_start(wst[:, :, :], ws_t[l]).then_inc(layer_in[0], 16)
                pool.dma_start(bsb[:, :, :].rearrange("p a b -> p (a b)"),
                               bs[l:l + 1, :].broadcast_to([P, HALF])).then_inc(layer_in[1], 16)
                pool.dma_start(gvb[:, :], g_v[l:l + 1, :].broadcast_to([P, HALF])).then_inc(layer_in[2], 16)
                pool.dma_start(ck_t[:, :, :], cache_k_t[l].rearrange("(j p) t -> p j t", p=P)).then_inc(layer_in[3], 16)
                pool.dma_start(cv[:, :, :], cache_v[l].rearrange("(n p) c -> p n c", p=P)).then_inc(layer_in[4], 16)

            def bias_rows():
                for l in range(2):
                    if l:
                        pool.wait_ge(ext_stored, 16 * l)
                    pool.dma_start(ext[:, :, EXT // 2 - 1:EXT - 1],
                                   bias_rev[l:l + 1, :, 0:TAB - 1].broadcast_to([P, HEADS, TAB - 1]),
                                   ).then_inc(ext_loaded, 16)
                    pool.wait_ge(ext_ready, l + 1)
                    pool.dma_start(bias_ext[l], ext.rearrange("p h c -> p (h c)")).then_inc(ext_stored, 16)

            def bias_tiles(l):
                row = HEADS * EXT
                pool.dma_start(bias[:, :, :], bass.AP(bias_ext.tensor, bias_ext[l].offset + 127,
                                                      [[row - 1, P], [EXT, HEADS], [1, BIAS_W]])
                               ).then_inc(bias_loaded, 16)
                for j in range(4):
                    for r in range(2):
                        head = 2 * j + r
                        pool.dma_start(bias2[32 * j:32 * j + 32, r, :],
                                       bass.AP(bias_ext.tensor, bias_ext[l].offset + head * EXT + 127,
                                               [[row - 1, DEC], [1, TOK]])).then_inc(bias2_loaded, 16)

            pool.dma_start(x[:, :, :], x_t.rearrange("(k p) t -> p k t", p=P)).then_inc(x_in, 16)
            pool.dma_start(vec[:, :], vecs).then_inc(vec_in, 16)
            bias_rows()
            pool.wait_ge(ext_stored, 32)
            layer_inputs(0)
            bias_tiles(0)
            pool.dma_start(rw[:, :, :], router.rearrange("(k p) e -> p k e", p=P)).then_inc(layer_in[5], 16)
            pool.dma_start(rb[:, :], router_b.broadcast_to([P, EXPERTS])).then_inc(layer_in[5], 16)
            for l in range(2):
                pool.wait_ge(vn_ready, 3 * (l + 1))
                pool.dma_start(vn_rows[l], vg[0:DEC, 2, :]).then_inc(rows_stored, 16)
                pool.wait_ge(qk_ready, 8 * (l + 1))
                pool.dma_start(k_t[l].rearrange("(j p) t -> p j t", p=P), key_t[:, :, :]).then_inc(keys_stored, 16)
                pool.wait_ge(v_ready, 6 * (l + 1))
                pool.dma_start(v_rows[l, 0:SEQ, :].rearrange("(n p) c -> p n c", p=P),
                               v_tok[:, 0:2, :]).then_inc(values_stored, 16)
                pool.dma_start(v_rows[l, SEQ:TOK, :], v_tok[0:DEC, 2, :]).then_inc(values_stored, 16)
                pool.wait_ge(z_ready, BT * (l + 1))
                for at, to in ((SEQ, 0), (TOK + 2, 2)):
                    pool.dma_start(z_state[l, :, :, to:to + 2], z[:, :, at:at + 2]).then_inc(state_stored, 16)
                if l == 0:
                    layer_inputs(1)
                    bias_tiles(1)
            pool.wait_ge(y_out, DT)
            pool.dma_start(y_t.rearrange("(k p) t -> p k t", p=P), h[:, :, :]).then_inc(out_done, 16)
            pool.wait_ge(out_done, 16)
            pool.wait_ge(rows_stored, 32)
            pool.wait_ge(keys_stored, 32)
            pool.wait_ge(values_stored, 64)
            pool.wait_ge(state_stored, 64)

        @block.scalar
        def _(act):
            turns = Turns()
            act.wait_ge(zeroed, 3)

            def squares(n):
                if n == 0:
                    act.wait_ge(x_in, 16)
                    act.wait_ge(ext_stored, 32)
                for k in range(DT):
                    if n in (1, 3):
                        act.wait_ge(x_ready, DT * (n // 2) + k + 1)
                    elif n == 2:
                        act.wait_ge(sum_ready, DT * (DENSE_UNITS - 1) + k + 1)
                    elif n == 4:
                        act.wait_ge(x_ready, MIXER_SUMS + DT * (EXPERTS - 1) + k + 1)
                    nc.scalar.activation(sq[:, k, :], x[:, k, :], ACT.Square).then_inc(squared, 1)

            def root(n):
                act.wait_ge(bank_full, turns.full(("norm", n)))
                nc.scalar.activation(rms[:, :], bank(("norm", n)), ACT.Sqrt, bias=eps[:, 0:1]).then_inc(rms_ready, 1)

            def evacuate(name, dst, rows, cols, done, func=ACT.Copy, scale=1.0):
                act.wait_ge(bank_full, turns.full(name))
                nc.scalar.activation(dst, bank(name, rows, cols), func, scale=scale).then_inc(done, 1)

            for l in range(2):
                squares(NORM_OF_LAYER[l])
                root(NORM_OF_LAYER[l])
                for j in range(BT):
                    evacuate(("ua", l, j), u_t[:, j, :], P, TOK, u_ready, ACT.Gelu_apprx_tanh)
                if l:
                    act.wait_ge(rows_stored, 16)
                for hf in range(2):
                    for n, (t0, rows) in enumerate(TILES):
                        evacuate(("va", l, hf, n), vg[0:rows, n, hf * 256:(hf + 1) * 256], rows, 256, vg_ready,
                                 ACT.Gelu_apprx_tanh)
                act.wait_ge(vg_ready, 6 * (l + 1))
                for n, (t0, rows) in enumerate(TILES):
                    spare = (a_t, b_t, c_t)[n]
                    nc.scalar.activation(spare[0:rows, 0:2, 0:256], vg[0:rows, n, :].rearrange("p (a b) -> p a b", a=2),
                                         ACT.Square, accum_out=vsq[0:rows, n:n + 1]).then_inc(vsq_ready, 1)
                act.wait_ge(vsq_ready, 3 * (l + 1))
                for n, (t0, rows) in enumerate(TILES):
                    nc.scalar.activation(vrs[0:rows, n:n + 1], vsq[0:rows, n:n + 1], ACT.Sqrt, scale=1.0 / HALF,
                                         bias=eps[0:rows, 0:1]).then_inc(vrms_ready, 1)
                if l:
                    act.wait_ge(values_stored, 32)
                for hf in range(2):
                    for n, (t0, rows) in enumerate(TILES):
                        evacuate(("v", l, hf, n), v_tok[0:rows, n, hf * 256:(hf + 1) * 256], rows, 256, v_ready)
                for hd in range(HEADS):
                    act.wait_ge(top_ready, 9 * l + hd + 1)
                    for t, (c0, c1) in enumerate(((0, 128), (128, 384))):
                        ins = nc.scalar.activation(prob[:, hd, c0:c1], prob[:, hd, c0:c1], ACT.Exp,
                                                   bias=top[:, 2 * hd + t:2 * hd + t + 1],
                                                   accum_out=total[:, 2 * hd + t:2 * hd + t + 1])
                    ins.then_inc(exp_ready, 1)
                act.wait_ge(top_ready, 9 * l + 9)
                for r in range(2):
                    ins = nc.scalar.activation(prob2[:, r, :], prob2[:, r, :], ACT.Exp,
                                               bias=top[:, 16 + r:17 + r], accum_out=total[:, 16 + r:17 + r])
                ins.then_inc(exp_ready, 1)
                if l:
                    act.wait_ge(state_stored, 32)
                for j in range(BT):
                    evacuate(("cin", l, j), z[:, j, 2:2 + TOK], P, TOK, cin_ready)
                for j in range(24):
                    evacuate(("gate", l, j), gate[:, j, :], P, TOK, gate_ready, ACT.Tanh, scale=0.5)
                for r in range(2):
                    act.wait_ge(bank_full, turns.full(("pt2", l, r)))
                    src = bank(("pt2", l, r), P, 384).rearrange("p (a b) -> p a b", a=3)
                    nc.scalar.activation(pt2[:, r, 0:2, :], src[:, 0:2, :], ACT.Copy)
                    nc.scalar.activation(pt2[0:DEC, r, 2, :], src[0:DEC, 2, :], ACT.Copy).then_inc(pt2_ready, 1)
                for hd in range(HEADS):
                    if hd >= 2:
                        act.wait_ge(bank_full, turns.full(("pv", l, hd // 2 - 1)))
                    evacuate(("pt", l, hd), pt[:, hd % 2, :], P, 384, pt_ready)
                squares(2 * l + 1)
                root(2 * l + 1)
                if l == 0:
                    for u in range(FF // UNIT):
                        for b in range(KB):
                            if u >= 2:
                                act.wait_ge(hid_ready, KB * (u - 2) + b + 1)
                            evacuate(("a", ("dense", u), b), silu[:, KB * (u % 2) + b, :], P, TOK, silu_ready, ACT.Silu)
            act.wait_ge(gap_ready, 1)
            nc.scalar.activation(rs[:, 5, :], rs[:, 4, :], ACT.Exp).then_inc(gap_exp, 1)
            for n, (t0, rows) in enumerate(TILES):
                for hf in range(2):
                    evacuate(("htok", n, hf), h_tok[0:rows, n, hf * 512:(hf + 1) * 512], rows, 512, htok_ready)
            dense_blocks = KB * DENSE_UNITS
            with act.Fori(0, EXPERTS) as e:
                turns.e = e
                for j in range(DT):
                    evacuate(("gather", j), he[:, j, :], P, TOK, he_ready)
                with act.Fori(0, PAIRS) as i:
                    turns.i = i
                    for u in range(2):
                        for b in range(KB):
                            act.wait_ge(hid_ready, e * (2 * KB * PAIRS) + i * (2 * KB)
                                        + (dense_blocks + KB * (u - 2) + b + 1))
                            evacuate(("a", ("moe", u), b), silu[:, KB * u + b, :], P, TOK, silu_ready, ACT.Silu)
                    turns.i = None
                for s in range(ST):
                    for hf in range(2):
                        evacuate(("ytok", s, hf), y_tok[0:SLOT, s, hf * 512:(hf + 1) * 512], SLOT, 512, ytok_ready)
                turns.e = None
            squares(4)
            root(4)

        @block.vector
        def _(dve):
            turns = Turns()
            steps = [0]

            def done(ins):
                ins.then_inc(dve_step, 1)
                steps[0] += 1

            def settle():
                dve.wait_ge(dve_step, steps[0])

            def full(name):
                dve.wait_ge(bank_full, turns.full(name))

            def norm(n, gain, dst):
                dve.wait_ge(rms_ready, n + 1)
                nc.vector.reciprocal(rstd[:, :], rms[:, :]).then_inc(rstd_ready, 1)
                dve.wait_ge(rstd_ready, n + 1)
                for k in range(DT):
                    ins = nc.vector.scalar_tensor_tensor(out=h[:, k, :], in0=x[:, k, :], scalar=vec[:, gain + k:gain + k + 1],
                                                         in1=rstd[:, :], op0=ALU.mult, op1=ALU.mult)
                    ins.then_inc(dst, 1)

            nc.vector.memset(psum[:, :, :], 0.0).then_inc(zeroed, 1)
            nc.vector.memset(eps[:, :], EPS).then_inc(zeroed, 1)
            nc.vector.memset(mean_w[:, :], 1.0 / D).then_inc(zeroed, 1)
            done(nc.vector.memset(valid[:, :], 1.0))
            done(nc.vector.memset(z[:, :, 0:2], 0.0))
            settle()
            done(nc.vector.memset(valid[:, 2:3], 0.0))
            settle()
            done(nc.vector.memset(valid[0:DEC, 2:3], 1.0))
            for l in range(2):
                dve.wait_ge(ext_loaded, 16 * (l + 1))
                done(nc.vector.tensor_copy(ext[:, :, 0:EXT // 2 - 1], ext[:, :, EXT // 2 - 1:EXT // 2].broadcast_to([P, HEADS, EXT // 2 - 1])))
                settle()
                nc.vector.memset(ext[:, :, EXT - 1:EXT], 0.0).then_inc(ext_ready, 1)
            dve.wait_ge(vec_in, 16)
            dve.wait_ge(made, 4)

            for l in range(2):
                norm(NORM_OF_LAYER[l], VEC_MIX + DT * l, h_ready)
                dve.wait_ge(bias_loaded, 16 * (l + 1))
                nc.vector.memset(bias[0:CHUNK, :, 256 + CHUNK:BIAS_W], MASKED).then_inc(bias_masked, 1)
                dve.wait_ge(layer_in[0], 16 * (l + 1))
                nc.vector.memset(wst[CHUNK:P, :, 0:CHUNK], 0.0).then_inc(mix_masked, 1)
                dve.wait_ge(vrms_ready, 3 * (l + 1))
                for n, (t0, rows) in enumerate(TILES):
                    done(nc.vector.reciprocal(vrs[0:rows, n:n + 1], vrs[0:rows, n:n + 1]))
                settle()
                dve.wait_ge(layer_in[2], 16 * (l + 1))
                for n, (t0, rows) in enumerate(TILES):
                    nc.vector.scalar_tensor_tensor(out=vg[0:rows, n, :], in0=vg[0:rows, n, :], scalar=vrs[0:rows, n:n + 1],
                                                   in1=gvb[0:rows, :], op0=ALU.mult, op1=ALU.mult).then_inc(vn_ready, 1)
                for s, dst in (("q", q_t), ("k", key_t)):
                    for j in range(BT):
                        full((s, l, j))
                        nc.vector.tensor_copy(dst[:, j, :], bank((s, l, j))).then_inc(qk_ready, 1)
                dve.wait_ge(bias_masked, l + 1)
                for hd in range(HEADS):
                    full(("s", l, hd))
                    p = bank(("s", l, hd), P, 384)
                    nc.vector.scalar_tensor_tensor(out=prob[:, hd, 0:128], in0=p[:, 0:128], scalar=SCALE,
                                                   in1=bias[:, hd, 256:384], op0=ALU.mult, op1=ALU.add)
                    ins = nc.vector.scalar_tensor_tensor(out=prob[:, hd, 128:384], in0=p[:, 128:384], scalar=SCALE,
                                                         in1=bias[:, hd, 128:384], op0=ALU.mult, op1=ALU.add)
                    ins.then_inc(score_ready, 1)
                    dve.wait_ge(score_ready, 10 * l + hd + 1)
                    nc.vector.tensor_reduce(top[:, 2 * hd:2 * hd + 1], prob[:, hd, 0:128], AX.X, ALU.max, negate=True)
                    nc.vector.tensor_reduce(top[:, 2 * hd + 1:2 * hd + 2], prob[:, hd, 128:384], AX.X, ALU.max,
                                            negate=True).then_inc(top_ready, 1)
                dve.wait_ge(bias2_loaded, 16 * 8 * (l + 1))
                for r in range(2):
                    full(("s2", l, r))
                    ins = nc.vector.scalar_tensor_tensor(out=prob2[:, r, :], in0=bank(("s2", l, r)), scalar=SCALE,
                                                         in1=bias2[:, r, :], op0=ALU.mult, op1=ALU.add)
                    ins.then_inc(score_ready, 1)
                dve.wait_ge(score_ready, 10 * l + 10)
                nc.vector.tensor_reduce(top[:, 16:18], prob2[:, :, :], AX.X, ALU.max, negate=True).then_inc(top_ready, 1)

                for j in range(BT):
                    full(("gc", l, j))
                    dve.wait_ge(cin_ready, BT * l + j + 1)
                    ins = nc.vector.tensor_tensor(tmp[:, j % 2, 0:TOK], z[:, j, 2:2 + TOK], bank(("gc", l, j)), ALU.mult)
                    ins.then_inc(gc_read, 1)
                    dve.wait_ge(gc_read, BT * l + j + 1)
                    nc.vector.tensor_copy(z[:, j, 2:2 + SEQ], tmp[:, j % 2, 0:SEQ])
                    nc.vector.tensor_copy(z[:, j, SEQ + 4:TOK + 4], tmp[:, j % 2, SEQ:TOK])
                    st = VEC_STATE + 8 * l + 2 * j
                    nc.vector.tensor_copy(z[:, j, SEQ + 2:SEQ + 4], vec[:, st:st + 2]).then_inc(z_ready, 1)
                dve.wait_ge(z_ready, BT * (l + 1))
                for j in range(BT):
                    w = VEC_CONV + 12 * l + j
                    y = tmp[:, j % 2, 0:TOK + 2]
                    done(nc.vector.tensor_scalar(y, z[:, j, 0:TOK + 2], vec[:, w:w + 1], None, ALU.mult))
                    settle()
                    done(nc.vector.scalar_tensor_tensor(out=y, in0=z[:, j, 1:TOK + 3], scalar=vec[:, w + 4:w + 5], in1=y,
                                                        op0=ALU.mult, op1=ALU.add))
                    settle()
                    done(nc.vector.scalar_tensor_tensor(out=y, in0=z[:, j, 2:TOK + 4], scalar=vec[:, w + 8:w + 9], in1=y,
                                                        op0=ALU.mult, op1=ALU.add))
                    settle()
                    full(("gb", l, j))
                    p = bank(("gb", l, j))
                    nc.vector.tensor_tensor(c_t[:, j, 0:SEQ], y[:, 0:SEQ], p[:, 0:SEQ], ALU.mult)
                    ins = nc.vector.tensor_tensor(c_t[:, j, SEQ:TOK], y[:, SEQ + 2:TOK + 2], p[:, SEQ:TOK], ALU.mult)
                    ins.then_inc(c_ready, 1)

                dve.wait_ge(layer_in[1], 16 * (l + 1))
                dve.wait_ge(u_ready, BT * (l + 1))
                for j in range(BT):
                    full(("mixed", l, j))
                    p = bank(("mixed", l, j))
                    b2 = bsb[:, j:j + 1, :].broadcast_to([P, 2, P])
                    nc.vector.tensor_tensor(a_t[:, j, 0:SEQ].rearrange("p (a b) -> p a b", a=2),
                                            p[:, 0:SEQ].rearrange("p (a b) -> p a b", a=2), b2, ALU.add)
                    ins = nc.vector.tensor_tensor(a_t[:, j, SEQ:TOK], p[:, SEQ:TOK], bsb[:, j, 0:DEC], ALU.add)
                    ins.then_inc(mixed_read, 1)
                    dve.wait_ge(mixed_read, BT * l + j + 1)
                    nc.vector.tensor_tensor(a_t[:, j, :], a_t[:, j, :], u_t[:, j, :], ALU.mult).then_inc(a_ready, 1)

                for hd in range(HEADS):
                    dve.wait_ge(exp_ready, 9 * l + hd + 1)
                    done(nc.vector.reciprocal(part[:, 2 * hd:2 * hd + 2], total[:, 2 * hd:2 * hd + 2]))
                dve.wait_ge(exp_ready, 9 * l + 9)
                done(nc.vector.reciprocal(part[:, 16:18], total[:, 16:18]))
                settle()
                for r in range(2):
                    ins = nc.vector.tensor_scalar(prob2[:, r, :], prob2[:, r, :], part[:, 16 + r:17 + r], None, ALU.mult)
                ins.then_inc(prob_ready, 1)
                for hd in range(HEADS):
                    for t, (c0, c1) in enumerate(((0, 128), (128, 384))):
                        ins = nc.vector.tensor_scalar(prob[:, hd, c0:c1], prob[:, hd, c0:c1],
                                                      part[:, 2 * hd + t:2 * hd + t + 1], None, ALU.mult)
                    ins.then_inc(prob_ready, 1)
                for b in range(BT):
                    full(("pv", l, b))
                    nc.vector.tensor_copy(b_t[:, b, :], bank(("pv", l, b))).then_inc(b_ready, 1)

                for hf in range(2):
                    for b in range(3):
                        for j in range(4):
                            name = ("branch", l, hf, b, j)
                            full(name)
                            g = 8 * b + 4 * hf + j
                            dve.wait_ge(gate_ready, 24 * l + g + 1)
                            if hf == 1 and b == 0 and j == 0:
                                dve.wait_ge(keys_stored, 16 * (l + 1))
                            dst = m_t[hf][:, j, :] if b == 0 else tmp[:, j % 2, 0:TOK]
                            ins = nc.vector.scalar_tensor_tensor(out=dst, in0=gate[:, g, :], scalar=1.0, in1=bank(name),
                                                                 op0=ALU.add, op1=ALU.mult)
                            ins.then_inc(branch_read, 1)
                            if b:
                                dve.wait_ge(branch_read, 24 * l + 12 * hf + 4 * b + j + 1)
                                ins = nc.vector.tensor_tensor(m_t[hf][:, j, :], m_t[hf][:, j, :], tmp[:, j % 2, 0:TOK], ALU.add)
                            if b == 2:
                                ins.then_inc(m_ready, 1)
                for j in range(DT):
                    full(("out", l, j))
                    ins = nc.vector.scalar_tensor_tensor(out=x[:, j, :], in0=bank(("out", l, j)), scalar=0.5, in1=x[:, j, :],
                                                         op0=ALU.mult, op1=ALU.add)
                    ins.then_inc(x_ready, 1)
                dve.wait_ge(x_ready, DT * (l + 1))
                norm(2 * l + 1, VEC_FFN + DT * l, h_ready)
                if l == 0:
                    for u in range(FF // UNIT):
                        for b in range(KB):
                            name = ("g", ("dense", u), b)
                            full(name)
                            dve.wait_ge(silu_ready, KB * u + b + 1)
                            ins = nc.vector.tensor_tensor(hid[:, KB * (u % 2) + b, :], silu[:, KB * (u % 2) + b, :], bank(name), ALU.mult)
                            ins.then_inc(hid_ready, 1)
                        for j in range(DT):
                            name = ("y", ("dense", u), j)
                            full(name)
                            if j == 0 and u:
                                dve.wait_ge(sum_ready, DT * u)
                            ins = nc.vector.tensor_tensor(x[:, j, :], x[:, j, :], bank(name), ALU.add)
                            ins.then_inc(sum_ready, 1)
                    dve.wait_ge(sum_ready, DT * DENSE_UNITS)

            LG, EQ, OH1, LG2, OH2, MASK, COMB, POS, T0 = range(9)

            def wide(a):
                return rs[:, a, :].rearrange("p (n o) -> p n o", o=1).broadcast_to([P, 3, EXPERTS])

            done(nc.vector.memset(rt[:, LG], 0.0))
            settle()
            dve.wait_ge(layer_in[5], 32)
            full(("logits",))
            p = bank(("logits",), P, 24).rearrange("p (n e) -> p n e", n=3)
            rb1 = rb[:, :].rearrange("p (o e) -> p o e", o=1)
            done(nc.vector.tensor_tensor(rt[:, LG, 0:2], p[:, 0:2, :], rb1.broadcast_to([P, 2, EXPERTS]), ALU.add))
            ins = nc.vector.tensor_tensor(rt[0:DEC, LG, 2], p[0:DEC, 2, :], rb[0:DEC, :], ALU.add)
            ins.then_inc(logits_read, 1)
            dve.wait_ge(logits_read, 1)

            def pick(src, top_at, key_at, hot):
                done(nc.vector.tensor_reduce(rs[:, top_at, :], rt[:, src], AX.X, ALU.max))
                settle()
                done(nc.vector.tensor_tensor(rt[:, EQ], rt[:, src], wide(top_at), ALU.is_equal))
                settle()
                done(nc.vector.tensor_tensor(rt[:, EQ], rt[:, EQ], rank[:, :, :], ALU.mult))
                settle()
                done(nc.vector.tensor_reduce(rs[:, key_at, :], rt[:, EQ], AX.X, ALU.max))
                settle()
                done(nc.vector.tensor_tensor(rt[:, hot], rt[:, EQ], wide(key_at), ALU.is_equal))
                settle()

            pick(LG, 0, 1, OH1)
            done(nc.vector.scalar_tensor_tensor(out=rt[:, LG2], in0=rt[:, OH1], scalar=-3.0e38, in1=rt[:, LG],
                                                op0=ALU.mult, op1=ALU.add))
            settle()
            pick(LG2, 2, 3, OH2)
            nc.vector.tensor_tensor(rs[:, 4, :], rs[:, 2, :], rs[:, 0, :], ALU.subtract).then_inc(gap_ready, 1)
            done(nc.vector.tensor_tensor(rt[:, MASK], rt[:, OH1], rt[:, OH2], ALU.add))
            settle()
            valid3 = valid[:, :].rearrange("p (n o) -> p n o", o=1).broadcast_to([P, 3, EXPERTS])
            ins = nc.vector.tensor_tensor(rt[:, MASK], rt[:, MASK], valid3, ALU.mult)
            ins.then_inc(mask_ready, 1)
            dve.wait_ge(gap_exp, 1)
            done(nc.vector.tensor_scalar(rs[:, 6, :], rs[:, 5, :], 1.0, None, ALU.add))
            settle()
            done(nc.vector.reciprocal(rs[:, 6, :], rs[:, 6, :]))
            settle()
            done(nc.vector.tensor_tensor(rs[:, 7, :], rs[:, 5, :], rs[:, 6, :], ALU.mult))
            settle()
            done(nc.vector.tensor_tensor(rt[:, COMB], rt[:, OH1], wide(6), ALU.mult))
            done(nc.vector.tensor_tensor(rt[:, T0], rt[:, OH2], wide(7), ALU.mult))
            settle()
            done(nc.vector.tensor_tensor(rt[:, COMB], rt[:, COMB], rt[:, T0], ALU.add))
            full(("counts",))
            pc = bank(("counts",), P, 32)
            done(nc.vector.scalar_tensor_tensor(out=rt[:, POS], in0=pc[:, 0:24].rearrange("p (n e) -> p n e", n=3), scalar=1.0,
                                                in1=rt[:, MASK], op0=ALU.add, op1=ALU.mult))
            nc.vector.tensor_copy(count[0:1, :], pc[0:1, 24:32]).then_inc(count_ready, 1)
            settle()
            done(nc.vector.tensor_scalar(rt[:, POS], rt[:, POS], -1.0, None, ALU.add))
            settle()

            dense_blocks = KB * DENSE_UNITS
            with dve.Fori(0, EXPERTS) as e:
                turns.e = e
                for n, (t0, rows) in enumerate(TILES):
                    at = rt[0:rows, POS, n, bass.ds(e, 1)]
                    nc.vector.tensor_scalar(spread[0:rows, n, :], slot_id[0:rows, :], at, None,
                                            ALU.is_equal).then_inc(spread_ready, 1)
                for n, (t0, rows) in enumerate(TILES):
                    at = rt[0:rows, POS, n, bass.ds(e, 1)]
                    nc.vector.tensor_scalar(wspread[0:rows, n, :], slot_id[0:rows, :], at,
                                            rt[0:rows, COMB, n, bass.ds(e, 1)], ALU.is_equal, ALU.mult
                                            ).then_inc(spread_ready, 1)
                nc.vector.memset(y_sum, 0.0)
                for s in range(ST):
                    full(("dwt", s))
                    nc.vector.tensor_copy(wspread_t[0:SLOT, s, :], bank(("dwt", s), SLOT)).then_inc(spread_t_ready, 1)
                with dve.Fori(0, PAIRS) as i:
                    turns.i = i
                    dve.wait_ge(spread_t_ready, e * ST + ST)
                    for u in range(2):
                        for b in range(KB):
                            name = ("g", ("moe", u), b)
                            full(name)
                            dve.wait_ge(silu_ready, e * (2 * KB * PAIRS) + i * (2 * KB)
                                        + (dense_blocks + KB * u + b + 1))
                            ins = nc.vector.tensor_tensor(hid[:, KB * u + b, :], silu[:, KB * u + b, :], bank(name), ALU.mult)
                            ins.then_inc(hid_ready, 1)
                        for j in range(DT):
                            name = ("y", ("moe", u), j)
                            full(name)
                            if j == 0:
                                dve.wait_ge(sum_ready, e * (2 * DT * PAIRS) + i * (2 * DT) + DT * (DENSE_UNITS + u))
                            ins = nc.vector.tensor_tensor(y_sum[:, j, :], y_sum[:, j, :], bank(name), ALU.add)
                            ins.then_inc(sum_ready, 1)
                    turns.i = None
                for j in range(DT):
                    full(("scatter", j))
                    ins = nc.vector.tensor_tensor(x[:, j, :], x[:, j, :], bank(("scatter", j)), ALU.add)
                    ins.then_inc(x_ready, 1)
                dve.wait_ge(x_ready, e * DT + (MIXER_SUMS + DT))
                turns.e = None
            norm(4, VEC_FIN, y_out)

        @block.tensor
        def _(pe):
            turns = Turns()

            def take(name):
                for n, when in GROUP[name][2]:
                    ready, value, per_expert, per_pair = reader(n)
                    if when == "last_pair":
                        value -= per_pair
                    if when == "end_of_pairs":
                        value += (PAIRS - 1) * per_pair
                    if when == "last_expert":
                        value -= per_expert
                    if when == "end_of_experts":
                        value += (EXPERTS - 1) * per_expert
                    pe.wait_ge(ready, turns.value(value, per_expert, 0 if when == "end_of_pairs" else per_pair))

            def give(ins):
                ins.then_inc(bank_full, 1)

            def loaded(i):
                pe.wait_ge(slot_loaded[slot_of(i)], 16 * loads_of(i))

            def slab(s, c=256):
                return ring[s][:, :].rearrange("p (k c) -> p k c", c=c)

            def mean(n):
                take(("norm", n))
                for k in range(DT):
                    pe.wait_ge(squared, DT * n + k + 1)
                    ins = nc.tensor.matmul(bank(("norm", n)), mean_w[:, :], sq[:, k, :], start=(k == 0), stop=(k == DT - 1))
                give(ins)

            def features(seg, l):
                n = 24 if seg == "gate" else BT
                for j in range(n):
                    i = STREAM[(seg, l, j // 2)]
                    loaded(i)
                    w = slab(slot_of(i))
                    take((seg, l, j))
                    for k in range(DT):
                        if seg == "ua" and j == 0:
                            pe.wait_ge(h_ready, 2 * DT * l + k + 1)
                        ins = nc.tensor.matmul(bank((seg, l, j)), w[:, k, (j % 2) * P:(j % 2 + 1) * P], h[:, k, :],
                                               start=(k == 0), stop=(k == DT - 1))
                    give(ins)

            def rows_of(seg, l):
                for hf in range(2):
                    i = STREAM[(seg, l, hf)]
                    loaded(i)
                    w = slab(slot_of(i))
                    for n, (t0, rows) in enumerate(TILES):
                        take((seg, l, hf, n))
                        for k in range(DT):
                            ins = nc.tensor.matmul(bank((seg, l, hf, n), rows, 256), h[:, k, t0:t0 + rows], w[:, k, :],
                                                   start=(k == 0), stop=(k == DT - 1))
                        give(ins)

            def scores(l):
                pe.wait_ge(qk_ready, 8 * (l + 1))
                pe.wait_ge(layer_in[3], 16 * (l + 1))
                for hd in range(HEADS):
                    r0, j = DH * (hd % 2), hd // 2
                    q, k = q_t[r0:r0 + DH, j, :], key_t[r0:r0 + DH, j, :]
                    take(("s", l, hd))
                    p = bank(("s", l, hd), P, 384)
                    nc.tensor.matmul(p[:, 0:128], q[:, 0:128], k[:, 0:128], start=True, stop=True)
                    give(nc.tensor.matmul(p[:, 128:384], q[:, 128:256], k[:, 0:256], start=True, stop=True))
                for r in range(2):
                    take(("s2", l, r))
                    for j in range(4):
                        p = bank(("s2", l, r), DEC, TOK, 32 * j)
                        q = q_t[DH * r:DH * r + DH, j, SEQ:TOK]
                        nc.tensor.matmul(p[:, 0:PAST], q, ck_t[DH * r:DH * r + DH, j, :], start=True, stop=True,
                                         tile_position=(DH * r, 32 * j))
                        ins = nc.tensor.matmul(p[:, PAST:TOK], q, key_t[DH * r:DH * r + DH, j, SEQ:TOK], start=True, stop=True,
                                               tile_position=(DH * r, 32 * j))
                    give(ins)

            def mixed(l):
                pe.wait_ge(vn_ready, 3 * (l + 1))
                pe.wait_ge(mix_masked, l + 1)
                for j in range(BT):
                    take(("mixed", l, j))
                    for n, (t0, rows) in enumerate(TILES):
                        ins = nc.tensor.matmul(bank(("mixed", l, j))[:, t0:t0 + rows], vg[0:rows, n, j * P:(j + 1) * P],
                                               wst[0:rows, j, 0:rows], start=True, stop=True)
                    give(ins)

            def attention(l):
                pe.wait_ge(prob_ready, 9 * l + 1)
                for r in range(2):
                    take(("pt2", l, r))
                    for n, rows in enumerate((P, P, DEC)):
                        ins = nc.tensor.transpose(bank(("pt2", l, r), rows, 384)[:, n * P:(n + 1) * P],
                                                  prob2[:, r, n * P:n * P + rows], ident[:, :])
                    give(ins)
                for b in range(BT):
                    for hd in (2 * b, 2 * b + 1):
                        pe.wait_ge(prob_ready, 9 * l + hd + 2)
                        take(("pt", l, hd))
                        p = bank(("pt", l, hd), P, 384)
                        for n in range(3):
                            ins = nc.tensor.transpose(p[:, n * P:(n + 1) * P], prob[:, hd, n * P:(n + 1) * P], ident[:, :])
                        give(ins)
                    take(("pv", l, b))
                    if b == 0:
                        pe.wait_ge(v_ready, 6 * (l + 1))
                        pe.wait_ge(layer_in[4], 16 * (l + 1))
                        pe.wait_ge(pt2_ready, 2 * (l + 1))
                    for hd in (2 * b, 2 * b + 1):
                        pe.wait_ge(pt_ready, 8 * l + hd + 1)
                        p = bank(("pv", l, b), DH, TOK, DH * (hd % 2))
                        t, c = pt[:, hd % 2, :], slice(DH * hd, DH * hd + DH)
                        nc.tensor.matmul(p[:, 0:128], v_tok[:, 0, c], t[:, 0:128], start=True, stop=True)
                        nc.tensor.matmul(p[:, 128:256], v_tok[:, 0, c], t[:, 128:256], start=True, stop=False)
                        nc.tensor.matmul(p[:, 128:256], v_tok[:, 1, c], t[:, 256:384], start=False, stop=True)
                        r, j = hd % 2, hd // 2
                        q = slice(32 * j, 32 * j + 32)
                        nc.tensor.matmul(p[:, 256:288], cv[:, 0, c], pt2[:, r, 0, q], start=True, stop=False)
                        nc.tensor.matmul(p[:, 256:288], cv[:, 1, c], pt2[:, r, 1, q], start=False, stop=False)
                        ins = nc.tensor.matmul(p[:, 256:288], v_tok[0:DEC, 2, c], pt2[0:DEC, r, 2, q], start=False, stop=True)
                    give(ins)

            def branches(l):
                for hf in range(2):
                    for b, (src, ready) in enumerate(((a_t, a_ready), (b_t, b_ready), (c_t, c_ready))):
                        i = STREAM[("branch", l, hf, b)]
                        loaded(i)
                        w = slab(slot_of(i), 512)
                        pe.wait_ge(ready, BT * (l + 1))
                        for j in range(4):
                            take(("branch", l, hf, b, j))
                            for k in range(BT):
                                ins = nc.tensor.matmul(bank(("branch", l, hf, b, j)), w[:, k, j * P:(j + 1) * P], src[:, k, :],
                                                       start=(k == 0), stop=(k == BT - 1))
                            give(ins)

            def project_out(l):
                for j in range(DT):
                    i = STREAM[("out", l, j // 2)]
                    loaded(i)
                    w = slab(slot_of(i))
                    take(("out", l, j))
                    for k in range(DT):
                        if j == 0:
                            pe.wait_ge(m_ready, DT * l + k + 1)
                        ins = nc.tensor.matmul(bank(("out", l, j)), w[:, k, (j % 2) * P:(j % 2 + 1) * P], m_t[k // 4][:, k % 4, :],
                                               start=(k == 0), stop=(k == DT - 1))
                    give(ins)

            def unit_in(u, src, w_a, w_g, cols, wait_a, wait_g):
                wait_a()
                for b in range(KB):
                    for s, w in (("a", w_a), ("g", w_g)):
                        if s == "g" and b == 0:
                            wait_g()
                        take((s, u, b))
                        for k in range(DT):
                            ins = nc.tensor.matmul(bank((s, u, b), P, cols), w[:, k, b * P:(b + 1) * P], src[:, k, 0:cols],
                                                   start=(k == 0), stop=(k == DT - 1))
                        give(ins)

            def unit_out(u, w, cols, buf):
                for j in range(DT):
                    take(("y", u, j))
                    for b in range(KB):
                        ins = nc.tensor.matmul(bank(("y", u, j), P, cols), w[:, b, j * P:(j + 1) * P], hid[:, buf + b, 0:cols],
                                               start=(b == 0), stop=(b == KB - 1))
                    give(ins)

            pe.wait_ge(zeroed, 3)
            pe.wait_ge(made, 4)
            for l in range(2):
                mean(NORM_OF_LAYER[l])
                features("ua", l)
                rows_of("va", l)
                features("q", l)
                features("k", l)
                rows_of("v", l)
                scores(l)
                features("cin", l)
                features("gc", l)
                features("gb", l)
                mixed(l)
                features("gate", l)
                attention(l)
                branches(l)
                project_out(l)
                mean(2 * l + 1)
                if l == 0:
                    pe.wait_ge(h_ready, DT * 2)
                    for u in range(FF // UNIT):
                        i = STREAM[("w1", u)]
                        unit_in(("dense", u), h, slab(slot_of(i)), slab(slot_of(i + 1)), TOK,
                                lambda: loaded(i), lambda: loaded(i + 1))
                        loaded(i + 2)
                        pe.wait_ge(hid_ready, KB * (u + 1))
                        unit_out(("dense", u), slab(slot_of(i + 2), D), TOK, KB * (u % 2))

            pe.wait_ge(h_ready, DT * 4)
            pe.wait_ge(layer_in[5], 32)
            take(("logits",))
            for n, (t0, rows) in enumerate(TILES):
                for k in range(DT):
                    ins = nc.tensor.matmul(bank(("logits",), rows, 24)[:, 8 * n:8 * n + 8], h[:, k, t0:t0 + rows], rw[:, k, :],
                                           start=(k == 0), stop=(k == DT - 1))
            give(ins)

            def place_tokens():
                pe.wait_ge(mask_ready, 1)
                take(("counts",))
                p = bank(("counts",), P, 32)
                for n in range(3):
                    for k in range(n + 1):
                        nc.tensor.matmul(p[:, 8 * n:8 * n + 8], before[:, :] if k == n else ones[:, :], rt[:, 5, k],
                                         start=(k == 0), stop=(k == n))
                for k in range(3):
                    ins = nc.tensor.matmul(p[:, 24:32], ones[:, :], rt[:, 5, k], start=(k == 0), stop=(k == 2))
                give(ins)

            place_tokens()
            for n, (t0, rows) in enumerate(TILES):
                for hf in range(2):
                    take(("htok", n, hf))
                    for k in range(4):
                        ins = nc.tensor.transpose(bank(("htok", n, hf), rows, 512)[:, k * P:(k + 1) * P],
                                                  h[:, 4 * hf + k, t0:t0 + rows], ident[:, :])
                    give(ins)
            pe.wait_ge(htok_ready, 6)
            pe.wait_ge(count_ready, 1)
            with pe.Fori(0, EXPERTS) as e:
                turns.e = e
                routed = pe.value_load(count[0:1, bass.ds(e, 1)], min_val=0, max_val=TOK)

                def expert(tiles):
                    cols = tiles * SLOT
                    pe.wait_ge(spread_ready, e * 6 + 3)
                    for j in range(DT):
                        take(("gather", j))
                        for n, (t0, rows) in enumerate(TILES):
                            ins = nc.tensor.matmul(bank(("gather", j), P, cols), h_tok[0:rows, n, j * P:(j + 1) * P],
                                                   spread[0:rows, n, 0:cols], start=(n == 0), stop=(n == 2))
                        give(ins)
                    pe.wait_ge(spread_ready, e * 6 + 6)
                    for s in range(ST):
                        take(("dwt", s))
                        for n, (t0, rows) in enumerate(TILES):
                            ins = nc.tensor.transpose(bank(("dwt", s), SLOT)[:, t0:t0 + rows],
                                                      wspread[0:rows, n, s * SLOT:(s + 1) * SLOT], ident[0:rows, 0:rows])
                        give(ins)
                    with pe.Fori(0, PAIRS) as i:
                        turns.i = i
                        pe.wait_ge(he_ready, e * DT + DT)
                        def slot_full(s):
                            before_experts = len([1 for m in range(LEAD) if slot_of(m) == s])
                            pe.wait_ge(slot_loaded[s], e * (16 * PAIRS) + i * 16 + 16 * (before_experts + 1))

                        for u in range(2):
                            unit_in(("moe", u), he, slab(3 * u), slab(3 * u + 1), cols,
                                    lambda: slot_full(3 * u), lambda: slot_full(3 * u + 1))
                            slot_full(3 * u + 2)
                            pe.wait_ge(hid_ready, e * (2 * KB * PAIRS) + i * (2 * KB)
                                       + (KB * (FF // UNIT) + KB * (u + 1)))
                            unit_out(("moe", u), slab(3 * u + 2, D), cols, KB * u)
                        turns.i = None
                    pe.wait_ge(sum_ready, e * (2 * DT * PAIRS) + DT * (DENSE_UNITS + 2 * PAIRS))
                    for s in range(ST):
                        for hf in range(2):
                            take(("ytok", s, hf))
                            for k in range(4):
                                ins = nc.tensor.transpose(bank(("ytok", s, hf), SLOT, 512)[:, k * P:(k + 1) * P],
                                                          y_sum[:, 4 * hf + k, s * SLOT:(s + 1) * SLOT], ident[:, :])
                            give(ins)
                    pe.wait_ge(ytok_ready, e * (2 * ST) + 2 * ST)
                    pe.wait_ge(spread_t_ready, e * ST + ST)
                    for j in range(DT):
                        take(("scatter", j))
                        for s in range(tiles):
                            ins = nc.tensor.matmul(bank(("scatter", j)), y_tok[0:SLOT, s, j * P:(j + 1) * P],
                                                   wspread_t[0:SLOT, s, :], start=(s == 0), stop=(s == tiles - 1))
                        give(ins)

                with pe.If(routed <= SLOT):
                    expert(1)
                with pe.Else():
                    expert(ST)
                turns.e = None
            mean(4)


def kernel(**inputs):
    import concourse.bacc as _bacc
    from concourse.bass_utils import run_bass_kernel_spmd as _run

    a = {k: np.asarray(v) for k, v in inputs.items()}

    def columns(v):
        return v.reshape(-1, P).T

    vecs = np.concatenate([
        columns(a["norm_mix_g"]), columns(a["norm_ffn_g"]), columns(a["final_norm_g"]),
        columns(a["conv_w"]),
        a["state_conv"].reshape(2, 2, BT, P).transpose(3, 0, 2, 1).reshape(P, 16)], axis=1)
    arrays = {
        "x_t": np.concatenate([a["x_prompt"][0], a["x_sample"][0]], axis=0).T,
        "vecs": vecs,
        "w_in": a["w_in"],
        "cache_k_t": a["cache_attn_k"].reshape(2, PAST, HALF).transpose(0, 2, 1),
        "cache_v": a["cache_attn_v"].reshape(2, PAST, HALF),
        "ws_t": a["gmlp_ws"].transpose(0, 3, 1, 2),
        "bs": a["gmlp_bs"].reshape(2, HALF),
        "g_v": a["gmlp_norm_g"],
        "bias_rev": a["attn_rel_bias"][:, :, ::-1],
        "w_branch": a["w_branch"],
        "w_out": a["w_out"],
        "w1": a["ffn_w1"][0], "w3": a["ffn_w3"][0], "w2": a["ffn_w2"][0],
        "router": a["moe_router"][0], "router_b": a["moe_router_b"],
        "e_w1": a["moe_w1"][0], "e_w3": a["moe_w3"][0], "e_w2": a["moe_w2"][0],
    }
    outs = {"y_t": (D, TOK), "k_t": (2, HALF, TOK), "v_rows": (2, TOK, HALF), "z_state": (2, P, BT, 4),
            "vn_rows": (2, DEC, HALF)}
    nc = _bacc.Bacc("TRN2", target_bir_lowering=False, num_devices=1)
    feed, args = {}, {}
    for name, v in arrays.items():
        v = np.ascontiguousarray(v)
        feed[f"in_{name}"] = v
        args[name] = nc.dram_tensor(f"in_{name}", v.shape, mybir.dt.from_np(v.dtype), kind="ExternalInput").ap()
    for name, shape in outs.items():
        args[name] = nc.dram_tensor(f"out_{name}", shape, mybir.dt.float32, kind="ExternalOutput").ap()
    encoder(nc, **args)
    r = _run(nc, [feed], core_ids=[0]).results[0]
    y, kt, vr = r["out_y_t"].T, r["out_k_t"].transpose(0, 2, 1), r["out_v_rows"]
    zs = r["out_z_state"].transpose(0, 3, 2, 1).reshape(2, 4, HALF)
    k5, v5 = (t.reshape(2, 1, TOK, HEADS, DH) for t in (kt, vr))
    c = np.ascontiguousarray
    return (c(y[None, :SEQ]), c(y[None, SEQ:]), c(k5[:, :, :SEQ]), c(v5[:, :, :SEQ]), c(zs[:, None, 0:2]),
            c(k5[:, :, SEQ:]), c(v5[:, :, SEQ:]), c(zs[:, None, 2:4]), c(r["out_vn_rows"][:, None]))
```

```python
import numpy as np
import concourse.bass as bass
from concourse import mybir
from contextlib import ExitStack

P = 128
D = 1024
DT = D // P
SEQ, DEC = 256, 32
TOK = SEQ + DEC
TILES = [(0, 128), (128, 128), (256, 32)]
HALF = D // 2
BT = HALF // P
HEADS, DH = 8, 64
CHUNK = 64
PAST = 256
CLIP = 128
TAB = 2 * CLIP + 1
IN_COLS = 7 * D
FF = 2816
EXPERTS = 8
FFE = 3584
SLOT = 128
EPS = 1e-6
MASKED = -1e30
SCALE = DH ** -0.5

RING = 4
EXPERT_RING = 6
UNIT = 256
KB = UNIT // P
UNITS = FFE // UNIT
DENSE_UNITS = FF // UNIT
TURNS = UNITS // 2 - 1
CHUNK_W = 1024
CHUNKS = 4
JOB_CHUNKS = 6 * UNITS
JOB_MATRICES = 3 * UNITS
MAX_JOBS = EXPERTS + 4
BIAS_W = 384
EXT = 512

VEC_MIX, VEC_FFN, VEC_FIN, VEC_CONV, VEC_STATE = 0, 16, 32, 40, 64
VECS = 80


def mixer_matrices(l):
    names = []
    for seg in ("q", "k", "v", "ua", "va", "cin", "gc", "gb"):
        names += [(seg, l, i) for i in range(2)]
    for h in range(2):
        for b in range(3):
            names += [("gate", l, 4 * b + 2 * h), ("gate", l, 4 * b + 2 * h + 1), ("branch", l, h, b)]
    names += [("out", l, i) for i in range(4)]
    return names


SEGMENT = {"ua": 0, "va": 1, "q": 2, "k": 3, "v": 4, "cin": 5, "gb": 6, "gc": 7, "gate": 8}


def weight_stream():
    names = mixer_matrices(0)
    for u in range(FF // UNIT + 1):
        if u < FF // UNIT:
            names += [("w1", u), ("w3", u)]
        if u:
            names += [("w2", u - 1)]
    names += mixer_matrices(1)
    return {n: i for i, n in enumerate(names)}


STREAM = weight_stream()
LEAD = len(STREAM)


def slot_of(i):
    return i % RING


def loads_of(i):
    return i // RING + 1


def mixer_groups(l):
    g = [("norm", 2 * l)]
    g += [("q", l, j) for j in range(BT)] + [("k", l, j) for j in range(BT)]
    g += [("v", l, h, n) for h in range(2) for n in range(3)]
    g += [("s", l, h) for h in range(HEADS)] + [("s2", l, r) for r in range(2)]
    g += [("ua", l, j) for j in range(BT)]
    g += [("va", l, h, n) for h in range(2) for n in range(3)]
    g += [(s, l, j) for s in ("cin", "gc", "gb") for j in range(BT)]
    g += [("mixed", l, j) for j in range(BT)]
    g += [("pt2", l, r) for r in range(2)]
    for b in range(BT):
        g += [("pt", l, 2 * b), ("pt", l, 2 * b + 1), ("pv", l, b)]
    for h in range(2):
        for b in range(3):
            g += [("gate", l, 12 * h + 4 * b + j) for j in range(4)]
            g += [("branch", l, h, b, j) for j in range(4)]
    g += [("out", l, j) for j in range(DT)]
    g += [("norm", 2 * l + 1)]
    return g


def groups_in(u):
    return [(s, u, b) for b in range(KB) for s in ("a", "g")]


def groups_out(u):
    return [("y", u, j) for j in range(DT)]


UNIT_AT = {"first": 0, "odd": 1, "next": 2, "last": UNITS - 1}
CHUNKS_IN = {"first": 4, "odd": 8, "next": 14, "last": JOB_CHUNKS - 4}


def counted(names):
    return len([n for n in names if n[0] != "ag"])


class Groups:

    def __init__(self):
        self.at, self.total, self.next, self.banks = {}, 0, 0, 8
        self.last = [[] for _ in range(8)]

    def add(self, names):
        for n in names:
            b, self.next = self.next, (self.next + 1) % self.banks
            self.at[n] = (b, self.total, list(self.last[b]))
            self.last[b] = [(n, "same")]
            self.total += counted([n])

    def close_loop(self, names, turns, back, end):
        for b in range(8):
            inside = [n for n in names if self.at[n][0] == b]
            if inside:
                self.at[inside[0]][2].append((inside[-1], back))
                self.last[b] = [(inside[-1], end)]
        self.total += (turns - 1) * counted(names)
        self.next = (self.at[names[-1]][0] + 1) % self.banks


def number_groups():
    g = Groups()
    g.add(mixer_groups(0))
    for u in range(DENSE_UNITS + 1):
        if u < DENSE_UNITS:
            g.add(groups_in(("dense", u)))
        if u:
            g.add(groups_out(("dense", u - 1)))
    g.add(mixer_groups(1))
    g.add([("logits",), ("counts",)] + [("htok", n, h) for n in range(3) for h in range(2)])
    g.next, g.banks = 0, 6
    g.add([("gather0", h) for h in range(2)])
    start = g.total
    g.add([("ag", "first"), ("tr", "first")])
    turn = [("ag", "odd"), ("tr", "odd"), ("ag", "next"), ("tr", "next")]
    g.add(turn)
    g.close_loop(turn, TURNS, "last_turn", "end_of_turns")
    g.add([("ag", "last"), ("tr", "last"), ("dwt", 0)] + [("gather", h) for h in range(2)])
    g.add([("scatter", j) for j in range(DT)])
    per_job = g.total - start
    g.close_loop([n for n in g.at if g.at[n][1] >= start], 1, "last_job", "last_job")
    g.total = start
    g.add([("norm", 4)])
    return g.at, counted(turn), per_job


GROUP, PER_TURN, PER_JOB = number_groups()


class Turns:

    def __init__(self):
        self.job = self.i = None

    def value(self, base, per_job, per_turn=0):
        v = base
        if self.job is not None and per_job:
            v = self.job * per_job + v
        if self.i is not None and per_turn:
            v = self.i * per_turn + v
        return v

    def full(self, name):
        return self.value(GROUP[name][1] + 1, PER_JOB, PER_TURN)

    def chunk(self, c, in_turn):
        return self.value(c + 1, JOB_CHUNKS, 12 if in_turn else 0)


EXPERT_STREAM = [(0, 0), (1, 0),
                 (0, 1), (1, 1), (2, 0), (0, 2), (1, 2), (2, 1),
                 (0, UNITS - 1), (1, UNITS - 1), (2, UNITS - 2), (2, UNITS - 1)]


def last_uses():
    uses = []
    for n in STREAM:
        kind = n[0]
        if kind in ("va", "v"):
            uses.append((kind, n[1], n[2], 2))
        elif kind == "branch":
            uses.append(("branch", n[1], n[2], n[3], 3))
        elif kind == "gate":
            b, h, k = n[2] // 4, n[2] // 2 % 2, n[2] % 2
            uses.append(("gate", n[1], 12 * h + 4 * b + 2 * k + 1))
        elif kind in ("w1", "w3", "w2"):
            uses.append({"w1": ("a", ("dense", n[1]), KB - 1), "w3": ("g", ("dense", n[1]), KB - 1),
                         "w2": ("y", ("dense", n[1]), DT - 1)}[kind])
        else:
            uses.append((kind, n[1], 2 * n[2] + 1))
    return uses


LAST_USE = last_uses()
MIXER_SUMS = 2 * DT


def encoder(nc, x_t, vecs, w_in, cache_k_t, cache_v, ws_t, bs, g_v, bias_rev, w_branch, w_out,
            w1, w3, w2, router, router_b, e_w1, e_w3, e_w2, y_t, k_t, v_rows, z_state, vn_rows):
    f32, i32 = mybir.dt.float32, mybir.dt.int32
    ALU, ACT, AX = mybir.AluOpType, mybir.ActivationFunctionType, mybir.AxisListType
    ctx = ExitStack()
    with ctx:
        def sb(name, shape, dt=f32):
            return ctx.enter_context(nc.sbuf_tensor(name, shape, dt))

        def sem(name):
            return ctx.enter_context(nc.semaphore(name))

        bias_ext = nc.dram_tensor("bias_ext", [2, P, HEADS * EXT], f32).ap()

        ring = [sb(f"ring{i}", [P, 2048]) for i in range(RING)]
        x = sb("x", [P, DT, TOK])
        h = sb("h", [P, DT, TOK])
        rms = sb("rms", [P, TOK])
        rstd = sb("rstd", [P, TOK])
        eps = sb("eps", [P, 1])
        vec = sb("vec", [P, VECS])
        mean_w = sb("mean_w", [P, P])
        ident = sb("ident", [P, P])
        ones = sb("ones", [P, P])
        before = sb("before", [P, P])
        slot_id = sb("slot_id", [P, TOK])
        rank = sb("rank", [P, 3, EXPERTS])
        valid = sb("valid", [P, 3])
        rows6 = sb("rows6", [P, 6, HALF])
        vg = rows6[:, 0:3, :]
        v_tok = rows6[:, 3:6, :]
        vsq = sb("vsq", [P, 3])
        vrs = sb("vrs", [P, 3])
        q_t = sb("q_t", [P, BT, TOK])
        key_t = sb("key_t", [P, BT, TOK])
        spare0 = sb("spare0", [P, 2048])
        spare1 = sb("spare1", [P, 2112])
        ck_t = spare0[:, 0:1024].rearrange("p (a b) -> p a b", a=BT)
        cv = spare0[:, 1024:2048].rearrange("p (a b) -> p a b", a=2)
        wst = spare1[:, 0:512].rearrange("p (a b) -> p a b", a=BT)
        bsb = spare1[:, 512:1024].rearrange("p (a b) -> p a b", a=BT)
        gvb = spare1[:, 1024:1536]
        bias = sb("bias", [P, HEADS, BIAS_W])
        bias2 = spare1[:, 1536:2112].rearrange("p (a b) -> p a b", a=2)
        attn = sb("attn", [P, 4416])
        prob = attn[:, 0:3072].rearrange("p (h c) -> p h c", h=HEADS)
        prob2 = attn[:, 3072:3648].rearrange("p (h c) -> p h c", h=2)
        pt = attn[:, 3648:4416].rearrange("p (h c) -> p h c", h=2)
        top = sb("top", [P, 2 * HEADS + 2])
        total = sb("total", [P, 2 * HEADS + 2])
        part = sb("part", [P, 2 * HEADS + 2])
        pt2 = sb("pt2", [P, 2, 3, P])
        z = sb("z", [P, BT, TOK + 4])
        gate = sb("gate", [P, 4, TOK])
        a_t = sb("a_t", [P, BT, TOK])
        b_t = sb("b_t", [P, BT, TOK])
        c_t = sb("c_t", [P, BT, TOK])
        tmp = sb("tmp", [P, 2, TOK + 4])
        silu, hid = q_t, key_t
        e_silu = q_t[:, :, :].rearrange("p a b -> p (a b)")[:, 0:UNIT]
        e_hid = key_t[:, :, :].rearrange("p a b -> p (a b)")[:, 0:UNIT]
        f32r = mybir.dt.float32r
        w_hi = [sb(f"w_hi{i}", [P, CHUNK_W], f32r) for i in range(CHUNKS)]
        w_lo = [sb(f"w_lo{i}", [P, CHUNK_W], f32r) for i in range(CHUNKS)]
        he_hi, he_lo = (sb(n, [P, DT, SLOT], f32r) for n in ("he_hi", "he_lo"))
        hid_hi, hid_lo = (sb(n, [P, KB, SLOT], f32r) for n in ("hid_hi", "hid_lo"))
        rw = sb("rw", [P, DT, EXPERTS])
        rb = sb("rb", [P, EXPERTS])
        place = sb("place", [P, 3, EXPERTS])
        weight = sb("weight", [P, 3, EXPERTS])
        job_expert = sb("job_expert", [1, MAX_JOBS + 1], i32)
        job_base = sb("job_base", [P, MAX_JOBS + 1])
        job_count = sb("job_count", [1, 2], i32)
        starts = sb("starts", [P, EXPERTS + 1])
        job_no = sb("job_no", [P, MAX_JOBS + 1])
        job_hit = sb("job_hit", [P, MAX_JOBS + 1, EXPERTS])
        rows_flat = rows6[:, :, :].rearrange("p a b -> p (a b)")
        sq = rows_flat[:, 0:DT * TOK].rearrange("p (a b) -> p a b", a=DT)
        m_t = q_t, key_t
        ext = attn[:, 0:HEADS * EXT].rearrange("p (h c) -> p h c", h=HEADS)
        h_tok = rows_flat[:, 0:3 * D].rearrange("p (n d) -> p n d", n=3)
        bias_flat = bias[:, :, :].rearrange("p a b -> p (a b)")
        zero_row = bias_flat[0:1, D:D + 512]
        y_tok = bias_flat[:, 0:D]
        spread = a_t[:, 0:3, 0:SLOT]
        wspread = b_t[:, 0:3, 0:SLOT]
        wspread_t = c_t[:, 0, :]
        rt = gate[:, 0, 0:288].rearrange("p (a n e) -> p a n e", a=12, n=3)
        rs = gate[:, 1, 0:24].rearrange("p (a n) -> p a n", a=8)
        expert_ring = ring + [spare0[:, :], spare1[:, 0:2048]]
        psum = ctx.enter_context(nc.psum_tensor("psum", [P, 8, 512], f32))

        slot_loaded = [sem(f"slot_loaded{i}") for i in range(EXPERT_RING)]
        bank_full = sem("bank_full")
        x_in = [sem("x_in0"), sem("x_in1")]
        vec_in = sem("vec_in")
        made = sem("made")
        dve_step = sem("dve_step")
        rms_ready = sem("rms_ready")
        rstd_ready = sem("rstd_ready")
        vrms_ready = sem("vrms_ready")
        vg_ready = sem("vg_ready")
        score_ready = sem("score_ready")
        gc_read = sem("gc_read")
        mixed_read = sem("mixed_read")
        branch_read = sem("branch_read")
        logits_read = sem("logits_read")
        sum_ready = sem("sum_ready")
        rows_stored = sem("rows_stored")
        keys_stored = sem("keys_stored")
        values_stored = sem("values_stored")
        state_stored = sem("state_stored")
        pool_step = sem("pool_step")
        zeroed = sem("zeroed")
        squared = sem("squared")
        h_ready = sem("h_ready")
        layer_in = [sem(f"layer_in{i}") for i in range(6)]
        ext_loaded = sem("ext_loaded")
        ext_ready = sem("ext_ready")
        ext_stored = sem("ext_stored")
        bias_loaded = sem("bias_loaded")
        bias2_loaded = sem("bias2_loaded")
        bias_masked = sem("bias_masked")
        mix_masked = sem("mix_masked")
        u_ready = sem("u_ready")
        vsq_ready = sem("vsq_ready")
        vn_ready = sem("vn_ready")
        qk_ready = sem("qk_ready")
        v_ready = sem("v_ready")
        top_ready = sem("top_ready")
        exp_ready = sem("exp_ready")
        prob_ready = sem("prob_ready")
        pt_ready = sem("pt_ready")
        pt2_ready = sem("pt2_ready")
        cin_ready = sem("cin_ready")
        z_ready = sem("z_ready")
        gate_ready = sem("gate_ready")
        a_ready = sem("a_ready")
        b_ready = sem("b_ready")
        c_ready = sem("c_ready")
        m_ready = sem("m_ready")
        x_ready = sem("x_ready")
        silu_ready = sem("silu_ready")
        hid_ready = sem("hid_ready")
        mask_ready = sem("mask_ready")
        gap_ready = sem("gap_ready")
        gap_exp = sem("gap_exp")
        count_ready = sem("count_ready")
        htok_ready = sem("htok_ready")
        spread_ready = sem("spread_ready")
        he_hi_ready = sem("he_hi_ready")
        he_ready = sem("he_ready")
        rounded = sem("rounded")
        split = sem("split")
        chunk_used = sem("chunk_used")
        hid_hi_ready = sem("hid_hi_ready")
        jobs_ready = sem("jobs_ready")
        spread_t_ready = sem("spread_t_ready")
        ytok_ready = sem("ytok_ready")
        y_out = sem("y_out")
        out_done = sem("out_done")
        NORM_OF_LAYER = (0, 2)

        slot_before = [len([1 for i in range(LEAD) if slot_of(i) == s]) for s in range(EXPERT_RING)]
        GELU_BUFS = ((b_t, 0), (c_t, 0), (b_t, 2))

        def chunk_at(at, half):
            return at % EXPERT_RING, (2 * at + half) % CHUNKS

        def bank(name, rows=P, cols=TOK, row0=0):
            return psum[row0:row0 + rows, GROUP[name][0], 0:cols]

        def reader(name):
            kind, at = name[0], name[1:]
            if kind in ("a", "g", "y"):
                (_, u), j = at
                n, ready = {"a": (KB, silu_ready), "g": (KB, hid_ready), "y": (DT, sum_ready)}[kind]
                return ready, n * u + j + 1, 0, 0
            if kind in ("ag", "tr"):
                u = at[0]
                per_turn = 4 if u in ("odd", "next") else 0
                return hid_ready, KB * DENSE_UNITS + 2 * UNIT_AT[u] + (1 if kind == "ag" else 2), 2 * UNITS, per_turn
            if kind == "branch":
                l, hf, b, j = at
                return branch_read, 24 * l + 12 * hf + 4 * b + j + 1, 0, 0
            if kind in ("va", "v"):
                l, hf, n = at
                return {"va": vg_ready, "v": v_ready}[kind], 6 * l + 3 * hf + n + 1, 0, 0
            if kind == "htok":
                return htok_ready, 2 * at[0] + at[1] + 1, 0, 0
            if kind == "gather0":
                return he_ready, at[0] + 1, 0, 0
            once = {"gather": (he_ready, 2, 2), "dwt": (spread_t_ready, 1, 0), "scatter": (x_ready, DT, MIXER_SUMS)}
            if kind in once:
                ready, n, base = once[kind]
                return ready, base + at[0] + 1, n, 0
            if kind in ("logits", "counts"):
                return {"logits": logits_read, "counts": count_ready}[kind], 1, 0, 0
            if kind == "norm":
                return rms_ready, at[0] + 1, 0, 0
            ready, per_layer, first = {
                "ua": (u_ready, BT, 0), "q": (qk_ready, 2 * BT, 0), "k": (qk_ready, 2 * BT, BT),
                "s": (score_ready, HEADS + 2, 0), "s2": (score_ready, HEADS + 2, HEADS),
                "cin": (cin_ready, BT, 0), "gc": (gc_read, BT, 0), "gb": (c_ready, BT, 0),
                "mixed": (mixed_read, BT, 0), "gate": (gate_ready, 24, 0), "pt2": (pt2_ready, 2, 0),
                "pt": (pt_ready, HEADS, 0), "pv": (b_ready, BT, 0), "out": (x_ready, DT, 0)}[kind]
            return ready, per_layer * at[0] + first + at[1] + 1, 0, 0

        block = ctx.enter_context(nc.Block())

        @block.sync
        def _(sp):
            def load(i, dst, src):
                if i >= RING:
                    sp.wait_ge(bank_full, GROUP[LAST_USE[i - RING]][1] + 1)
                sp.dma_start(dst, src).then_inc(slot_loaded[slot_of(i)], 16)

            def tall(s, c=256):
                return ring[s][:, :].rearrange("p (k c) -> p k c", c=c)

            def mixer(l):
                for n in mixer_matrices(l):
                    i = STREAM[n]
                    s = slot_of(i)
                    if n[0] == "branch":
                        _, _, half, b = n
                        src = w_branch[l, b, :, half * 512:(half + 1) * 512]
                        load(i, tall(s, 512), src.rearrange("(k p) c -> p k c", p=P))
                    elif n[0] == "out":
                        load(i, tall(s), w_out[l, :, n[2] * 256:(n[2] + 1) * 256].rearrange("(k p) c -> p k c", p=P))
                    else:
                        c = SEGMENT[n[0]] * 512 + n[2] * 256
                        load(i, tall(s), w_in[l, :, c:c + 256].rearrange("(k p) c -> p k c", p=P))

            mixer(0)
            for u in range(DENSE_UNITS + 1):
                if u < DENSE_UNITS:
                    for k, w in enumerate((w1, w3)):
                        i = STREAM[("w1", u)] + k
                        load(i, tall(slot_of(i)), w[:, u * UNIT:(u + 1) * UNIT].rearrange("(k p) c -> p k c", p=P))
                if u:
                    i = STREAM[("w2", u - 1)]
                    load(i, tall(slot_of(i), D), w2[(u - 1) * UNIT:u * UNIT, :].rearrange("(k p) c -> p k c", p=P))
            mixer(1)

            def expert_matrix(e, m, unit):
                which = EXPERT_STREAM[m][0]
                s = m % EXPERT_RING
                dst = expert_ring[s][:, 0:2048].rearrange("p (k c) -> p k c", c=D if which == 2 else UNIT)
                cols = bass.ds(unit * UNIT, UNIT)
                src = e_w2[bass.ds(e, 1), cols, :] if which == 2 else (e_w1, e_w3)[which][bass.ds(e, 1), :, cols]
                sp.dma_start(dst, src.rearrange("o (k p) c -> p (o k) c", p=P)).then_inc(slot_loaded[s], 16)

            HEAD, TAIL = 2, 8

            def split_before(job, m, turn):
                at = m + JOB_MATRICES - len(EXPERT_STREAM) if m >= TAIL else m
                value = job * JOB_CHUNKS + 2 * (at - EXPERT_RING + 1 + (0 if turn is None else EXPERT_RING))
                sp.wait_ge(split, value if turn is None else turn * (2 * EXPERT_RING) + value)


            def other_matrices(job, e):
                for m in range(EXPERT_RING, TAIL):
                    split_before(job, m, None)
                    expert_matrix(e, m, EXPERT_STREAM[m][1])
                with sp.Fori(0, TURNS - 1) as i:
                    for m in range(HEAD, TAIL):
                        split_before(job, m, i)
                        expert_matrix(e, m, i * 2 + (2 + EXPERT_STREAM[m][1]))
                for m in range(TAIL, len(EXPERT_STREAM)):
                    split_before(job, m, None)
                    expert_matrix(e, m, EXPERT_STREAM[m][1])

            for m in range(EXPERT_RING):
                if m < RING:
                    last = max(i for i in range(LEAD) if slot_of(i) == m)
                    sp.wait_ge(bank_full, GROUP[LAST_USE[last]][1] + 1)
                else:
                    sp.wait_ge(a_ready, 2 * BT)
                    sp.wait_ge(b_ready, 2 * BT)
                expert_matrix(0, m, EXPERT_STREAM[m][1])
            sp.wait_ge(jobs_ready, 1)
            last_job = sp.value_load(job_count[0:1, 1:2], min_val=EXPERTS - 1, max_val=MAX_JOBS - 1)
            with sp.Fori(0, last_job) as job:
                e = sp.value_load(job_expert[0:1, bass.ds(job, 1)], min_val=0, max_val=EXPERTS - 1)
                other_matrices(job, e)
                e_next = sp.value_load(job_expert[0:1, bass.ds(job + 1, 1)], min_val=0, max_val=EXPERTS - 1)
                for m in range(EXPERT_RING):
                    sp.wait_ge(split, job * JOB_CHUNKS + (JOB_CHUNKS + 2 * (m - EXPERT_RING + 1)))
                    expert_matrix(e_next, m, EXPERT_STREAM[m][1])
            e = sp.value_load(job_expert[0:1, bass.ds(last_job, 1)], min_val=0, max_val=EXPERTS - 1)
            other_matrices(last_job, e)

        @block.gpsimd
        def _(pool):
            nc.gpsimd.memset(ident[:, :], 0.0).then_inc(pool_step, 1)
            nc.gpsimd.memset(ones[:, :], 1.0).then_inc(pool_step, 1)
            nc.gpsimd.memset(before[:, :], 1.0).then_inc(pool_step, 1)
            nc.gpsimd.iota(slot_id[:, :], pattern=[[1, TOK]], base=0, channel_multiplier=0,
                           allow_small_or_imprecise_dtypes=True).then_inc(made, 1)
            nc.gpsimd.iota(job_no[:, :], pattern=[[1, MAX_JOBS + 1]], base=0, channel_multiplier=0,
                           allow_small_or_imprecise_dtypes=True).then_inc(made, 1)
            nc.gpsimd.iota(rank[:, :, :], pattern=[[0, 3], [-1, EXPERTS]], base=EXPERTS, channel_multiplier=0,
                           allow_small_or_imprecise_dtypes=True).then_inc(made, 1)
            pool.wait_ge(pool_step, 3)
            nc.gpsimd.affine_select(out=ident[:, :], in_=ident[:, :], compare_op=ALU.not_equal, fill=1.0,
                                    base=0, pattern=[[-1, P]], channel_multiplier=1).then_inc(made, 1)
            nc.gpsimd.affine_select(out=before[:, :], in_=before[:, :], compare_op=ALU.is_gt, fill=0.0,
                                    base=0, pattern=[[1, P]], channel_multiplier=-1).then_inc(made, 1)

            def layer_inputs(l):
                if l:
                    pool.wait_ge(a_ready, BT)
                    pool.wait_ge(b_ready, BT)
                pool.dma_start(wst[:, :, :], ws_t[l]).then_inc(layer_in[0], 16)
                pool.dma_start(bsb[:, :, :].rearrange("p a b -> p (a b)"),
                               bs[l:l + 1, :].broadcast_to([P, HALF])).then_inc(layer_in[1], 16)
                pool.dma_start(gvb[:, :], g_v[l:l + 1, :].broadcast_to([P, HALF])).then_inc(layer_in[2], 16)
                pool.dma_start(ck_t[:, :, :], cache_k_t[l].rearrange("(j p) t -> p j t", p=P)).then_inc(layer_in[3], 16)
                pool.dma_start(cv[:, :, :], cache_v[l].rearrange("(n p) c -> p n c", p=P)).then_inc(layer_in[4], 16)

            def bias_rows():
                for l in range(2):
                    if l:
                        pool.wait_ge(ext_stored, 16 * l)
                    pool.dma_start(ext[:, :, EXT // 2 - 1:EXT - 1],
                                   bias_rev[l:l + 1, :, 0:TAB - 1].broadcast_to([P, HEADS, TAB - 1]),
                                   ).then_inc(ext_loaded, 16)
                    pool.wait_ge(ext_ready, l + 1)
                    pool.dma_start(bias_ext[l], ext.rearrange("p h c -> p (h c)")).then_inc(ext_stored, 16)

            def bias_tiles(l):
                row = HEADS * EXT
                pool.dma_start(bias[:, :, :], bass.AP(bias_ext.tensor, bias_ext[l].offset + 127,
                                                      [[row - 1, P], [EXT, HEADS], [1, BIAS_W]])
                               ).then_inc(bias_loaded, 16)
                for j in range(4):
                    for r in range(2):
                        head = 2 * j + r
                        pool.dma_start(bias2[32 * j:32 * j + 32, r, :],
                                       bass.AP(bias_ext.tensor, bias_ext[l].offset + head * EXT + 127,
                                               [[row - 1, DEC], [1, TOK]])).then_inc(bias2_loaded, 16)

            pool.dma_start(vec[:, :], vecs).then_inc(vec_in, 16)
            bias_rows()
            pool.wait_ge(ext_stored, 32)
            layer_inputs(0)
            bias_tiles(0)
            pool.dma_start(rw[:, :, :], router.rearrange("(k p) e -> p k e", p=P)).then_inc(layer_in[5], 16)
            pool.dma_start(rb[:, :], router_b.broadcast_to([P, EXPERTS])).then_inc(layer_in[5], 16)
            for l in range(2):
                pool.wait_ge(vn_ready, 3 * (l + 1))
                pool.dma_start(vn_rows[l], vg[0:DEC, 2, :]).then_inc(rows_stored, 16)
                pool.wait_ge(qk_ready, 8 * (l + 1))
                pool.dma_start(k_t[l].rearrange("(j p) t -> p j t", p=P), key_t[:, :, :]).then_inc(keys_stored, 16)
                pool.wait_ge(v_ready, 6 * (l + 1))
                pool.dma_start(v_rows[l, 0:SEQ, :].rearrange("(n p) c -> p n c", p=P),
                               v_tok[:, 0:2, :]).then_inc(values_stored, 16)
                pool.dma_start(v_rows[l, SEQ:TOK, :], v_tok[0:DEC, 2, :]).then_inc(values_stored, 16)
                pool.wait_ge(z_ready, BT * (l + 1))
                for at, to in ((SEQ, 0), (TOK + 2, 2)):
                    pool.dma_start(z_state[l, :, :, to:to + 2], z[:, :, at:at + 2]).then_inc(state_stored, 16)
                if l == 0:
                    layer_inputs(1)
                    bias_tiles(1)
            pool.wait_ge(y_out, DT)
            pool.dma_start(y_t.rearrange("(k p) t -> p k t", p=P), h[:, :, :]).then_inc(out_done, 16)
            pool.wait_ge(out_done, 16)
            pool.wait_ge(rows_stored, 32)
            pool.wait_ge(keys_stored, 32)
            pool.wait_ge(values_stored, 64)
            pool.wait_ge(state_stored, 64)

        @block.scalar
        def _(act):
            turns = Turns()
            x_dram = x_t.rearrange("(k p) t -> p k t", p=P)
            for k in range(2):
                act.dma_start(x[:, 4 * k:4 * k + 4, :], x_dram[:, 4 * k:4 * k + 4, :]).then_inc(x_in[k], 16)
            act.wait_ge(zeroed, 3)

            def squares(n):
                if n in (1, 3):
                    act.wait_ge(rows_stored, 16 * (n // 2 + 1))
                    act.wait_ge(values_stored, 32 * (n // 2 + 1))
                for k in range(DT):
                    if n == 0:
                        act.wait_ge(x_in[k // 4], 16)
                    if n in (1, 3):
                        act.wait_ge(x_ready, DT * (n // 2) + k + 1)
                    elif n == 2:
                        act.wait_ge(sum_ready, DT * (DENSE_UNITS - 1) + k + 1)
                    elif n == 4:
                        act.wait_ge(x_ready, turns.job * DT + (MIXER_SUMS - DT + k + 1))
                    nc.scalar.activation(sq[:, k, :], x[:, k, :], ACT.Square).then_inc(squared, 1)

            def root(n):
                act.wait_ge(bank_full, turns.full(("norm", n)))
                nc.scalar.activation(rms[:, :], bank(("norm", n)), ACT.Sqrt, bias=eps[:, 0:1]).then_inc(rms_ready, 1)

            def evacuate(name, dst, rows, cols, done, func=ACT.Copy, scale=1.0):
                act.wait_ge(bank_full, turns.full(name))
                nc.scalar.activation(dst, bank(name, rows, cols), func, scale=scale).then_inc(done, 1)

            for l in range(2):
                squares(NORM_OF_LAYER[l])
                root(NORM_OF_LAYER[l])
                for hf in range(2):
                    for n, (t0, rows) in enumerate(TILES):
                        evacuate(("v", l, hf, n), v_tok[0:rows, n, hf * 256:(hf + 1) * 256], rows, 256, v_ready)
                for hd in range(HEADS):
                    act.wait_ge(top_ready, 9 * l + hd + 1)
                    for t, (c0, c1) in enumerate(((0, 128), (128, 384))):
                        ins = nc.scalar.activation(prob[:, hd, c0:c1], prob[:, hd, c0:c1], ACT.Exp,
                                                   bias=top[:, 2 * hd + t:2 * hd + t + 1],
                                                   accum_out=total[:, 2 * hd + t:2 * hd + t + 1])
                    ins.then_inc(exp_ready, 1)
                act.wait_ge(top_ready, 9 * l + 9)
                for r in range(2):
                    ins = nc.scalar.activation(prob2[:, r, :], prob2[:, r, :], ACT.Exp,
                                               bias=top[:, 16 + r:17 + r], accum_out=total[:, 16 + r:17 + r])
                ins.then_inc(exp_ready, 1)
                for j in range(BT):
                    evacuate(("ua", l, j), a_t[:, j, :], P, TOK, u_ready, ACT.Gelu_apprx_tanh)
                for hf in range(2):
                    for n, (t0, rows) in enumerate(TILES):
                        evacuate(("va", l, hf, n), vg[0:rows, n, hf * 256:(hf + 1) * 256], rows, 256, vg_ready,
                                 ACT.Gelu_apprx_tanh)
                act.wait_ge(vg_ready, 6 * (l + 1))
                for n, (t0, rows) in enumerate(TILES):
                    spare, at = GELU_BUFS[n]
                    nc.scalar.activation(spare[0:rows, at:at + 2, 0:256], vg[0:rows, n, :].rearrange("p (a b) -> p a b", a=2),
                                         ACT.Square, accum_out=vsq[0:rows, n:n + 1]).then_inc(vsq_ready, 1)
                act.wait_ge(vsq_ready, 3 * (l + 1))
                for n, (t0, rows) in enumerate(TILES):
                    nc.scalar.activation(vrs[0:rows, n:n + 1], vsq[0:rows, n:n + 1], ACT.Sqrt, scale=1.0 / HALF,
                                         bias=eps[0:rows, 0:1]).then_inc(vrms_ready, 1)
                if l:
                    act.wait_ge(state_stored, 32)
                for j in range(BT):
                    evacuate(("cin", l, j), z[:, j, 2:2 + TOK], P, TOK, cin_ready)
                for r in range(2):
                    act.wait_ge(bank_full, turns.full(("pt2", l, r)))
                    src = bank(("pt2", l, r), P, 384).rearrange("p (a b) -> p a b", a=3)
                    nc.scalar.activation(pt2[:, r, 0:2, :], src[:, 0:2, :], ACT.Copy)
                    nc.scalar.activation(pt2[0:DEC, r, 2, :], src[0:DEC, 2, :], ACT.Copy).then_inc(pt2_ready, 1)
                for hd in range(HEADS):
                    if hd >= 2:
                        act.wait_ge(bank_full, turns.full(("pv", l, hd // 2 - 1)))
                    evacuate(("pt", l, hd), pt[:, hd % 2, :], P, 384, pt_ready)
                for g in range(24):
                    if g >= 4:
                        act.wait_ge(branch_read, 24 * l + g - 3)
                    evacuate(("gate", l, g), gate[:, g % 4, :], P, TOK, gate_ready, ACT.Tanh, scale=0.5)
                squares(2 * l + 1)
                root(2 * l + 1)
                if l == 0:
                    for u in range(DENSE_UNITS):
                        for b in range(KB):
                            if u >= 2:
                                act.wait_ge(hid_ready, KB * (u - 2) + b + 1)
                            evacuate(("a", ("dense", u), b), silu[:, KB * (u % 2) + b, :], P, TOK, silu_ready, ACT.Silu)
            act.wait_ge(gap_ready, 1)
            nc.scalar.activation(rs[:, 5, :], rs[:, 4, :], ACT.Exp).then_inc(gap_exp, 1)
            for n, (t0, rows) in enumerate(TILES):
                for hf in range(2):
                    evacuate(("htok", n, hf), h_tok[0:rows, n, hf * 512:(hf + 1) * 512], rows, 512, htok_ready)
            def gathered(kind, hf):
                evacuate((kind, hf), he_hi[:, 4 * hf:4 * hf + 4, :].rearrange("p a b -> p (a b)"), P, 512, he_hi_ready)

            for hf in range(2):
                gathered("gather0", hf)

            def round_chunk(at, half, in_turn=False):
                s, buf = chunk_at(at, half)
                act.wait_ge(slot_loaded[s], turns.value(16 * (slot_before[s] + at // EXPERT_RING + 1),
                                                        16 * JOB_MATRICES // EXPERT_RING, 16 if in_turn else 0))
                act.wait_ge(chunk_used, turns.value(max(2 * at + half + 2 - CHUNKS, 1), JOB_CHUNKS, 12 if in_turn else 0))
                nc.scalar.activation(w_hi[buf][:, :], expert_ring[s][:, half * CHUNK_W:(half + 1) * CHUNK_W],
                                     ACT.Copy).then_inc(rounded, 1)

            def silu_unit(u):
                _, value, per_job, per_turn = reader(("ag", u))
                act.wait_ge(hid_ready, turns.value(value - 1, per_job, per_turn))
                act.wait_ge(chunk_used, turns.chunk(CHUNKS_IN[u], u in ("odd", "next")))
                nc.scalar.activation(e_silu, bank(("ag", u), P, UNIT), ACT.Silu).then_inc(silu_ready, 1)

            def hid_high(u):
                act.wait_ge(bank_full, turns.full(("tr", u)))
                nc.scalar.activation(hid_hi[:, :, :].rearrange("p a b -> p (a b)"), bank(("tr", u), P, KB * SLOT),
                                     ACT.Copy).then_inc(hid_hi_ready, 1)

            act.wait_ge(jobs_ready, 1)
            jobs = act.value_load(job_count[0:1, 0:1], min_val=EXPERTS, max_val=MAX_JOBS)
            with act.Fori(0, jobs) as job:
                turns.job = job
                for at in (0, 1, 2):
                    round_chunk(at, 0)
                    round_chunk(at, 1)
                round_chunk(3, 0)
                silu_unit("first")
                round_chunk(3, 1)
                hid_high("first")
                with act.Fori(0, TURNS) as i:
                    turns.i = i
                    for first, u in ((4, "odd"), (7, "next")):
                        round_chunk(first, 0, True)
                        round_chunk(first, 1, True)
                        round_chunk(first + 1, 0, True)
                        silu_unit(u)
                        round_chunk(first + 1, 1, True)
                        if u == "odd":
                            round_chunk(first + 2, 0, True)
                            round_chunk(first + 2, 1, True)
                            hid_high(u)
                    round_chunk(9, 0, True)
                    round_chunk(9, 1, True)
                    hid_high("next")
                    turns.i = None
                round_chunk(JOB_MATRICES - 2, 0)
                round_chunk(JOB_MATRICES - 2, 1)
                round_chunk(JOB_MATRICES - 1, 0)
                silu_unit("last")
                round_chunk(JOB_MATRICES - 1, 1)
                hid_high("last")
                act.wait_ge(chunk_used, job * JOB_CHUNKS + (JOB_CHUNKS + 1))
                for hf in range(2):
                    nc.scalar.activation(y_tok[:, hf * 512:(hf + 1) * 512], psum[:, 6 + hf, :], ACT.Copy).then_inc(ytok_ready, 1)
                for hf in range(2):
                    gathered("gather", hf)
                turns.job = None
            turns.job = jobs
            squares(4)
            root(4)

        @block.vector
        def _(dve):
            turns = Turns()
            steps = [0]

            def done(ins):
                ins.then_inc(dve_step, 1)
                steps[0] += 1

            def settle():
                dve.wait_ge(dve_step, steps[0])

            def full(name):
                dve.wait_ge(bank_full, turns.full(name))

            def norm(n, gain, dst):
                dve.wait_ge(rms_ready, n + 1)
                nc.vector.reciprocal(rstd[:, :], rms[:, :]).then_inc(rstd_ready, 1)
                dve.wait_ge(rstd_ready, n + 1)
                for k in range(DT):
                    ins = nc.vector.scalar_tensor_tensor(out=h[:, k, :], in0=x[:, k, :], scalar=vec[:, gain + k:gain + k + 1],
                                                         in1=rstd[:, :], op0=ALU.mult, op1=ALU.mult)
                    ins.then_inc(dst, 1)

            def hidden(u, parity):
                for b in range(KB):
                    name = ("g", u, b)
                    full(name)
                    ready, count, per_job, per_turn = reader(("a", u, b))
                    dve.wait_ge(ready, turns.value(count, per_job, per_turn))
                    nc.vector.tensor_tensor(hid[:, KB * parity + b, :], silu[:, KB * parity + b, :], bank(name),
                                            ALU.mult).then_inc(hid_ready, 1)

            def sums(u, dst):
                for j in range(DT):
                    name = ("y", u, j)
                    full(name)
                    ready, count, per_job, per_turn = reader(name)
                    if j == 0 and u != ("dense", 0):
                        dve.wait_ge(ready, turns.value(count - 1, per_job, per_turn))
                    nc.vector.tensor_tensor(dst[:, j, :], dst[:, j, :], bank(name), ALU.add).then_inc(ready, 1)

            nc.vector.memset(psum[:, :, :], 0.0).then_inc(zeroed, 1)
            nc.vector.memset(eps[:, :], EPS).then_inc(zeroed, 1)
            nc.vector.memset(mean_w[:, :], 1.0 / D).then_inc(zeroed, 1)
            done(nc.vector.memset(valid[:, :], 1.0))
            done(nc.vector.memset(z[:, :, 0:2], 0.0))
            settle()
            done(nc.vector.memset(valid[:, 2:3], 0.0))
            settle()
            done(nc.vector.memset(valid[0:DEC, 2:3], 1.0))
            for l in range(2):
                dve.wait_ge(ext_loaded, 16 * (l + 1))
                done(nc.vector.tensor_copy(ext[:, :, 0:EXT // 2 - 1], ext[:, :, EXT // 2 - 1:EXT // 2].broadcast_to([P, HEADS, EXT // 2 - 1])))
                settle()
                nc.vector.memset(ext[:, :, EXT - 1:EXT], 0.0).then_inc(ext_ready, 1)
            dve.wait_ge(vec_in, 16)
            dve.wait_ge(made, 5)

            for l in range(2):
                norm(NORM_OF_LAYER[l], VEC_MIX + DT * l, h_ready)
                dve.wait_ge(bias_loaded, 16 * (l + 1))
                nc.vector.memset(bias[0:CHUNK, :, 256 + CHUNK:BIAS_W], MASKED).then_inc(bias_masked, 1)
                for s, dst in (("q", q_t), ("k", key_t)):
                    for j in range(BT):
                        full((s, l, j))
                        nc.vector.tensor_copy(dst[:, j, :], bank((s, l, j))).then_inc(qk_ready, 1)
                dve.wait_ge(bias_masked, l + 1)
                for hd in range(HEADS):
                    full(("s", l, hd))
                    p = bank(("s", l, hd), P, 384)
                    nc.vector.scalar_tensor_tensor(out=prob[:, hd, 0:128], in0=p[:, 0:128], scalar=SCALE,
                                                   in1=bias[:, hd, 256:384], op0=ALU.mult, op1=ALU.add)
                    ins = nc.vector.scalar_tensor_tensor(out=prob[:, hd, 128:384], in0=p[:, 128:384], scalar=SCALE,
                                                         in1=bias[:, hd, 128:384], op0=ALU.mult, op1=ALU.add)
                    ins.then_inc(score_ready, 1)
                    dve.wait_ge(score_ready, 10 * l + hd + 1)
                    nc.vector.tensor_reduce(top[:, 2 * hd:2 * hd + 1], prob[:, hd, 0:128], AX.X, ALU.max, negate=True)
                    nc.vector.tensor_reduce(top[:, 2 * hd + 1:2 * hd + 2], prob[:, hd, 128:384], AX.X, ALU.max,
                                            negate=True).then_inc(top_ready, 1)
                dve.wait_ge(bias2_loaded, 16 * 8 * (l + 1))
                for r in range(2):
                    full(("s2", l, r))
                    ins = nc.vector.scalar_tensor_tensor(out=prob2[:, r, :], in0=bank(("s2", l, r)), scalar=SCALE,
                                                         in1=bias2[:, r, :], op0=ALU.mult, op1=ALU.add)
                    ins.then_inc(score_ready, 1)
                dve.wait_ge(score_ready, 10 * l + 10)
                nc.vector.tensor_reduce(top[:, 16:18], prob2[:, :, :], AX.X, ALU.max, negate=True).then_inc(top_ready, 1)

                dve.wait_ge(layer_in[0], 16 * (l + 1))
                nc.vector.memset(wst[CHUNK:P, :, 0:CHUNK], 0.0).then_inc(mix_masked, 1)
                dve.wait_ge(vrms_ready, 3 * (l + 1))
                for n, (t0, rows) in enumerate(TILES):
                    done(nc.vector.reciprocal(vrs[0:rows, n:n + 1], vrs[0:rows, n:n + 1]))
                settle()
                dve.wait_ge(layer_in[2], 16 * (l + 1))
                for n, (t0, rows) in enumerate(TILES):
                    nc.vector.scalar_tensor_tensor(out=vg[0:rows, n, :], in0=vg[0:rows, n, :], scalar=vrs[0:rows, n:n + 1],
                                                   in1=gvb[0:rows, :], op0=ALU.mult, op1=ALU.mult).then_inc(vn_ready, 1)

                for j in range(BT):
                    full(("gc", l, j))
                    dve.wait_ge(cin_ready, BT * l + j + 1)
                    ins = nc.vector.tensor_tensor(tmp[:, j % 2, 0:TOK], z[:, j, 2:2 + TOK], bank(("gc", l, j)), ALU.mult)
                    ins.then_inc(gc_read, 1)
                    dve.wait_ge(gc_read, BT * l + j + 1)
                    nc.vector.tensor_copy(z[:, j, 2:2 + SEQ], tmp[:, j % 2, 0:SEQ])
                    nc.vector.tensor_copy(z[:, j, SEQ + 4:TOK + 4], tmp[:, j % 2, SEQ:TOK])
                    st = VEC_STATE + 8 * l + 2 * j
                    nc.vector.tensor_copy(z[:, j, SEQ + 2:SEQ + 4], vec[:, st:st + 2]).then_inc(z_ready, 1)
                dve.wait_ge(z_ready, BT * (l + 1))
                for j in range(BT):
                    w = VEC_CONV + 12 * l + j
                    y = tmp[:, j % 2, 0:TOK + 2]
                    done(nc.vector.tensor_scalar(y, z[:, j, 0:TOK + 2], vec[:, w:w + 1], None, ALU.mult))
                    settle()
                    done(nc.vector.scalar_tensor_tensor(out=y, in0=z[:, j, 1:TOK + 3], scalar=vec[:, w + 4:w + 5], in1=y,
                                                        op0=ALU.mult, op1=ALU.add))
                    settle()
                    done(nc.vector.scalar_tensor_tensor(out=y, in0=z[:, j, 2:TOK + 4], scalar=vec[:, w + 8:w + 9], in1=y,
                                                        op0=ALU.mult, op1=ALU.add))
                    settle()
                    full(("gb", l, j))
                    p = bank(("gb", l, j))
                    nc.vector.tensor_tensor(c_t[:, j, 0:SEQ], y[:, 0:SEQ], p[:, 0:SEQ], ALU.mult)
                    ins = nc.vector.tensor_tensor(c_t[:, j, SEQ:TOK], y[:, SEQ + 2:TOK + 2], p[:, SEQ:TOK], ALU.mult)
                    ins.then_inc(c_ready, 1)

                dve.wait_ge(layer_in[1], 16 * (l + 1))
                dve.wait_ge(u_ready, BT * (l + 1))
                for j in range(BT):
                    full(("mixed", l, j))
                    p = bank(("mixed", l, j))
                    b2 = bsb[:, j:j + 1, :].broadcast_to([P, 2, P])
                    nc.vector.tensor_tensor(tmp[:, j % 2, 0:SEQ].rearrange("p (a b) -> p a b", a=2),
                                            p[:, 0:SEQ].rearrange("p (a b) -> p a b", a=2), b2, ALU.add)
                    ins = nc.vector.tensor_tensor(tmp[:, j % 2, SEQ:TOK], p[:, SEQ:TOK], bsb[:, j, 0:DEC], ALU.add)
                    ins.then_inc(mixed_read, 1)
                    dve.wait_ge(mixed_read, BT * l + j + 1)
                    nc.vector.tensor_tensor(a_t[:, j, :], a_t[:, j, :], tmp[:, j % 2, 0:TOK], ALU.mult).then_inc(a_ready, 1)

                for hd in range(HEADS):
                    dve.wait_ge(exp_ready, 9 * l + hd + 1)
                    done(nc.vector.reciprocal(part[:, 2 * hd:2 * hd + 2], total[:, 2 * hd:2 * hd + 2]))
                dve.wait_ge(exp_ready, 9 * l + 9)
                done(nc.vector.reciprocal(part[:, 16:18], total[:, 16:18]))
                settle()
                for r in range(2):
                    ins = nc.vector.tensor_scalar(prob2[:, r, :], prob2[:, r, :], part[:, 16 + r:17 + r], None, ALU.mult)
                ins.then_inc(prob_ready, 1)
                for hd in range(HEADS):
                    for t, (c0, c1) in enumerate(((0, 128), (128, 384))):
                        ins = nc.vector.tensor_scalar(prob[:, hd, c0:c1], prob[:, hd, c0:c1],
                                                      part[:, 2 * hd + t:2 * hd + t + 1], None, ALU.mult)
                    ins.then_inc(prob_ready, 1)
                for b in range(BT):
                    full(("pv", l, b))
                    nc.vector.tensor_copy(b_t[:, b, :], bank(("pv", l, b))).then_inc(b_ready, 1)

                for hf in range(2):
                    for b in range(3):
                        for j in range(4):
                            name = ("branch", l, hf, b, j)
                            full(name)
                            g = 12 * hf + 4 * b + j
                            dve.wait_ge(gate_ready, 24 * l + g + 1)
                            if hf == 1 and b == 0 and j == 0:
                                dve.wait_ge(keys_stored, 16 * (l + 1))
                            dst = m_t[hf][:, j, :] if b == 0 else tmp[:, j % 2, 0:TOK]
                            ins = nc.vector.scalar_tensor_tensor(out=dst, in0=gate[:, g % 4, :], scalar=1.0, in1=bank(name),
                                                                 op0=ALU.add, op1=ALU.mult)
                            ins.then_inc(branch_read, 1)
                            if b:
                                dve.wait_ge(branch_read, 24 * l + 12 * hf + 4 * b + j + 1)
                                ins = nc.vector.tensor_tensor(m_t[hf][:, j, :], m_t[hf][:, j, :], tmp[:, j % 2, 0:TOK], ALU.add)
                            if b == 2:
                                ins.then_inc(m_ready, 1)
                for j in range(DT):
                    full(("out", l, j))
                    ins = nc.vector.scalar_tensor_tensor(out=x[:, j, :], in0=bank(("out", l, j)), scalar=0.5, in1=x[:, j, :],
                                                         op0=ALU.mult, op1=ALU.add)
                    ins.then_inc(x_ready, 1)
                dve.wait_ge(x_ready, DT * (l + 1))
                norm(2 * l + 1, VEC_FFN + DT * l, h_ready)
                if l == 0:
                    for u in range(DENSE_UNITS + 1):
                        if u < DENSE_UNITS:
                            hidden(("dense", u), u % 2)
                        if u:
                            sums(("dense", u - 1), x)
                    dve.wait_ge(sum_ready, DT * DENSE_UNITS)

            LG, EQ, OH1, LG2, OH2, MASK, COMB, T0, TILES_OVER = range(9)

            def wide(a):
                return rs[:, a, :].rearrange("p (n o) -> p n o", o=1).broadcast_to([P, 3, EXPERTS])

            done(nc.vector.memset(rt[:, LG], 0.0))
            settle()
            dve.wait_ge(layer_in[5], 32)
            full(("logits",))
            p = bank(("logits",), P, 24).rearrange("p (n e) -> p n e", n=3)
            rb1 = rb[:, :].rearrange("p (o e) -> p o e", o=1)
            done(nc.vector.tensor_tensor(rt[:, LG, 0:2], p[:, 0:2, :], rb1.broadcast_to([P, 2, EXPERTS]), ALU.add))
            ins = nc.vector.tensor_tensor(rt[0:DEC, LG, 2], p[0:DEC, 2, :], rb[0:DEC, :], ALU.add)
            ins.then_inc(logits_read, 1)
            dve.wait_ge(logits_read, 1)

            def pick(src, top_at, key_at, hot):
                done(nc.vector.tensor_reduce(rs[:, top_at, :], rt[:, src], AX.X, ALU.max))
                settle()
                done(nc.vector.tensor_tensor(rt[:, EQ], rt[:, src], wide(top_at), ALU.is_equal))
                settle()
                done(nc.vector.tensor_tensor(rt[:, EQ], rt[:, EQ], rank[:, :, :], ALU.mult))
                settle()
                done(nc.vector.tensor_reduce(rs[:, key_at, :], rt[:, EQ], AX.X, ALU.max))
                settle()
                done(nc.vector.tensor_tensor(rt[:, hot], rt[:, EQ], wide(key_at), ALU.is_equal))
                settle()

            pick(LG, 0, 1, OH1)
            done(nc.vector.scalar_tensor_tensor(out=rt[:, LG2], in0=rt[:, OH1], scalar=-3.0e38, in1=rt[:, LG],
                                                op0=ALU.mult, op1=ALU.add))
            settle()
            pick(LG2, 2, 3, OH2)
            nc.vector.tensor_tensor(rs[:, 4, :], rs[:, 2, :], rs[:, 0, :], ALU.subtract).then_inc(gap_ready, 1)
            done(nc.vector.tensor_tensor(rt[:, MASK], rt[:, OH1], rt[:, OH2], ALU.add))
            settle()
            valid3 = valid[:, :].rearrange("p (n o) -> p n o", o=1).broadcast_to([P, 3, EXPERTS])
            ins = nc.vector.tensor_tensor(rt[:, MASK], rt[:, MASK], valid3, ALU.mult)
            ins.then_inc(mask_ready, 1)
            dve.wait_ge(gap_exp, 1)
            done(nc.vector.tensor_scalar(rs[:, 6, :], rs[:, 5, :], 1.0, None, ALU.add))
            settle()
            done(nc.vector.reciprocal(rs[:, 6, :], rs[:, 6, :]))
            settle()
            done(nc.vector.tensor_tensor(rs[:, 7, :], rs[:, 5, :], rs[:, 6, :], ALU.mult))
            settle()
            done(nc.vector.tensor_tensor(rt[:, COMB], rt[:, OH1], wide(6), ALU.mult))
            done(nc.vector.tensor_tensor(rt[:, T0], rt[:, OH2], wide(7), ALU.mult))
            settle()
            done(nc.vector.tensor_tensor(weight[:, :, :], rt[:, COMB], rt[:, T0], ALU.add))
            full(("counts",))
            pc = bank(("counts",), P, 32)
            done(nc.vector.scalar_tensor_tensor(out=rt[:, EQ], in0=pc[:, 0:24].rearrange("p (n e) -> p n e", n=3), scalar=1.0,
                                                in1=rt[:, MASK], op0=ALU.add, op1=ALU.mult))
            done(nc.vector.tensor_scalar(rt[:, TILES_OVER, 0], pc[:, 24:32], float(SLOT), None, ALU.is_gt))
            nc.vector.tensor_scalar(rt[:, TILES_OVER, 1], pc[:, 24:32], float(2 * SLOT), None, ALU.is_gt).then_inc(count_ready, 1)
            settle()
            done(nc.vector.tensor_scalar(place[:, :, :], rt[:, EQ], -1.0, None, ALU.add))
            done(nc.vector.memset(starts[:, 0:1], 0.0))
            done(nc.vector.memset(zero_row, 0.0))
            dve.wait_ge(count_ready, 1)
            done(nc.vector.scalar_tensor_tensor(out=rt[:, TILES_OVER, 2], in0=rt[:, TILES_OVER, 0], scalar=1.0, in1=rt[:, TILES_OVER, 1],
                                                op0=ALU.add, op1=ALU.add))
            settle()
            for e in range(EXPERTS):
                done(nc.vector.tensor_tensor(starts[:, e + 1:e + 2], starts[:, e:e + 1], rt[:, TILES_OVER, 2, e:e + 1], ALU.add))
                settle()
            slots = [P, MAX_JOBS + 1, EXPERTS]
            starts_wide = starts[:, 0:EXPERTS].rearrange("p (o e) -> p o e", o=1).broadcast_to(slots)
            done(nc.vector.tensor_tensor(job_hit[:, :, :], starts_wide,
                                         job_no[:, :].rearrange("p (j o) -> p j o", o=1).broadcast_to(slots), ALU.is_le))
            settle()
            done(nc.vector.tensor_reduce(job_base[:, :], job_hit[:, :, :], AX.X, ALU.add))
            settle()
            done(nc.vector.tensor_scalar(job_expert[0:1, :], job_base[0:1, :], -1.0, None, ALU.add))
            done(nc.vector.tensor_copy(job_count[0:1, 0:1], starts[0:1, EXPERTS:EXPERTS + 1]))
            done(nc.vector.tensor_scalar(job_count[0:1, 1:2], starts[0:1, EXPERTS:EXPERTS + 1], -1.0, None, ALU.add))
            done(nc.vector.tensor_tensor(job_hit[:, :, :], job_hit[:, :, :], starts_wide, ALU.mult))
            settle()
            done(nc.vector.tensor_reduce(job_base[:, :], job_hit[:, :, :], AX.X, ALU.max))
            settle()
            done(nc.vector.tensor_tensor(job_base[:, :], job_no[:, :], job_base[:, :], ALU.subtract))
            settle()
            nc.vector.tensor_scalar(job_base[:, :], job_base[:, :], float(SLOT), None, ALU.mult).then_inc(jobs_ready, 1)
            dve.wait_ge(jobs_ready, 1)

            def hot_rows(dst, job, e):
                for n, (t0, rows) in enumerate(TILES):
                    nc.vector.tensor_scalar(dst[0:rows, n, :], slot_id[0:rows, 0:SLOT], job_base[0:rows, bass.ds(job, 1)],
                                            place[0:rows, n, bass.ds(e, 1)], ALU.add, ALU.is_equal).then_inc(spread_ready, 1)

            def low_chunk(at, half, in_turn=False):
                s, buf = chunk_at(at, half)
                dve.wait_ge(rounded, turns.value(2 * at + half + 1, JOB_CHUNKS, 12 if in_turn else 0))
                nc.vector.tensor_tensor(w_lo[buf][:, :], expert_ring[s][:, half * CHUNK_W:(half + 1) * CHUNK_W],
                                        w_hi[buf][:, :].bitcast(f32), ALU.subtract).then_inc(split, 1)

            def silu_times_g(u):
                dve.wait_ge(silu_ready, turns.value(KB * DENSE_UNITS + UNIT_AT[u] + 1, UNITS, 2 if u in ("odd", "next") else 0))
                nc.vector.tensor_tensor(e_hid, e_silu, psum[:, GROUP[("ag", u)][0], UNIT:2 * UNIT], ALU.mult).then_inc(hid_ready, 1)

            def hid_low(u):
                dve.wait_ge(hid_hi_ready, turns.value(UNIT_AT[u] + 1, UNITS, 2 if u in ("odd", "next") else 0))
                nc.vector.tensor_tensor(hid_lo[:, :, :].rearrange("p a b -> p (a b)"), bank(("tr", u), P, KB * SLOT),
                                        hid_hi[:, :, :].bitcast(f32).rearrange("p a b -> p (a b)"), ALU.subtract).then_inc(hid_ready, 1)

            def gathered_low(name, value):
                dve.wait_ge(he_hi_ready, value)
                tiles = slice(4 * name[1], 4 * name[1] + 4)
                nc.vector.tensor_tensor(he_lo[:, tiles, :].rearrange("p a b -> p (a b)"), bank(name, P, 512),
                                        he_hi[:, tiles, :].bitcast(f32).rearrange("p a b -> p (a b)"), ALU.subtract
                                        ).then_inc(he_ready, 1)

            hot_rows(spread, 0, 0)
            for hf in range(2):
                gathered_low(("gather0", hf), hf + 1)
            jobs = dve.value_load(job_count[0:1, 0:1], min_val=EXPERTS, max_val=MAX_JOBS)
            with dve.Fori(0, jobs) as job:
                turns.job = job
                e = dve.value_load(job_expert[0:1, bass.ds(job, 1)], min_val=0, max_val=EXPERTS - 1)
                e_next = dve.value_load(job_expert[0:1, bass.ds(job + 1, 1)], min_val=0, max_val=EXPERTS - 1)
                for at in (0, 1, 2):
                    low_chunk(at, 0)
                    low_chunk(at, 1)
                low_chunk(3, 0)
                silu_times_g("first")
                low_chunk(3, 1)
                hid_low("first")
                hot_rows(spread, job + 1, e_next)
                hot_rows(wspread, job, e)
                dve.wait_ge(spread_ready, job * 9 + 9)
                for n, (t0, rows) in enumerate(TILES):
                    nc.vector.tensor_scalar(wspread[0:rows, n, :], wspread[0:rows, n, :], weight[0:rows, n, bass.ds(e, 1)],
                                            None, ALU.mult).then_inc(spread_ready, 1)
                with dve.Fori(0, TURNS) as i:
                    turns.i = i
                    for first, u in ((4, "odd"), (7, "next")):
                        low_chunk(first, 0, True)
                        low_chunk(first, 1, True)
                        low_chunk(first + 1, 0, True)
                        silu_times_g(u)
                        low_chunk(first + 1, 1, True)
                        if u == "odd":
                            low_chunk(first + 2, 0, True)
                            low_chunk(first + 2, 1, True)
                            hid_low(u)
                    low_chunk(9, 0, True)
                    low_chunk(9, 1, True)
                    hid_low("next")
                    turns.i = None
                low_chunk(JOB_MATRICES - 2, 0)
                low_chunk(JOB_MATRICES - 2, 1)
                low_chunk(JOB_MATRICES - 1, 0)
                silu_times_g("last")
                low_chunk(JOB_MATRICES - 1, 1)
                hid_low("last")
                full(("dwt", 0))
                nc.vector.tensor_copy(wspread_t, bank(("dwt", 0))).then_inc(spread_t_ready, 1)
                for hf in range(2):
                    gathered_low(("gather", hf), job * 2 + (hf + 3))
                dve.wait_ge(x_ready, job * DT + MIXER_SUMS)
                for j in range(DT):
                    full(("scatter", j))
                    nc.vector.tensor_tensor(x[:, j, :], x[:, j, :], bank(("scatter", j)), ALU.add).then_inc(x_ready, 1)
                turns.job = None
            dve.wait_ge(x_ready, jobs * DT + MIXER_SUMS)
            norm(4, VEC_FIN, y_out)

        @block.tensor
        def _(pe):
            turns = Turns()

            def take(name):
                for n, when in GROUP[name][2]:
                    ready, value, per_job, per_turn = reader(n)
                    if when == "last_turn":
                        value -= per_turn
                    if when == "end_of_turns":
                        value += (TURNS - 1) * per_turn
                    if when == "last_job":
                        value -= per_job
                    pe.wait_ge(ready, turns.value(value, per_job, 0 if when == "end_of_turns" else per_turn))

            def give(ins):
                ins.then_inc(bank_full, 1)

            def loaded(i):
                pe.wait_ge(slot_loaded[slot_of(i)], 16 * loads_of(i))

            def slab(s, c=256):
                return ring[s][:, :].rearrange("p (k c) -> p k c", c=c)

            def mean(n):
                take(("norm", n))
                for k in range(DT):
                    pe.wait_ge(squared, DT * n + k + 1)
                    ins = nc.tensor.matmul(bank(("norm", n)), mean_w[:, :], sq[:, k, :], start=(k == 0), stop=(k == DT - 1))
                give(ins)

            def features(seg, l):
                for j in range(BT):
                    i = STREAM[(seg, l, j // 2)]
                    loaded(i)
                    w = slab(slot_of(i))
                    take((seg, l, j))
                    for k in range(DT):
                        if seg == "q" and j == 0:
                            pe.wait_ge(h_ready, 2 * DT * l + k + 1)
                        ins = nc.tensor.matmul(bank((seg, l, j)), w[:, k, (j % 2) * P:(j % 2 + 1) * P], h[:, k, :],
                                               start=(k == 0), stop=(k == DT - 1))
                    give(ins)

            def rows_of(seg, l):
                for hf in range(2):
                    i = STREAM[(seg, l, hf)]
                    loaded(i)
                    w = slab(slot_of(i))
                    for n, (t0, rows) in enumerate(TILES):
                        take((seg, l, hf, n))
                        for k in range(DT):
                            ins = nc.tensor.matmul(bank((seg, l, hf, n), rows, 256), h[:, k, t0:t0 + rows], w[:, k, :],
                                                   start=(k == 0), stop=(k == DT - 1))
                        give(ins)

            def scores(l):
                pe.wait_ge(qk_ready, 8 * (l + 1))
                pe.wait_ge(layer_in[3], 16 * (l + 1))
                for hd in range(HEADS):
                    r0, j = DH * (hd % 2), hd // 2
                    q, k = q_t[r0:r0 + DH, j, :], key_t[r0:r0 + DH, j, :]
                    take(("s", l, hd))
                    p = bank(("s", l, hd), P, 384)
                    nc.tensor.matmul(p[:, 0:128], q[:, 0:128], k[:, 0:128], start=True, stop=True)
                    give(nc.tensor.matmul(p[:, 128:384], q[:, 128:256], k[:, 0:256], start=True, stop=True))
                for r in range(2):
                    take(("s2", l, r))
                    for j in range(4):
                        p = bank(("s2", l, r), DEC, TOK, 32 * j)
                        q = q_t[DH * r:DH * r + DH, j, SEQ:TOK]
                        nc.tensor.matmul(p[:, 0:PAST], q, ck_t[DH * r:DH * r + DH, j, :], start=True, stop=True,
                                         tile_position=(DH * r, 32 * j))
                        ins = nc.tensor.matmul(p[:, PAST:TOK], q, key_t[DH * r:DH * r + DH, j, SEQ:TOK], start=True, stop=True,
                                               tile_position=(DH * r, 32 * j))
                    give(ins)

            def mixed(l):
                pe.wait_ge(vn_ready, 3 * (l + 1))
                pe.wait_ge(mix_masked, l + 1)
                for j in range(BT):
                    take(("mixed", l, j))
                    for n, (t0, rows) in enumerate(TILES):
                        ins = nc.tensor.matmul(bank(("mixed", l, j))[:, t0:t0 + rows], vg[0:rows, n, j * P:(j + 1) * P],
                                               wst[0:rows, j, 0:rows], start=True, stop=True)
                    give(ins)

            def attention(l):
                pe.wait_ge(prob_ready, 9 * l + 1)
                for r in range(2):
                    take(("pt2", l, r))
                    for n, rows in enumerate((P, P, DEC)):
                        ins = nc.tensor.transpose(bank(("pt2", l, r), rows, 384)[:, n * P:(n + 1) * P],
                                                  prob2[:, r, n * P:n * P + rows], ident[:, :])
                    give(ins)
                for b in range(BT):
                    for hd in (2 * b, 2 * b + 1):
                        pe.wait_ge(prob_ready, 9 * l + hd + 2)
                        take(("pt", l, hd))
                        p = bank(("pt", l, hd), P, 384)
                        for n in range(3):
                            ins = nc.tensor.transpose(p[:, n * P:(n + 1) * P], prob[:, hd, n * P:(n + 1) * P], ident[:, :])
                        give(ins)
                    take(("pv", l, b))
                    if b == 0:
                        pe.wait_ge(v_ready, 6 * (l + 1))
                        pe.wait_ge(layer_in[4], 16 * (l + 1))
                        pe.wait_ge(pt2_ready, 2 * (l + 1))
                    for hd in (2 * b, 2 * b + 1):
                        pe.wait_ge(pt_ready, 8 * l + hd + 1)
                        p = bank(("pv", l, b), DH, TOK, DH * (hd % 2))
                        t, c = pt[:, hd % 2, :], slice(DH * hd, DH * hd + DH)
                        nc.tensor.matmul(p[:, 0:128], v_tok[:, 0, c], t[:, 0:128], start=True, stop=True)
                        nc.tensor.matmul(p[:, 128:256], v_tok[:, 0, c], t[:, 128:256], start=True, stop=False)
                        nc.tensor.matmul(p[:, 128:256], v_tok[:, 1, c], t[:, 256:384], start=False, stop=True)
                        r, j = hd % 2, hd // 2
                        q = slice(32 * j, 32 * j + 32)
                        nc.tensor.matmul(p[:, 256:288], cv[:, 0, c], pt2[:, r, 0, q], start=True, stop=False)
                        nc.tensor.matmul(p[:, 256:288], cv[:, 1, c], pt2[:, r, 1, q], start=False, stop=False)
                        ins = nc.tensor.matmul(p[:, 256:288], v_tok[0:DEC, 2, c], pt2[0:DEC, r, 2, q], start=False, stop=True)
                    give(ins)

            def branches(l):
                for hf in range(2):
                    for b, (src, ready) in enumerate(((a_t, a_ready), (b_t, b_ready), (c_t, c_ready))):
                        for j in range(4):
                            i = STREAM[("gate", l, 4 * b + 2 * hf + j // 2)]
                            loaded(i)
                            w = slab(slot_of(i))
                            name = ("gate", l, 12 * hf + 4 * b + j)
                            take(name)
                            for k in range(DT):
                                ins = nc.tensor.matmul(bank(name), w[:, k, (j % 2) * P:(j % 2 + 1) * P], h[:, k, :],
                                                       start=(k == 0), stop=(k == DT - 1))
                            give(ins)
                        i = STREAM[("branch", l, hf, b)]
                        loaded(i)
                        w = slab(slot_of(i), 512)
                        pe.wait_ge(ready, BT * (l + 1))
                        for j in range(4):
                            take(("branch", l, hf, b, j))
                            for k in range(BT):
                                ins = nc.tensor.matmul(bank(("branch", l, hf, b, j)), w[:, k, j * P:(j + 1) * P], src[:, k, :],
                                                       start=(k == 0), stop=(k == BT - 1))
                            give(ins)

            def project_out(l):
                for j in range(DT):
                    i = STREAM[("out", l, j // 2)]
                    loaded(i)
                    w = slab(slot_of(i))
                    take(("out", l, j))
                    for k in range(DT):
                        if j == 0:
                            pe.wait_ge(m_ready, DT * l + k + 1)
                        ins = nc.tensor.matmul(bank(("out", l, j)), w[:, k, (j % 2) * P:(j % 2 + 1) * P], m_t[k // 4][:, k % 4, :],
                                               start=(k == 0), stop=(k == DT - 1))
                    give(ins)

            def unit_in(u, src, w_a, w_g, cols, wait_a, wait_g):
                wait_a()
                for b in range(KB):
                    for s, w in (("a", w_a), ("g", w_g)):
                        if s == "g" and b == 0:
                            wait_g()
                        take((s, u, b))
                        for k in range(DT):
                            ins = nc.tensor.matmul(bank((s, u, b), P, cols), w[:, k, b * P:(b + 1) * P], src[:, k, 0:cols],
                                                   start=(k == 0), stop=(k == DT - 1))
                        give(ins)

            def unit_out(u, w, cols, buf):
                for j in range(DT):
                    take(("y", u, j))
                    for b in range(KB):
                        ins = nc.tensor.matmul(bank(("y", u, j), P, cols), w[:, b, j * P:(j + 1) * P], hid[:, buf + b, 0:cols],
                                               start=(b == 0), stop=(b == KB - 1))
                    give(ins)

            pe.wait_ge(zeroed, 3)
            pe.wait_ge(made, 5)
            for l in range(2):
                mean(NORM_OF_LAYER[l])
                features("q", l)
                features("k", l)
                rows_of("v", l)
                scores(l)
                features("ua", l)
                rows_of("va", l)
                features("cin", l)
                features("gc", l)
                features("gb", l)
                mixed(l)
                attention(l)
                branches(l)
                project_out(l)
                mean(2 * l + 1)
                if l == 0:
                    pe.wait_ge(h_ready, DT * 2)
                    for u in range(DENSE_UNITS + 1):
                        if u < DENSE_UNITS:
                            i = STREAM[("w1", u)]
                            unit_in(("dense", u), h, slab(slot_of(i)), slab(slot_of(i + 1)), TOK,
                                    lambda: loaded(i), lambda: loaded(i + 1))
                        if u:
                            i = STREAM[("w2", u - 1)]
                            loaded(i)
                            pe.wait_ge(hid_ready, KB * u)
                            unit_out(("dense", u - 1), slab(slot_of(i), D), TOK, KB * ((u - 1) % 2))

            pe.wait_ge(h_ready, DT * 4)
            pe.wait_ge(layer_in[5], 32)
            take(("logits",))
            for n, (t0, rows) in enumerate(TILES):
                for k in range(DT):
                    ins = nc.tensor.matmul(bank(("logits",), rows, 24)[:, 8 * n:8 * n + 8], h[:, k, t0:t0 + rows], rw[:, k, :],
                                           start=(k == 0), stop=(k == DT - 1))
            give(ins)

            def place_tokens():
                pe.wait_ge(mask_ready, 1)
                take(("counts",))
                p = bank(("counts",), P, 32)
                for n in range(3):
                    for k in range(n + 1):
                        nc.tensor.matmul(p[:, 8 * n:8 * n + 8], before[:, :] if k == n else ones[:, :], rt[:, 5, k],
                                         start=(k == 0), stop=(k == n))
                for k in range(3):
                    ins = nc.tensor.matmul(p[:, 24:32], ones[:, :], rt[:, 5, k], start=(k == 0), stop=(k == 2))
                give(ins)

            place_tokens()
            for n, (t0, rows) in enumerate(TILES):
                for hf in range(2):
                    take(("htok", n, hf))
                    for k in range(4):
                        ins = nc.tensor.transpose(bank(("htok", n, hf), rows, 512)[:, k * P:(k + 1) * P],
                                                  h[:, 4 * hf + k, t0:t0 + rows], ident[:, :])
                    give(ins)
            pe.wait_ge(htok_ready, 6)
            pe.wait_ge(count_ready, 1)

            def gather(kind):
                for hf in range(2):
                    take((kind, hf))
                    for j in range(4):
                        at = (4 * hf + j) * P
                        for n, (t0, rows) in enumerate(TILES):
                            ins = nc.tensor.matmul(bank((kind, hf), P, 512)[:, j * P:(j + 1) * P], h_tok[0:rows, n, at:at + P],
                                                   spread[0:rows, n, :], start=(n == 0), stop=(n == 2))
                            if kind == "gather0" and hf + j + n == 0:
                                ins.then_inc(chunk_used, 1)
                    give(ins)

            def split_chunk(at, half, in_turn):
                c = 2 * at + half
                pe.wait_ge(split, turns.value(c + 1, JOB_CHUNKS, 12 if in_turn else 0))
                return w_hi[c % CHUNKS], w_lo[c % CHUNKS]

            def unit_rows(u, at):
                in_turn = u in ("odd", "next")
                take(("ag", u))
                out = bank(("ag", u), P, 2 * UNIT)
                for m in range(2):
                    p = out[:, m * UNIT:(m + 1) * UNIT]
                    for half in range(2):
                        hi, lo = split_chunk(at + m, half, in_turn)
                        for q in range(4):
                            k = 4 * half + q
                            w_high, w_low = hi[:, q * UNIT:(q + 1) * UNIT], lo[:, q * UNIT:(q + 1) * UNIT]
                            nc.tensor.matmul(p, he_hi[:, k, :], w_high, start=(k == 0), stop=False)
                            nc.tensor.matmul(p, he_hi[:, k, :], w_low, start=False, stop=False)
                            ins = nc.tensor.matmul(p, he_lo[:, k, :], w_high, start=False, stop=(k == DT - 1))
                        ins.then_inc(chunk_used, 1)

            def transpose_hidden(u):
                take(("tr", u))
                _, value, per_job, per_turn = reader(("ag", u))
                pe.wait_ge(hid_ready, turns.value(value, per_job, per_turn))
                for b in range(KB):
                    ins = nc.tensor.transpose(bank(("tr", u), P, 512)[:, b * P:(b + 1) * P], e_hid[:, b * P:(b + 1) * P], ident[:, :])
                give(ins)

            def unit_down(u, at):
                _, value, per_job, per_turn = reader(("tr", u))
                if (u, at) == ("next", JOB_MATRICES - 2):
                    value += (TURNS - 1) * per_turn
                before_turn = u == "next" and at == 4
                in_turn = at in (4, 7)
                pe.wait_ge(hid_ready, turns.value(value - (per_turn if before_turn else 0), per_job, per_turn if in_turn else 0))
                for b in range(KB):
                    hi, lo = split_chunk(at, b, in_turn)
                    last = u == "last" and b == KB - 1
                    for h_part, w_part in ((hid_hi, hi), (hid_hi, lo), (hid_lo, hi)):
                        for hf in range(2):
                            ins = nc.tensor.matmul(psum[:, 6 + hf, :], h_part[:, b, :], w_part[:, hf * 512:(hf + 1) * 512],
                                                   start=False, stop=(last and h_part is hid_lo))
                    ins.then_inc(chunk_used, 1)

            pe.wait_ge(spread_ready, 3)
            gather("gather0")
            pe.wait_ge(jobs_ready, 1)
            jobs = pe.value_load(job_count[0:1, 0:1], min_val=EXPERTS, max_val=MAX_JOBS)
            with pe.Fori(0, jobs) as job:
                turns.job = job
                pe.wait_ge(he_ready, job * 2 + 2)
                for hf in range(2):
                    nc.tensor.matmul(psum[:, 6 + hf, :], zero_row[:, 0:P], zero_row, start=True, stop=False)
                unit_rows("first", 0)
                transpose_hidden("first")
                with pe.Fori(0, TURNS) as i:
                    turns.i = i
                    unit_rows("odd", 2)
                    unit_down("next", 4)
                    transpose_hidden("odd")
                    unit_rows("next", 5)
                    unit_down("odd", 7)
                    transpose_hidden("next")
                    turns.i = None
                unit_rows("last", JOB_MATRICES - 4)
                unit_down("next", JOB_MATRICES - 2)
                transpose_hidden("last")
                unit_down("last", JOB_MATRICES - 1)
                pe.wait_ge(spread_ready, job * 9 + 12)
                take(("dwt", 0))
                for n, (t0, rows) in enumerate(TILES):
                    ins = nc.tensor.transpose(bank(("dwt", 0))[:, t0:t0 + rows], wspread[0:rows, n, :], ident[0:rows, 0:rows])
                give(ins)
                gather("gather")
                pe.wait_ge(ytok_ready, job * 2 + 2)
                pe.wait_ge(spread_t_ready, job + 1)
                for j in range(DT):
                    take(("scatter", j))
                    give(nc.tensor.matmul(bank(("scatter", j)), y_tok[:, j * P:(j + 1) * P], wspread_t, start=True, stop=True))
                turns.job = None
            turns.job = jobs
            mean(4)


def kernel(**inputs):
    import concourse.bacc as _bacc
    from concourse.bass_utils import run_bass_kernel_spmd as _run

    a = {k: np.asarray(v) for k, v in inputs.items()}

    def columns(v):
        return v.reshape(-1, P).T

    vecs = np.concatenate([
        columns(a["norm_mix_g"]), columns(a["norm_ffn_g"]), columns(a["final_norm_g"]),
        columns(a["conv_w"]),
        a["state_conv"].reshape(2, 2, BT, P).transpose(3, 0, 2, 1).reshape(P, 16)], axis=1)
    arrays = {
        "x_t": np.concatenate([a["x_prompt"][0], a["x_sample"][0]], axis=0).T,
        "vecs": vecs,
        "w_in": a["w_in"],
        "cache_k_t": a["cache_attn_k"].reshape(2, PAST, HALF).transpose(0, 2, 1),
        "cache_v": a["cache_attn_v"].reshape(2, PAST, HALF),
        "ws_t": a["gmlp_ws"].transpose(0, 3, 1, 2),
        "bs": a["gmlp_bs"].reshape(2, HALF),
        "g_v": a["gmlp_norm_g"],
        "bias_rev": a["attn_rel_bias"][:, :, ::-1],
        "w_branch": a["w_branch"],
        "w_out": a["w_out"],
        "w1": a["ffn_w1"][0], "w3": a["ffn_w3"][0], "w2": a["ffn_w2"][0],
        "router": a["moe_router"][0], "router_b": a["moe_router_b"],
        "e_w1": a["moe_w1"][0], "e_w3": a["moe_w3"][0], "e_w2": a["moe_w2"][0],
    }
    outs = {"y_t": (D, TOK), "k_t": (2, HALF, TOK), "v_rows": (2, TOK, HALF), "z_state": (2, P, BT, 4),
            "vn_rows": (2, DEC, HALF)}
    nc = _bacc.Bacc("TRN2", target_bir_lowering=False, num_devices=1)
    feed, args = {}, {}
    for name, v in arrays.items():
        v = np.ascontiguousarray(v)
        feed[f"in_{name}"] = v
        args[name] = nc.dram_tensor(f"in_{name}", v.shape, mybir.dt.from_np(v.dtype), kind="ExternalInput").ap()
    for name, shape in outs.items():
        args[name] = nc.dram_tensor(f"out_{name}", shape, mybir.dt.float32, kind="ExternalOutput").ap()
    encoder(nc, **args)
    r = _run(nc, [feed], core_ids=[0]).results[0]
    y, kt, vr = r["out_y_t"].T, r["out_k_t"].transpose(0, 2, 1), r["out_v_rows"]
    zs = r["out_z_state"].transpose(0, 3, 2, 1).reshape(2, 4, HALF)
    k5, v5 = (t.reshape(2, 1, TOK, HEADS, DH) for t in (kt, vr))
    c = np.ascontiguousarray
    return (c(y[None, :SEQ]), c(y[None, SEQ:]), c(k5[:, :, :SEQ]), c(v5[:, :, :SEQ]), c(zs[:, None, 0:2]),
            c(k5[:, :, SEQ:]), c(v5[:, :, SEQ:]), c(zs[:, None, 2:4]), c(r["out_vn_rows"][:, None]))
```

```python
import numpy as np
import concourse.bass as bass
from concourse import mybir
from contextlib import ExitStack

P = 128
D = 1024
DT = D // P
SEQ, DEC = 256, 32
TOK = SEQ + DEC
TILES = [(0, 128), (128, 128), (256, 32)]
HALF = D // 2
BT = HALF // P
HEADS, DH = 8, 64
CHUNK = 64
PAST = 256
CLIP = 128
TAB = 2 * CLIP + 1
IN_COLS = 7 * D
FF = 2816
EXPERTS = 8
FFE = 3584
SLOT = 128
EPS = 1e-6
MASKED = -1e30
SCALE = DH ** -0.5

RING = 4
EXPERT_RING = 6
UNIT = 256
KB = UNIT // P
UNITS = FFE // UNIT
DENSE_UNITS = FF // UNIT
TURNS = UNITS // 2 - 1
CHUNK_W = 1024
CHUNKS = 4
JOB_CHUNKS = 6 * UNITS
JOB_MATRICES = 3 * UNITS
MAX_JOBS = EXPERTS + 4
BIAS_W = 384
EXT = 512

VEC_MIX, VEC_FFN, VEC_FIN, VEC_CONV, VEC_STATE = 0, 16, 32, 40, 64
VECS = 80


def mixer_matrices(l):
    names = []
    for seg in ("v", "q", "k", "ua", "va", "cin", "gc", "gb"):
        names += [(seg, l, i) for i in range(2)]
    for h in range(2):
        for b in range(3):
            names += [("gate", l, 4 * b + 2 * h), ("gate", l, 4 * b + 2 * h + 1), ("branch", l, h, b)]
    names += [("out", l, i) for i in range(4)]
    return names


SEGMENT = {"ua": 0, "va": 1, "q": 2, "k": 3, "v": 4, "cin": 5, "gb": 6, "gc": 7, "gate": 8}


def weight_stream():
    names = mixer_matrices(0)
    for u in range(FF // UNIT + 1):
        if u < FF // UNIT:
            names += [("w1", u), ("w3", u)]
        if u:
            names += [("w2", u - 1)]
    names += mixer_matrices(1)
    return {n: i for i, n in enumerate(names)}


STREAM = weight_stream()
LEAD = len(STREAM)


def slot_of(i):
    return i % RING


def loads_of(i):
    return i // RING + 1


FEATURE_SEGMENTS = ("q", "k", "ua", "cin", "gc", "gb")


def split_order():
    order = []
    for l in range(2):
        order += [((seg, l, i), part) for seg in FEATURE_SEGMENTS for i in range(2) for part in range(2)]
        order += [(("gate", l, 4 * b + 2 * h + i), part) for h in range(2) for b in range(3)
                  for i in range(2) for part in range(2)]
        for u in range(DENSE_UNITS + 1 if l == 0 else 0):
            if u < DENSE_UNITS:
                order += [((w, u), b) for b in range(KB) for w in ("w1", "w3")]
            if u:
                order += [(("w2", u - 1), part) for part in range(2)]
    return order


def chunk_results(matrix, part):
    kind, at = matrix[0], matrix[1:]
    if kind in FEATURE_SEGMENTS:
        return [(kind, at[0], 2 * at[1] + part)]
    if kind == "gate":
        return [("gate", at[0], 12 * (at[1] // 2 % 2) + 4 * (at[1] // 4) + 2 * (at[1] % 2) + part)]
    if kind == "w2":
        return [("y", ("dense", at[0]), 4 * part + q) for q in range(4)]
    return [({"w1": "a", "w3": "g"}[kind], ("dense", at[0]), part)]


LEAD_ORDER = split_order()
LEAD_CHUNKS = len(LEAD_ORDER)
CHUNK_AT = {mp: c for c, mp in enumerate(LEAD_ORDER)}
CHUNK_OF = {name: c for c, mp in enumerate(LEAD_ORDER) for name in chunk_results(*mp)}


def lead_buffer(c):
    return (c - LEAD_CHUNKS) % CHUNKS


def mixer_groups(l):
    g = [("norm", 2 * l)]
    g += [("v", l, h, n) for h in range(2) for n in range(3)]
    g += [("q", l, j) for j in range(BT)] + [("k", l, j) for j in range(BT)]
    g += [("ua", l, j) for j in range(BT)]
    g += [("va", l, h, n) for h in range(2) for n in range(3)]
    g += [("s", l, h) for h in range(HEADS)] + [("s2", l, r) for r in range(2)]
    g += [(s, l, j) for s in ("cin", "gc", "gb") for j in range(BT)]
    g += [("mixed", l, j) for j in range(BT)]
    g += [("pt2", l, r) for r in range(2)]
    for b in range(BT):
        g += [("pt", l, 2 * b), ("pt", l, 2 * b + 1), ("pv", l, b)]
    for h in range(2):
        for b in range(3):
            g += [("gate", l, 12 * h + 4 * b + j) for j in range(4)]
            g += [("branch", l, h, b, j) for j in range(4)]
    g += [("out", l, j) for j in range(DT)]
    g += [("norm", 2 * l + 1)]
    return g


def groups_in(u):
    return [(s, u, b) for b in range(KB) for s in ("a", "g")]


def groups_out(u):
    return [("y", u, j) for j in range(DT)]


UNIT_AT = {"first": 0, "odd": 1, "next": 2, "last": UNITS - 1}
CHUNKS_IN = {"first": 4, "odd": 8, "next": 14, "last": JOB_CHUNKS - 4}


def counted(names):
    return len([n for n in names if n[0] != "ag" and n not in CHUNK_OF])


class Groups:

    def __init__(self):
        self.at, self.total, self.next, self.banks = {}, 0, 0, 8
        self.last = [[] for _ in range(8)]

    def add(self, names):
        for n in names:
            b, self.next = self.next, (self.next + 1) % self.banks
            self.at[n] = (b, self.total, list(self.last[b]))
            self.last[b] = [(n, "same")]
            self.total += counted([n])

    def close_loop(self, names, turns, back, end):
        for b in range(8):
            inside = [n for n in names if self.at[n][0] == b]
            if inside:
                self.at[inside[0]][2].append((inside[-1], back))
                self.last[b] = [(inside[-1], end)]
        self.total += (turns - 1) * counted(names)
        self.next = (self.at[names[-1]][0] + 1) % self.banks


def number_groups():
    g = Groups()
    g.add(mixer_groups(0))
    for u in range(DENSE_UNITS + 1):
        if u < DENSE_UNITS:
            g.add(groups_in(("dense", u)))
        if u:
            g.add(groups_out(("dense", u - 1)))
    g.add(mixer_groups(1))
    g.add([("logits",), ("counts",)] + [("htok", n, h) for n in range(3) for h in range(2)])
    g.next, g.banks = 0, 6
    g.add([("gather0", h) for h in range(2)])
    start = g.total
    g.add([("ag", "first"), ("tr", "first")])
    turn = [("ag", "odd"), ("tr", "odd"), ("ag", "next"), ("tr", "next")]
    g.add(turn)
    g.close_loop(turn, TURNS, "last_turn", "end_of_turns")
    g.add([("ag", "last"), ("tr", "last"), ("dwt", 0)] + [("gather", h) for h in range(2)])
    g.add([("scatter", j) for j in range(DT)])
    per_job = g.total - start
    g.close_loop([n for n in g.at if g.at[n][1] >= start], 1, "last_job", "last_job")
    g.total = start
    g.add([("norm", 4)])
    return g.at, counted(turn), per_job


GROUP, PER_TURN, PER_JOB = number_groups()


class Turns:

    def __init__(self):
        self.job = self.i = None
        self.ahead = False

    def value(self, base, per_job, per_turn=0):
        v = base + (per_job if self.ahead else 0)
        if self.job is not None and per_job:
            v = self.job * per_job + v
        if self.i is not None and per_turn:
            v = self.i * per_turn + v
        return v

    def full(self, name):
        return self.value(GROUP[name][1] + 1, PER_JOB, PER_TURN)

    def chunk(self, c, in_turn):
        return self.value(LEAD_CHUNKS + c, JOB_CHUNKS, 12 if in_turn else 0)


EXPERT_STREAM = [(0, 0), (1, 0),
                 (0, 1), (1, 1), (2, 0), (0, 2), (1, 2), (2, 1),
                 (0, UNITS - 1), (1, UNITS - 1), (2, UNITS - 2), (2, UNITS - 1)]


def last_uses():
    uses = []
    for n in STREAM:
        kind = n[0]
        if kind in ("va", "v"):
            uses.append((kind, n[1], n[2], 2))
        elif kind == "branch":
            uses.append(("branch", n[1], n[2], n[3], 3))
        elif kind == "gate":
            b, h, k = n[2] // 4, n[2] // 2 % 2, n[2] % 2
            uses.append(("gate", n[1], 12 * h + 4 * b + 2 * k + 1))
        elif kind in ("w1", "w3", "w2"):
            uses.append({"w1": ("a", ("dense", n[1]), KB - 1), "w3": ("g", ("dense", n[1]), KB - 1),
                         "w2": ("y", ("dense", n[1]), DT - 1)}[kind])
        else:
            uses.append((kind, n[1], 2 * n[2] + 1))
    return uses


LAST_USE = last_uses()
MIXER_SUMS = 2 * DT


def encoder(nc, x_t, vecs, w_in, cache_k_t, cache_v, ws_t, bs, g_v, bias_rev, w_branch, w_out,
            w1, w3, w2, router, router_b, e_w1, e_w3, e_w2, y_t, k_t, v_rows, z_state, vn_rows):
    f32, i32 = mybir.dt.float32, mybir.dt.int32
    ALU, ACT, AX = mybir.AluOpType, mybir.ActivationFunctionType, mybir.AxisListType
    ctx = ExitStack()
    with ctx:
        def sb(name, shape, dt=f32):
            return ctx.enter_context(nc.sbuf_tensor(name, shape, dt))

        def sem(name):
            return ctx.enter_context(nc.semaphore(name))

        bias_ext = nc.dram_tensor("bias_ext", [2, P, HEADS * EXT], f32).ap()

        ring = [sb(f"ring{i}", [P, 2048]) for i in range(RING)]
        x = sb("x", [P, DT, TOK])
        h = sb("h", [P, DT, TOK])
        rms = sb("rms", [P, TOK])
        rstd = sb("rstd", [P, TOK])
        eps = sb("eps", [P, 1])
        vec = sb("vec", [P, VECS])
        mean_w = sb("mean_w", [P, P])
        ident = sb("ident", [P, P])
        ones = sb("ones", [P, P])
        before = sb("before", [P, P])
        slot_id = sb("slot_id", [P, TOK])
        rank = sb("rank", [P, 3, EXPERTS])
        valid = sb("valid", [P, 3])
        rows6 = sb("rows6", [P, 6, HALF])
        vg = rows6[:, 0:3, :]
        v_tok = rows6[:, 3:6, :]
        vsq = sb("vsq", [P, 3])
        vrs = sb("vrs", [P, 3])
        q_t = sb("q_t", [P, BT, TOK])
        key_t = sb("key_t", [P, BT, TOK])
        spare0 = sb("spare0", [P, 2048])
        spare1 = sb("spare1", [P, 2112])
        ck_t = spare0[:, 0:1024].rearrange("p (a b) -> p a b", a=BT)
        cv = spare0[:, 1024:2048].rearrange("p (a b) -> p a b", a=2)
        wst = spare1[:, 0:512].rearrange("p (a b) -> p a b", a=BT)
        bsb = spare1[:, 512:1024].rearrange("p (a b) -> p a b", a=BT)
        gvb = spare1[:, 1024:1536]
        bias = sb("bias", [P, HEADS, BIAS_W])
        bias2 = spare1[:, 1536:2112].rearrange("p (a b) -> p a b", a=2)
        attn = sb("attn", [P, 4416])
        prob = attn[:, 0:3072].rearrange("p (h c) -> p h c", h=HEADS)
        prob2 = attn[:, 3072:3648].rearrange("p (h c) -> p h c", h=2)
        pt = attn[:, 3648:4416].rearrange("p (h c) -> p h c", h=2)
        top = sb("top", [P, 2 * HEADS + 2])
        total = sb("total", [P, 2 * HEADS + 2])
        part = sb("part", [P, 2 * HEADS + 2])
        pt2 = sb("pt2", [P, 2, 3, P])
        z = sb("z", [P, BT, TOK + 4])
        gate = sb("gate", [P, 4, TOK])
        a_t = sb("a_t", [P, BT, TOK])
        b_t = sb("b_t", [P, BT, TOK])
        c_t = sb("c_t", [P, BT, TOK])
        tmp = sb("tmp", [P, 2, TOK + 4])
        silu, hid = q_t, key_t
        e_silu = q_t[:, :, :].rearrange("p a b -> p (a b)")[:, 0:UNIT]
        e_hid = key_t[:, :, :].rearrange("p a b -> p (a b)")[:, 0:UNIT]
        f32r = mybir.dt.float32r
        w_hi = [sb(f"w_hi{i}", [P, CHUNK_W], f32r) for i in range(CHUNKS)]
        w_lo = [sb(f"w_lo{i}", [P, CHUNK_W], f32r) for i in range(CHUNKS)]
        h_split = [sb(n, [P, DT * TOK], f32r) for n in ("h_hi", "h_lo")]
        h_hi, h_lo = (t[:, :].rearrange("p (k t) -> p k t", k=DT) for t in h_split)
        he_hi, he_lo = (t[:, 0:DT * SLOT].rearrange("p (k t) -> p k t", k=DT) for t in h_split)
        hid_split = [sb(n, [P, KB * TOK], f32r) for n in ("hid_hi", "hid_lo")]
        hd_hi, hd_lo = (t[:, :].rearrange("p (k t) -> p k t", k=KB) for t in hid_split)
        hid_hi, hid_lo = (t[:, 0:KB * SLOT].rearrange("p (k t) -> p k t", k=KB) for t in hid_split)
        rw = sb("rw", [P, DT, EXPERTS])
        rb = sb("rb", [P, EXPERTS])
        place = sb("place", [P, 3, EXPERTS])
        weight = sb("weight", [P, 3, EXPERTS])
        job_expert = sb("job_expert", [1, MAX_JOBS + 1], i32)
        job_base = sb("job_base", [P, MAX_JOBS + 1])
        last_job_no = sb("last_job_no", [1, 1], i32)
        starts = sb("starts", [P, EXPERTS + 1])
        job_no = sb("job_no", [P, MAX_JOBS + 1])
        job_hit = sb("job_hit", [P, MAX_JOBS + 1, EXPERTS])
        rows_flat = rows6[:, :, :].rearrange("p a b -> p (a b)")
        sq = rows_flat[:, 0:DT * TOK].rearrange("p (a b) -> p a b", a=DT)
        m_t = q_t, key_t
        ext = attn[:, 0:HEADS * EXT].rearrange("p (h c) -> p h c", h=HEADS)
        h_tok = rows_flat[:, 0:3 * D].rearrange("p (n d) -> p n d", n=3)
        bias_flat = bias[:, :, :].rearrange("p a b -> p (a b)")
        zero_row = bias_flat[0:1, D:D + 512]
        y_tok = bias_flat[:, 0:D]
        spread = a_t[:, 0:3, 0:SLOT]
        wspread = b_t[:, 0:3, 0:SLOT]
        wspread_t = c_t[:, 0, :]
        rt = gate[:, 0, 0:288].rearrange("p (a n e) -> p a n e", a=12, n=3)
        rs = gate[:, 1, 0:24].rearrange("p (a n) -> p a n", a=8)
        expert_ring = ring + [spare0[:, :], spare1[:, 0:2048]]
        psum = ctx.enter_context(nc.psum_tensor("psum", [P, 8, 512], f32))

        slot_loaded = [sem(f"slot_loaded{i}") for i in range(EXPERT_RING)]
        bank_full = sem("bank_full")
        x_in = [sem("x_in0"), sem("x_in1")]
        vec_in = sem("vec_in")
        made = sem("made")
        dve_step = sem("dve_step")
        rms_ready = sem("rms_ready")
        rstd_ready = sem("rstd_ready")
        vrms_ready = sem("vrms_ready")
        vg_ready = sem("vg_ready")
        score_ready = sem("score_ready")
        gc_read = sem("gc_read")
        mixed_read = sem("mixed_read")
        branch_read = sem("branch_read")
        logits_read = sem("logits_read")
        sum_ready = sem("sum_ready")
        rows_stored = sem("rows_stored")
        keys_stored = sem("keys_stored")
        values_stored = sem("values_stored")
        state_stored = sem("state_stored")
        pool_step = sem("pool_step")
        zeroed = sem("zeroed")
        squared = sem("squared")
        h_ready = sem("h_ready")
        layer_in = [sem(f"layer_in{i}") for i in range(6)]
        ext_loaded = sem("ext_loaded")
        ext_ready = sem("ext_ready")
        ext_stored = sem("ext_stored")
        bias_loaded = sem("bias_loaded")
        bias2_loaded = sem("bias2_loaded")
        bias_masked = sem("bias_masked")
        mix_masked = sem("mix_masked")
        u_ready = sem("u_ready")
        vsq_ready = sem("vsq_ready")
        vn_ready = sem("vn_ready")
        qk_ready = sem("qk_ready")
        v_ready = sem("v_ready")
        top_ready = sem("top_ready")
        exp_ready = sem("exp_ready")
        prob_ready = sem("prob_ready")
        pt_ready = sem("pt_ready")
        pt2_ready = sem("pt2_ready")
        cin_ready = sem("cin_ready")
        z_ready = sem("z_ready")
        gate_ready = sem("gate_ready")
        a_ready = sem("a_ready")
        b_ready = sem("b_ready")
        c_ready = sem("c_ready")
        m_ready = sem("m_ready")
        x_ready = sem("x_ready")
        silu_ready = sem("silu_ready")
        hid_ready = sem("hid_ready")
        mask_ready = sem("mask_ready")
        gap_ready = sem("gap_ready")
        gap_exp = sem("gap_exp")
        count_ready = sem("count_ready")
        htok_ready = sem("htok_ready")
        spread_ready = sem("spread_ready")
        he_hi_ready = sem("he_hi_ready")
        he_ready = sem("he_ready")
        rounded = sem("rounded")
        split = sem("split")
        chunk_used = sem("chunk_used")
        h_rounded = sem("h_rounded")
        h_low_ready = sem("h_low_ready")
        hidden_split = sem("hidden_split")
        hid_hi_ready = sem("hid_hi_ready")
        jobs_ready = sem("jobs_ready")
        spread_t_ready = sem("spread_t_ready")
        ytok_ready = sem("ytok_ready")
        y_out = sem("y_out")
        out_done = sem("out_done")
        NORM_OF_LAYER = (0, 2)

        slot_before = [len([1 for i in range(LEAD) if slot_of(i) == s]) for s in range(EXPERT_RING)]
        GELU_BUFS = ((b_t, 0), (c_t, 0), (b_t, 2))

        FIRST_CHUNK = {0: 0, 1: CHUNK_AT[("w1", 0), 0], 2: CHUNK_AT[("q", 1, 0), 0]}

        def chunk_at(at, half):
            return at % EXPERT_RING, (2 * at + half) % CHUNKS

        def chunk_views(matrix, buf, slot, part):
            k, c = (KB, D) if matrix[0] == "w2" else (DT, UNIT)
            return (buf[:, :].rearrange("p (k c) -> p k c", k=k),
                    ring[slot][:, :].rearrange("p (k c) -> p k c", k=k)[:, :, part * (c // 2):(part + 1) * (c // 2)])

        def complete(name, turns):
            return (chunk_used, CHUNK_OF[name] + 1) if name in CHUNK_OF else (bank_full, turns.full(name))

        def bank(name, rows=P, cols=TOK, row0=0):
            return psum[row0:row0 + rows, GROUP[name][0], 0:cols]

        def reader(name):
            kind, at = name[0], name[1:]
            if kind in ("a", "g", "y"):
                (_, u), j = at
                n, ready = {"a": (KB, silu_ready), "g": (KB, hid_ready), "y": (DT, sum_ready)}[kind]
                return ready, n * u + j + 1, 0, 0
            if kind in ("ag", "tr"):
                u = at[0]
                per_turn = 4 if u in ("odd", "next") else 0
                return hid_ready, KB * DENSE_UNITS + 2 * UNIT_AT[u] + (1 if kind == "ag" else 2), 2 * UNITS, per_turn
            if kind == "branch":
                l, hf, b, j = at
                return branch_read, 24 * l + 12 * hf + 4 * b + j + 1, 0, 0
            if kind in ("va", "v"):
                l, hf, n = at
                return {"va": vg_ready, "v": v_ready}[kind], 6 * l + 3 * hf + n + 1, 0, 0
            if kind == "htok":
                return htok_ready, 2 * at[0] + at[1] + 1, 0, 0
            if kind == "gather0":
                return he_ready, at[0] + 1, 0, 0
            once = {"gather": (he_ready, 2, 2), "dwt": (spread_t_ready, 1, 0), "scatter": (x_ready, DT, MIXER_SUMS)}
            if kind in once:
                ready, n, base = once[kind]
                return ready, base + at[0] + 1, n, 0
            if kind in ("logits", "counts"):
                return {"logits": logits_read, "counts": count_ready}[kind], 1, 0, 0
            if kind == "norm":
                return rms_ready, at[0] + 1, 0, 0
            ready, per_layer, first = {
                "ua": (u_ready, BT, 0), "q": (qk_ready, 2 * BT, 0), "k": (qk_ready, 2 * BT, BT),
                "s": (score_ready, HEADS + 2, 0), "s2": (score_ready, HEADS + 2, HEADS),
                "cin": (cin_ready, BT, 0), "gc": (gc_read, BT, 0), "gb": (c_ready, BT, 0),
                "mixed": (mixed_read, BT, 0), "gate": (gate_ready, 24, 0), "pt2": (pt2_ready, 2, 0),
                "pt": (pt_ready, HEADS, 0), "pv": (b_ready, BT, 0), "out": (x_ready, DT, 0)}[kind]
            return ready, per_layer * at[0] + first + at[1] + 1, 0, 0

        block = ctx.enter_context(nc.Block())

        @block.sync
        def _(sp):
            lead_split = {STREAM[matrix]: c + 1 for c, (matrix, part) in enumerate(LEAD_ORDER) if part == 1}

            def load(i, dst, src):
                if i >= RING and i - RING in lead_split:
                    sp.wait_ge(split, lead_split[i - RING])
                elif i >= RING:
                    sp.wait_ge(bank_full, GROUP[LAST_USE[i - RING]][1] + 1)
                sp.dma_start(dst, src).then_inc(slot_loaded[slot_of(i)], 16)

            def tall(s, c=256):
                return ring[s][:, :].rearrange("p (k c) -> p k c", c=c)

            def mixer(l):
                for n in mixer_matrices(l):
                    i = STREAM[n]
                    s = slot_of(i)
                    if n[0] == "branch":
                        _, _, half, b = n
                        src = w_branch[l, b, :, half * 512:(half + 1) * 512]
                        load(i, tall(s, 512), src.rearrange("(k p) c -> p k c", p=P))
                    elif n[0] == "out":
                        load(i, tall(s), w_out[l, :, n[2] * 256:(n[2] + 1) * 256].rearrange("(k p) c -> p k c", p=P))
                    else:
                        c = SEGMENT[n[0]] * 512 + n[2] * 256
                        load(i, tall(s), w_in[l, :, c:c + 256].rearrange("(k p) c -> p k c", p=P))

            mixer(0)
            for u in range(DENSE_UNITS + 1):
                if u < DENSE_UNITS:
                    for k, w in enumerate((w1, w3)):
                        i = STREAM[("w1", u)] + k
                        load(i, tall(slot_of(i)), w[:, u * UNIT:(u + 1) * UNIT].rearrange("(k p) c -> p k c", p=P))
                if u:
                    i = STREAM[("w2", u - 1)]
                    load(i, tall(slot_of(i), D), w2[(u - 1) * UNIT:u * UNIT, :].rearrange("(k p) c -> p k c", p=P))
            mixer(1)

            def expert_matrix(e, m, unit):
                which = EXPERT_STREAM[m][0]
                s = m % EXPERT_RING
                dst = expert_ring[s][:, 0:2048].rearrange("p (k c) -> p k c", c=D if which == 2 else UNIT)
                cols = bass.ds(unit * UNIT, UNIT)
                src = e_w2[bass.ds(e, 1), cols, :] if which == 2 else (e_w1, e_w3)[which][bass.ds(e, 1), :, cols]
                sp.dma_start(dst, src.rearrange("o (k p) c -> p (o k) c", p=P)).then_inc(slot_loaded[s], 16)

            HEAD, TAIL = 2, 8

            def split_before(job, m, turn):
                at = m + JOB_MATRICES - len(EXPERT_STREAM) if m >= TAIL else m
                value = job * JOB_CHUNKS + (LEAD_CHUNKS + 2 * (at - EXPERT_RING + 1 + (0 if turn is None else EXPERT_RING)))
                sp.wait_ge(split, value if turn is None else turn * (2 * EXPERT_RING) + value)


            def other_matrices(job, e):
                for m in range(EXPERT_RING, TAIL):
                    split_before(job, m, None)
                    expert_matrix(e, m, EXPERT_STREAM[m][1])
                with sp.Fori(0, TURNS - 1) as i:
                    for m in range(HEAD, TAIL):
                        split_before(job, m, i)
                        expert_matrix(e, m, i * 2 + (2 + EXPERT_STREAM[m][1]))
                for m in range(TAIL, len(EXPERT_STREAM)):
                    split_before(job, m, None)
                    expert_matrix(e, m, EXPERT_STREAM[m][1])

            for m in range(EXPERT_RING):
                if m < RING:
                    last = max(i for i in range(LEAD) if slot_of(i) == m)
                    sp.wait_ge(bank_full, GROUP[LAST_USE[last]][1] + 1)
                else:
                    sp.wait_ge(a_ready, 2 * BT)
                    sp.wait_ge(b_ready, 2 * BT)
                expert_matrix(0, m, EXPERT_STREAM[m][1])
            sp.wait_ge(jobs_ready, 1)
            last_job = sp.value_load(last_job_no[0:1, 0:1], min_val=EXPERTS - 1, max_val=MAX_JOBS - 1)
            with sp.Fori(0, last_job) as job:
                e = sp.value_load(job_expert[0:1, bass.ds(job, 1)], min_val=0, max_val=EXPERTS - 1)
                other_matrices(job, e)
                e_next = sp.value_load(job_expert[0:1, bass.ds(job + 1, 1)], min_val=0, max_val=EXPERTS - 1)
                for m in range(EXPERT_RING):
                    sp.wait_ge(split, job * JOB_CHUNKS + (LEAD_CHUNKS + JOB_CHUNKS + 2 * (m - EXPERT_RING + 1)))
                    expert_matrix(e_next, m, EXPERT_STREAM[m][1])
            e = sp.value_load(job_expert[0:1, bass.ds(last_job, 1)], min_val=0, max_val=EXPERTS - 1)
            other_matrices(last_job, e)

        @block.gpsimd
        def _(pool):
            nc.gpsimd.memset(ident[:, :], 0.0).then_inc(pool_step, 1)
            nc.gpsimd.memset(ones[:, :], 1.0).then_inc(pool_step, 1)
            nc.gpsimd.memset(before[:, :], 1.0).then_inc(pool_step, 1)
            nc.gpsimd.iota(slot_id[:, :], pattern=[[1, TOK]], base=0, channel_multiplier=0,
                           allow_small_or_imprecise_dtypes=True).then_inc(made, 1)
            nc.gpsimd.iota(job_no[:, :], pattern=[[1, MAX_JOBS + 1]], base=0, channel_multiplier=0,
                           allow_small_or_imprecise_dtypes=True).then_inc(made, 1)
            nc.gpsimd.iota(rank[:, :, :], pattern=[[0, 3], [-1, EXPERTS]], base=EXPERTS, channel_multiplier=0,
                           allow_small_or_imprecise_dtypes=True).then_inc(made, 1)
            pool.wait_ge(pool_step, 3)
            nc.gpsimd.affine_select(out=ident[:, :], in_=ident[:, :], compare_op=ALU.not_equal, fill=1.0,
                                    base=0, pattern=[[-1, P]], channel_multiplier=1).then_inc(made, 1)
            nc.gpsimd.affine_select(out=before[:, :], in_=before[:, :], compare_op=ALU.is_gt, fill=0.0,
                                    base=0, pattern=[[1, P]], channel_multiplier=-1).then_inc(made, 1)

            def layer_inputs(l):
                if l:
                    pool.wait_ge(a_ready, BT)
                    pool.wait_ge(b_ready, BT)
                pool.dma_start(wst[:, :, :], ws_t[l]).then_inc(layer_in[0], 16)
                pool.dma_start(bsb[:, :, :].rearrange("p a b -> p (a b)"),
                               bs[l:l + 1, :].broadcast_to([P, HALF])).then_inc(layer_in[1], 16)
                pool.dma_start(gvb[:, :], g_v[l:l + 1, :].broadcast_to([P, HALF])).then_inc(layer_in[2], 16)
                pool.dma_start(ck_t[:, :, :], cache_k_t[l].rearrange("(j p) t -> p j t", p=P)).then_inc(layer_in[3], 16)
                pool.dma_start(cv[:, :, :], cache_v[l].rearrange("(n p) c -> p n c", p=P)).then_inc(layer_in[4], 16)

            def bias_rows():
                for l in range(2):
                    if l:
                        pool.wait_ge(ext_stored, 16 * l)
                    pool.dma_start(ext[:, :, EXT // 2 - 1:EXT - 1],
                                   bias_rev[l:l + 1, :, 0:TAB - 1].broadcast_to([P, HEADS, TAB - 1]),
                                   ).then_inc(ext_loaded, 16)
                    pool.wait_ge(ext_ready, l + 1)
                    pool.dma_start(bias_ext[l], ext.rearrange("p h c -> p (h c)")).then_inc(ext_stored, 16)

            def bias_tiles(l):
                row = HEADS * EXT
                pool.dma_start(bias[:, :, :], bass.AP(bias_ext.tensor, bias_ext[l].offset + 127,
                                                      [[row - 1, P], [EXT, HEADS], [1, BIAS_W]])
                               ).then_inc(bias_loaded, 16)
                for j in range(4):
                    for r in range(2):
                        head = 2 * j + r
                        pool.dma_start(bias2[32 * j:32 * j + 32, r, :],
                                       bass.AP(bias_ext.tensor, bias_ext[l].offset + head * EXT + 127,
                                               [[row - 1, DEC], [1, TOK]])).then_inc(bias2_loaded, 16)

            pool.dma_start(vec[:, :], vecs).then_inc(vec_in, 16)
            bias_rows()
            pool.wait_ge(ext_stored, 32)
            layer_inputs(0)
            bias_tiles(0)
            pool.dma_start(rw[:, :, :], router.rearrange("(k p) e -> p k e", p=P)).then_inc(layer_in[5], 16)
            pool.dma_start(rb[:, :], router_b.broadcast_to([P, EXPERTS])).then_inc(layer_in[5], 16)
            for l in range(2):
                pool.wait_ge(vn_ready, 3 * (l + 1))
                pool.dma_start(vn_rows[l], vg[0:DEC, 2, :]).then_inc(rows_stored, 16)
                pool.wait_ge(qk_ready, 8 * (l + 1))
                pool.dma_start(k_t[l].rearrange("(j p) t -> p j t", p=P), key_t[:, :, :]).then_inc(keys_stored, 16)
                pool.wait_ge(v_ready, 6 * (l + 1))
                pool.dma_start(v_rows[l, 0:SEQ, :].rearrange("(n p) c -> p n c", p=P),
                               v_tok[:, 0:2, :]).then_inc(values_stored, 16)
                pool.dma_start(v_rows[l, SEQ:TOK, :], v_tok[0:DEC, 2, :]).then_inc(values_stored, 16)
                pool.wait_ge(z_ready, BT * (l + 1))
                for at, to in ((SEQ, 0), (TOK + 2, 2)):
                    pool.dma_start(z_state[l, :, :, to:to + 2], z[:, :, at:at + 2]).then_inc(state_stored, 16)
                if l == 0:
                    layer_inputs(1)
                    bias_tiles(1)
            pool.wait_ge(y_out, DT)
            pool.dma_start(y_t.rearrange("(k p) t -> p k t", p=P), h[:, :, :]).then_inc(out_done, 16)
            pool.wait_ge(out_done, 16)
            pool.wait_ge(rows_stored, 32)
            pool.wait_ge(keys_stored, 32)
            pool.wait_ge(values_stored, 64)
            pool.wait_ge(state_stored, 64)

        @block.scalar
        def _(act):
            turns = Turns()
            x_dram = x_t.rearrange("(k p) t -> p k t", p=P)
            for k in range(2):
                act.dma_start(x[:, 4 * k:4 * k + 4, :], x_dram[:, 4 * k:4 * k + 4, :]).then_inc(x_in[k], 16)
            act.wait_ge(zeroed, 3)

            def round_lead(c):
                matrix, part = LEAD_ORDER[c]
                i = STREAM[matrix]
                act.wait_ge(slot_loaded[slot_of(i)], 16 * loads_of(i))
                if c >= CHUNKS:
                    act.wait_ge(chunk_used, c + 1 - CHUNKS)
                dst, src = chunk_views(matrix, w_hi[lead_buffer(c)], slot_of(i), part)
                nc.scalar.activation(dst, src, ACT.Copy).then_inc(rounded, 1)

            def round_h(n):
                for k in range(DT):
                    act.wait_ge(h_ready, DT * n + k + 1)
                    nc.scalar.activation(h_hi[:, k, :], h[:, k, :], ACT.Copy).then_inc(h_rounded, 1)

            def squares(n):
                if n in (1, 3):
                    act.wait_ge(rows_stored, 16 * (n // 2 + 1))
                    act.wait_ge(values_stored, 32 * (n // 2 + 1))
                for k in range(DT):
                    if n == 0:
                        act.wait_ge(x_in[k // 4], 16)
                    if n in (1, 3):
                        act.wait_ge(x_ready, DT * (n // 2) + k + 1)
                    elif n == 2:
                        act.wait_ge(sum_ready, DT * (DENSE_UNITS - 1) + k + 1)
                    elif n == 4:
                        act.wait_ge(x_ready, turns.job * DT + (MIXER_SUMS + k + 1))
                    nc.scalar.activation(sq[:, k, :], x[:, k, :], ACT.Square).then_inc(squared, 1)
                    if n == 1 and k >= DT - 3:
                        round_lead(FIRST_CHUNK[1] + k - (DT - 3))

            def root(n):
                turns.ahead = n == 4
                act.wait_ge(bank_full, turns.full(("norm", n)))
                turns.ahead = False
                nc.scalar.activation(rms[:, :], bank(("norm", n)), ACT.Sqrt, bias=eps[:, 0:1]).then_inc(rms_ready, 1)

            def evacuate(name, dst, rows, cols, done, func=ACT.Copy, scale=1.0):
                act.wait_ge(*complete(name, turns))
                nc.scalar.activation(dst, bank(name, rows, cols), func, scale=scale).then_inc(done, 1)

            for l in range(2):
                squares(NORM_OF_LAYER[l])
                root(NORM_OF_LAYER[l])
                round_h(NORM_OF_LAYER[l])
                for c in range(CHUNKS):
                    round_lead(CHUNK_AT[("q", l, 0), 0] + c)
                for hf in range(2):
                    for n, (t0, rows) in enumerate(TILES):
                        evacuate(("v", l, hf, n), v_tok[0:rows, n, hf * 256:(hf + 1) * 256], rows, 256, v_ready)
                for c in range(CHUNKS, 2 * CHUNKS):
                    round_lead(CHUNK_AT[("q", l, 0), 0] + c)
                for j in range(BT):
                    round_lead(CHUNK_OF[("ua", l, j)])
                for j in range(BT):
                    evacuate(("ua", l, j), a_t[:, j, :], P, TOK, u_ready, ACT.Gelu_apprx_tanh)
                    round_lead(CHUNK_OF[("cin", l, j)])
                for hf in range(2):
                    for n, (t0, rows) in enumerate(TILES):
                        evacuate(("va", l, hf, n), vg[0:rows, n, hf * 256:(hf + 1) * 256], rows, 256, vg_ready,
                                 ACT.Gelu_apprx_tanh)
                act.wait_ge(vg_ready, 6 * (l + 1))
                for n, (t0, rows) in enumerate(TILES):
                    spare, at = GELU_BUFS[n]
                    nc.scalar.activation(spare[0:rows, at:at + 2, 0:256], vg[0:rows, n, :].rearrange("p (a b) -> p a b", a=2),
                                         ACT.Square, accum_out=vsq[0:rows, n:n + 1]).then_inc(vsq_ready, 1)
                act.wait_ge(vsq_ready, 3 * (l + 1))
                for n, (t0, rows) in enumerate(TILES):
                    nc.scalar.activation(vrs[0:rows, n:n + 1], vsq[0:rows, n:n + 1], ACT.Sqrt, scale=1.0 / HALF,
                                         bias=eps[0:rows, 0:1]).then_inc(vrms_ready, 1)
                for hd in range(HEADS):
                    act.wait_ge(top_ready, 9 * l + hd + 1)
                    for t, (c0, c1) in enumerate(((0, 128), (128, 384))):
                        ins = nc.scalar.activation(prob[:, hd, c0:c1], prob[:, hd, c0:c1], ACT.Exp,
                                                   bias=top[:, 2 * hd + t:2 * hd + t + 1],
                                                   accum_out=total[:, 2 * hd + t:2 * hd + t + 1])
                    ins.then_inc(exp_ready, 1)
                act.wait_ge(top_ready, 9 * l + 9)
                for r in range(2):
                    ins = nc.scalar.activation(prob2[:, r, :], prob2[:, r, :], ACT.Exp,
                                               bias=top[:, 16 + r:17 + r], accum_out=total[:, 16 + r:17 + r])
                ins.then_inc(exp_ready, 1)
                if l:
                    act.wait_ge(state_stored, 32)
                for j in range(BT):
                    evacuate(("cin", l, j), z[:, j, 2:2 + TOK], P, TOK, cin_ready)
                    round_lead(CHUNK_OF[("gc", l, j)])
                for j in range(BT):
                    round_lead(CHUNK_OF[("gb", l, j)])
                gates = CHUNK_AT[("gate", l, 0), 0]
                for c in range(CHUNKS):
                    round_lead(gates + c)
                for r in range(2):
                    act.wait_ge(bank_full, turns.full(("pt2", l, r)))
                    src = bank(("pt2", l, r), P, 384).rearrange("p (a b) -> p a b", a=3)
                    nc.scalar.activation(pt2[:, r, 0:2, :], src[:, 0:2, :], ACT.Copy)
                    nc.scalar.activation(pt2[0:DEC, r, 2, :], src[0:DEC, 2, :], ACT.Copy).then_inc(pt2_ready, 1)
                for hd in range(HEADS):
                    if hd >= 2:
                        act.wait_ge(bank_full, turns.full(("pv", l, hd // 2 - 1)))
                    evacuate(("pt", l, hd), pt[:, hd % 2, :], P, 384, pt_ready)
                for g in range(24):
                    if g >= 4:
                        act.wait_ge(branch_read, 24 * l + g - 3)
                    evacuate(("gate", l, g), gate[:, g % 4, :], P, TOK, gate_ready, ACT.Tanh, scale=0.5)
                    if g + CHUNKS < 24:
                        round_lead(gates + g + CHUNKS)
                squares(2 * l + 1)
                root(2 * l + 1)
                if l == 0:
                    round_h(1)
                    first = FIRST_CHUNK[1]
                    for c in range(first + 3, first + 6 * DENSE_UNITS):
                        (w, u), b = LEAD_ORDER[c - CHUNKS] if c >= first + CHUNKS else ((None, None), None)
                        if w == "w1":
                            if u >= 2:
                                act.wait_ge(hid_ready, KB * (u - 2) + b + 1)
                            act.wait_ge(chunk_used, c + 1 - CHUNKS)
                            nc.scalar.activation(silu[:, KB * (u % 2) + b, :], bank(("a", ("dense", u), b)),
                                                 ACT.Silu).then_inc(silu_ready, 1)
                        round_lead(c)
            act.wait_ge(gap_ready, 1)
            nc.scalar.activation(rs[:, 5, :], rs[:, 4, :], ACT.Exp).then_inc(gap_exp, 1)
            for n, (t0, rows) in enumerate(TILES):
                for hf in range(2):
                    evacuate(("htok", n, hf), h_tok[0:rows, n, hf * 512:(hf + 1) * 512], rows, 512, htok_ready)
            def gathered(kind, hf):
                evacuate((kind, hf), he_hi[:, 4 * hf:4 * hf + 4, :].rearrange("p a b -> p (a b)"), P, 512, he_hi_ready)


            def round_chunk(at, half, in_turn=False):
                s, buf = chunk_at(at, half)
                act.wait_ge(slot_loaded[s], turns.value(16 * (slot_before[s] + at // EXPERT_RING + 1),
                                                        16 * JOB_MATRICES // EXPERT_RING, 16 if in_turn else 0))
                act.wait_ge(chunk_used, turns.chunk(2 * at + half + 1 - CHUNKS, in_turn))
                nc.scalar.activation(w_hi[buf][:, :], expert_ring[s][:, half * CHUNK_W:(half + 1) * CHUNK_W],
                                     ACT.Copy).then_inc(rounded, 1)

            def silu_unit(u):
                _, value, per_job, per_turn = reader(("ag", u))
                act.wait_ge(hid_ready, turns.value(value - 1, per_job, per_turn))
                act.wait_ge(chunk_used, turns.chunk(CHUNKS_IN[u], u in ("odd", "next")))
                nc.scalar.activation(e_silu, bank(("ag", u), P, UNIT), ACT.Silu).then_inc(silu_ready, 1)

            def hid_high(u):
                act.wait_ge(bank_full, turns.full(("tr", u)))
                nc.scalar.activation(hid_hi[:, :, :].rearrange("p a b -> p (a b)"), bank(("tr", u), P, KB * SLOT),
                                     ACT.Copy).then_inc(hid_hi_ready, 1)

            def next_chunks(first, end):
                turns.ahead = True
                for c in range(first, end):
                    round_chunk(c // 2, c % 2)
                turns.ahead = False

            def job_units(job, is_last):
                round_chunk(2, 0)
                round_chunk(2, 1)
                round_chunk(3, 0)
                silu_unit("first")
                round_chunk(3, 1)
                hid_high("first")
                with act.Fori(0, TURNS) as i:
                    turns.i = i
                    for first, u in ((4, "odd"), (7, "next")):
                        round_chunk(first, 0, True)
                        round_chunk(first, 1, True)
                        round_chunk(first + 1, 0, True)
                        silu_unit(u)
                        round_chunk(first + 1, 1, True)
                        if u == "odd":
                            round_chunk(first + 2, 0, True)
                            round_chunk(first + 2, 1, True)
                            hid_high(u)
                    round_chunk(9, 0, True)
                    round_chunk(9, 1, True)
                    hid_high("next")
                    turns.i = None
                round_chunk(JOB_MATRICES - 2, 0)
                round_chunk(JOB_MATRICES - 2, 1)
                round_chunk(JOB_MATRICES - 1, 0)
                silu_unit("last")
                round_chunk(JOB_MATRICES - 1, 1)
                hid_high("last")
                if not is_last:
                    next_chunks(0, 3)
                act.wait_ge(chunk_used, job * JOB_CHUNKS + (LEAD_CHUNKS + JOB_CHUNKS))
                for hf in range(2):
                    nc.scalar.activation(y_tok[:, hf * 512:(hf + 1) * 512], psum[:, 6 + hf, :], ACT.Copy).then_inc(ytok_ready, 1)
                if not is_last:
                    next_chunks(3, 4)
                for hf in range(2):
                    gathered("gather", hf)

            for c in range(4):
                round_chunk(c // 2, c % 2)
            for hf in range(2):
                gathered("gather0", hf)
            act.wait_ge(jobs_ready, 1)
            last_job = act.value_load(last_job_no[0:1, 0:1], min_val=EXPERTS - 1, max_val=MAX_JOBS - 1)
            with act.Fori(0, last_job) as job:
                turns.job = job
                job_units(job, False)
            turns.job = last_job
            job_units(last_job, True)
            squares(4)
            root(4)

        @block.vector
        def _(dve):
            turns = Turns()
            steps = [0]

            def done(ins):
                ins.then_inc(dve_step, 1)
                steps[0] += 1

            def settle():
                dve.wait_ge(dve_step, steps[0])

            def full(name):
                dve.wait_ge(*complete(name, turns))

            def norm(n, gain, dst):
                dve.wait_ge(rms_ready, n + 1)
                nc.vector.reciprocal(rstd[:, :], rms[:, :]).then_inc(rstd_ready, 1)
                dve.wait_ge(rstd_ready, n + 1)
                for k in range(DT):
                    ins = nc.vector.scalar_tensor_tensor(out=h[:, k, :], in0=x[:, k, :], scalar=vec[:, gain + k:gain + k + 1],
                                                         in1=rstd[:, :], op0=ALU.mult, op1=ALU.mult)
                    ins.then_inc(dst, 1)

            def low_lead(c):
                matrix, part = LEAD_ORDER[c]
                dve.wait_ge(rounded, c + 1)
                high, src = chunk_views(matrix, w_hi[lead_buffer(c)], slot_of(STREAM[matrix]), part)
                low, _ = chunk_views(matrix, w_lo[lead_buffer(c)], 0, part)
                nc.vector.tensor_tensor(low, src, high.bitcast(f32), ALU.subtract).then_inc(split, 1)

            def low_h(n):
                for k in range(DT):
                    dve.wait_ge(h_rounded, DT * n + k + 1)
                    nc.vector.tensor_tensor(h_lo[:, k, :], h[:, k, :], h_hi[:, k, :].bitcast(f32), ALU.subtract
                                            ).then_inc(h_low_ready, 1)

            def split_hidden(u):
                dve.wait_ge(hid_ready, KB * (u + 1))
                flat = hid[:, :, :].rearrange("p a b -> p (a b)")[:, KB * TOK * (u % 2):KB * TOK * (u % 2 + 1)]
                done(nc.vector.tensor_copy(hid_split[0][:, :], flat))
                settle()
                nc.vector.tensor_tensor(hid_split[1][:, :], flat, hid_split[0][:, :].bitcast(f32), ALU.subtract
                                        ).then_inc(hidden_split, 1)

            def after_dense(c):
                (w, u), part = LEAD_ORDER[c]
                if w == "w1":
                    return
                dve.wait_ge(chunk_used, c + 1)
                if w == "w3":
                    dve.wait_ge(silu_ready, KB * u + part + 1)
                    t = KB * (u % 2) + part
                    nc.vector.tensor_tensor(hid[:, t, :], silu[:, t, :], bank(("g", ("dense", u), part)),
                                            ALU.mult).then_inc(hid_ready, 1)
                    if (u, part) == (0, KB - 1):
                        split_hidden(0)
                else:
                    if part == 1 and u + 1 < DENSE_UNITS:
                        split_hidden(u + 1)
                    if part == 0 and u:
                        dve.wait_ge(sum_ready, DT * u)
                    for j in range(4 * part, 4 * part + 4):
                        nc.vector.tensor_tensor(x[:, j, :], x[:, j, :], bank(("y", ("dense", u), j)), ALU.add
                                                ).then_inc(sum_ready, 1)

            nc.vector.memset(psum[:, :, :], 0.0).then_inc(zeroed, 1)
            nc.vector.memset(eps[:, :], EPS).then_inc(zeroed, 1)
            nc.vector.memset(mean_w[:, :], 1.0 / D).then_inc(zeroed, 1)
            done(nc.vector.memset(valid[:, :], 1.0))
            done(nc.vector.memset(z[:, :, 0:2], 0.0))
            settle()
            done(nc.vector.memset(valid[:, 2:3], 0.0))
            settle()
            done(nc.vector.memset(valid[0:DEC, 2:3], 1.0))
            def extend_rows(l):
                dve.wait_ge(ext_loaded, 16 * (l + 1))
                done(nc.vector.tensor_copy(ext[:, :, 0:EXT // 2 - 1], ext[:, :, EXT // 2 - 1:EXT // 2].broadcast_to([P, HEADS, EXT // 2 - 1])))
                settle()
                nc.vector.memset(ext[:, :, EXT - 1:EXT], 0.0).then_inc(ext_ready, 1)

            dve.wait_ge(vec_in, 16)
            dve.wait_ge(made, 5)

            for l in range(2):
                norm(NORM_OF_LAYER[l], VEC_MIX + DT * l, h_ready)
                low_h(NORM_OF_LAYER[l])
                first = FIRST_CHUNK[NORM_OF_LAYER[l]]
                for c in range(CHUNKS):
                    low_lead(first + c)
                if l == 0:
                    for layer in range(2):
                        extend_rows(layer)
                for s, dst in (("q", q_t), ("k", key_t)):
                    for j in range(BT):
                        full((s, l, j))
                        nc.vector.tensor_copy(dst[:, j, :], bank((s, l, j))).then_inc(qk_ready, 1)
                        low_lead(CHUNK_OF[({"q": "k", "k": "ua"}[s], l, j)])
                for j in range(BT):
                    low_lead(CHUNK_OF[("cin", l, j)])
                dve.wait_ge(bias_loaded, 16 * (l + 1))
                nc.vector.memset(bias[0:CHUNK, :, 256 + CHUNK:BIAS_W], MASKED).then_inc(bias_masked, 1)
                dve.wait_ge(bias_masked, l + 1)
                for hd in range(HEADS):
                    full(("s", l, hd))
                    p = bank(("s", l, hd), P, 384)
                    nc.vector.scalar_tensor_tensor(out=prob[:, hd, 0:128], in0=p[:, 0:128], scalar=SCALE,
                                                   in1=bias[:, hd, 256:384], op0=ALU.mult, op1=ALU.add)
                    ins = nc.vector.scalar_tensor_tensor(out=prob[:, hd, 128:384], in0=p[:, 128:384], scalar=SCALE,
                                                         in1=bias[:, hd, 128:384], op0=ALU.mult, op1=ALU.add)
                    ins.then_inc(score_ready, 1)
                    dve.wait_ge(score_ready, 10 * l + hd + 1)
                    nc.vector.tensor_reduce(top[:, 2 * hd:2 * hd + 1], prob[:, hd, 0:128], AX.X, ALU.max, negate=True)
                    nc.vector.tensor_reduce(top[:, 2 * hd + 1:2 * hd + 2], prob[:, hd, 128:384], AX.X, ALU.max,
                                            negate=True).then_inc(top_ready, 1)
                dve.wait_ge(bias2_loaded, 16 * 8 * (l + 1))
                for r in range(2):
                    full(("s2", l, r))
                    ins = nc.vector.scalar_tensor_tensor(out=prob2[:, r, :], in0=bank(("s2", l, r)), scalar=SCALE,
                                                         in1=bias2[:, r, :], op0=ALU.mult, op1=ALU.add)
                    ins.then_inc(score_ready, 1)
                dve.wait_ge(score_ready, 10 * l + 10)
                nc.vector.tensor_reduce(top[:, 16:18], prob2[:, :, :], AX.X, ALU.max, negate=True).then_inc(top_ready, 1)

                dve.wait_ge(layer_in[0], 16 * (l + 1))
                nc.vector.memset(wst[CHUNK:P, :, 0:CHUNK], 0.0).then_inc(mix_masked, 1)
                dve.wait_ge(vrms_ready, 3 * (l + 1))
                for n, (t0, rows) in enumerate(TILES):
                    done(nc.vector.reciprocal(vrs[0:rows, n:n + 1], vrs[0:rows, n:n + 1]))
                settle()
                dve.wait_ge(layer_in[2], 16 * (l + 1))
                for n, (t0, rows) in enumerate(TILES):
                    nc.vector.scalar_tensor_tensor(out=vg[0:rows, n, :], in0=vg[0:rows, n, :], scalar=vrs[0:rows, n:n + 1],
                                                   in1=gvb[0:rows, :], op0=ALU.mult, op1=ALU.mult).then_inc(vn_ready, 1)

                for j in range(BT):
                    low_lead(CHUNK_OF[("gc", l, j)])
                for j in range(BT):
                    full(("gc", l, j))
                    dve.wait_ge(cin_ready, BT * l + j + 1)
                    ins = nc.vector.tensor_tensor(tmp[:, j % 2, 0:TOK], z[:, j, 2:2 + TOK], bank(("gc", l, j)), ALU.mult)
                    ins.then_inc(gc_read, 1)
                    dve.wait_ge(gc_read, BT * l + j + 1)
                    nc.vector.tensor_copy(z[:, j, 2:2 + SEQ], tmp[:, j % 2, 0:SEQ])
                    nc.vector.tensor_copy(z[:, j, SEQ + 4:TOK + 4], tmp[:, j % 2, SEQ:TOK])
                    st = VEC_STATE + 8 * l + 2 * j
                    nc.vector.tensor_copy(z[:, j, SEQ + 2:SEQ + 4], vec[:, st:st + 2]).then_inc(z_ready, 1)
                    low_lead(CHUNK_OF[("gb", l, j)])
                dve.wait_ge(z_ready, BT * (l + 1))
                gates = CHUNK_AT[("gate", l, 0), 0]
                for j in range(BT):
                    w = VEC_CONV + 12 * l + j
                    y = tmp[:, j % 2, 0:TOK + 2]
                    done(nc.vector.tensor_scalar(y, z[:, j, 0:TOK + 2], vec[:, w:w + 1], None, ALU.mult))
                    settle()
                    done(nc.vector.scalar_tensor_tensor(out=y, in0=z[:, j, 1:TOK + 3], scalar=vec[:, w + 4:w + 5], in1=y,
                                                        op0=ALU.mult, op1=ALU.add))
                    settle()
                    done(nc.vector.scalar_tensor_tensor(out=y, in0=z[:, j, 2:TOK + 4], scalar=vec[:, w + 8:w + 9], in1=y,
                                                        op0=ALU.mult, op1=ALU.add))
                    settle()
                    full(("gb", l, j))
                    p = bank(("gb", l, j))
                    nc.vector.tensor_tensor(c_t[:, j, 0:SEQ], y[:, 0:SEQ], p[:, 0:SEQ], ALU.mult)
                    ins = nc.vector.tensor_tensor(c_t[:, j, SEQ:TOK], y[:, SEQ + 2:TOK + 2], p[:, SEQ:TOK], ALU.mult)
                    ins.then_inc(c_ready, 1)
                    low_lead(gates + j)

                dve.wait_ge(layer_in[1], 16 * (l + 1))
                dve.wait_ge(u_ready, BT * (l + 1))
                for j in range(BT):
                    full(("mixed", l, j))
                    p = bank(("mixed", l, j))
                    b2 = bsb[:, j:j + 1, :].broadcast_to([P, 2, P])
                    nc.vector.tensor_tensor(tmp[:, j % 2, 0:SEQ].rearrange("p (a b) -> p a b", a=2),
                                            p[:, 0:SEQ].rearrange("p (a b) -> p a b", a=2), b2, ALU.add)
                    ins = nc.vector.tensor_tensor(tmp[:, j % 2, SEQ:TOK], p[:, SEQ:TOK], bsb[:, j, 0:DEC], ALU.add)
                    ins.then_inc(mixed_read, 1)
                    dve.wait_ge(mixed_read, BT * l + j + 1)
                    nc.vector.tensor_tensor(a_t[:, j, :], a_t[:, j, :], tmp[:, j % 2, 0:TOK], ALU.mult).then_inc(a_ready, 1)

                for hd in range(HEADS):
                    dve.wait_ge(exp_ready, 9 * l + hd + 1)
                    done(nc.vector.reciprocal(part[:, 2 * hd:2 * hd + 2], total[:, 2 * hd:2 * hd + 2]))
                dve.wait_ge(exp_ready, 9 * l + 9)
                done(nc.vector.reciprocal(part[:, 16:18], total[:, 16:18]))
                settle()
                for r in range(2):
                    ins = nc.vector.tensor_scalar(prob2[:, r, :], prob2[:, r, :], part[:, 16 + r:17 + r], None, ALU.mult)
                ins.then_inc(prob_ready, 1)
                for hd in range(HEADS):
                    for t, (c0, c1) in enumerate(((0, 128), (128, 384))):
                        ins = nc.vector.tensor_scalar(prob[:, hd, c0:c1], prob[:, hd, c0:c1],
                                                      part[:, 2 * hd + t:2 * hd + t + 1], None, ALU.mult)
                    ins.then_inc(prob_ready, 1)
                for b in range(BT):
                    full(("pv", l, b))
                    nc.vector.tensor_copy(b_t[:, b, :], bank(("pv", l, b))).then_inc(b_ready, 1)

                for hf in range(2):
                    for b in range(3):
                        for j in range(4):
                            if 12 * hf + 4 * b + j + CHUNKS < 24:
                                low_lead(gates + 12 * hf + 4 * b + j + CHUNKS)
                        for j in range(4):
                            name = ("branch", l, hf, b, j)
                            full(name)
                            g = 12 * hf + 4 * b + j
                            dve.wait_ge(gate_ready, 24 * l + g + 1)
                            if hf == 1 and b == 0 and j == 0:
                                dve.wait_ge(keys_stored, 16 * (l + 1))
                            dst = m_t[hf][:, j, :] if b == 0 else tmp[:, j % 2, 0:TOK]
                            ins = nc.vector.scalar_tensor_tensor(out=dst, in0=gate[:, g % 4, :], scalar=1.0, in1=bank(name),
                                                                 op0=ALU.add, op1=ALU.mult)
                            ins.then_inc(branch_read, 1)
                            if b:
                                dve.wait_ge(branch_read, 24 * l + 12 * hf + 4 * b + j + 1)
                                ins = nc.vector.tensor_tensor(m_t[hf][:, j, :], m_t[hf][:, j, :], tmp[:, j % 2, 0:TOK], ALU.add)
                            if b == 2:
                                ins.then_inc(m_ready, 1)
                for j in range(DT):
                    full(("out", l, j))
                    ins = nc.vector.scalar_tensor_tensor(out=x[:, j, :], in0=bank(("out", l, j)), scalar=0.5, in1=x[:, j, :],
                                                         op0=ALU.mult, op1=ALU.add)
                    ins.then_inc(x_ready, 1)
                dve.wait_ge(x_ready, DT * (l + 1))
                if l == 0:
                    for c in range(3):
                        low_lead(FIRST_CHUNK[1] + c)
                norm(2 * l + 1, VEC_FFN + DT * l, h_ready)
                if l == 0:
                    low_h(1)
                    first, end = FIRST_CHUNK[1], FIRST_CHUNK[1] + 6 * DENSE_UNITS
                    for c in range(first + 3, end + CHUNKS):
                        if c >= first + CHUNKS:
                            after_dense(c - CHUNKS)
                        if c < end:
                            low_lead(c)
                    dve.wait_ge(sum_ready, DT * DENSE_UNITS)

            LG, EQ, OH1, LG2, OH2, MASK, COMB, T0, TILES_OVER = range(9)

            def wide(a):
                return rs[:, a, :].rearrange("p (n o) -> p n o", o=1).broadcast_to([P, 3, EXPERTS])

            done(nc.vector.memset(rt[:, LG], 0.0))
            settle()
            dve.wait_ge(layer_in[5], 32)
            full(("logits",))
            p = bank(("logits",), P, 24).rearrange("p (n e) -> p n e", n=3)
            rb1 = rb[:, :].rearrange("p (o e) -> p o e", o=1)
            done(nc.vector.tensor_tensor(rt[:, LG, 0:2], p[:, 0:2, :], rb1.broadcast_to([P, 2, EXPERTS]), ALU.add))
            ins = nc.vector.tensor_tensor(rt[0:DEC, LG, 2], p[0:DEC, 2, :], rb[0:DEC, :], ALU.add)
            ins.then_inc(logits_read, 1)
            dve.wait_ge(logits_read, 1)

            def pick(src, top_at, key_at, hot):
                done(nc.vector.tensor_reduce(rs[:, top_at, :], rt[:, src], AX.X, ALU.max))
                settle()
                done(nc.vector.tensor_tensor(rt[:, EQ], rt[:, src], wide(top_at), ALU.is_equal))
                settle()
                done(nc.vector.tensor_tensor(rt[:, EQ], rt[:, EQ], rank[:, :, :], ALU.mult))
                settle()
                done(nc.vector.tensor_reduce(rs[:, key_at, :], rt[:, EQ], AX.X, ALU.max))
                settle()
                done(nc.vector.tensor_tensor(rt[:, hot], rt[:, EQ], wide(key_at), ALU.is_equal))
                settle()

            pick(LG, 0, 1, OH1)
            done(nc.vector.scalar_tensor_tensor(out=rt[:, LG2], in0=rt[:, OH1], scalar=-3.0e38, in1=rt[:, LG],
                                                op0=ALU.mult, op1=ALU.add))
            settle()
            pick(LG2, 2, 3, OH2)
            nc.vector.tensor_tensor(rs[:, 4, :], rs[:, 2, :], rs[:, 0, :], ALU.subtract).then_inc(gap_ready, 1)
            done(nc.vector.tensor_tensor(rt[:, MASK], rt[:, OH1], rt[:, OH2], ALU.add))
            settle()
            valid3 = valid[:, :].rearrange("p (n o) -> p n o", o=1).broadcast_to([P, 3, EXPERTS])
            ins = nc.vector.tensor_tensor(rt[:, MASK], rt[:, MASK], valid3, ALU.mult)
            ins.then_inc(mask_ready, 1)
            dve.wait_ge(gap_exp, 1)
            done(nc.vector.tensor_scalar(rs[:, 6, :], rs[:, 5, :], 1.0, None, ALU.add))
            settle()
            done(nc.vector.reciprocal(rs[:, 6, :], rs[:, 6, :]))
            settle()
            done(nc.vector.tensor_tensor(rs[:, 7, :], rs[:, 5, :], rs[:, 6, :], ALU.mult))
            settle()
            done(nc.vector.tensor_tensor(rt[:, COMB], rt[:, OH1], wide(6), ALU.mult))
            done(nc.vector.tensor_tensor(rt[:, T0], rt[:, OH2], wide(7), ALU.mult))
            settle()
            done(nc.vector.tensor_tensor(weight[:, :, :], rt[:, COMB], rt[:, T0], ALU.add))
            full(("counts",))
            pc = bank(("counts",), P, 32)
            done(nc.vector.scalar_tensor_tensor(out=rt[:, EQ], in0=pc[:, 0:24].rearrange("p (n e) -> p n e", n=3), scalar=1.0,
                                                in1=rt[:, MASK], op0=ALU.add, op1=ALU.mult))
            done(nc.vector.tensor_scalar(rt[:, TILES_OVER, 0], pc[:, 24:32], float(SLOT), None, ALU.is_gt))
            nc.vector.tensor_scalar(rt[:, TILES_OVER, 1], pc[:, 24:32], float(2 * SLOT), None, ALU.is_gt).then_inc(count_ready, 1)
            settle()
            done(nc.vector.tensor_scalar(place[:, :, :], rt[:, EQ], -1.0, None, ALU.add))
            done(nc.vector.memset(starts[:, 0:1], 0.0))
            done(nc.vector.memset(zero_row, 0.0))
            dve.wait_ge(count_ready, 1)
            done(nc.vector.scalar_tensor_tensor(out=rt[:, TILES_OVER, 2], in0=rt[:, TILES_OVER, 0], scalar=1.0, in1=rt[:, TILES_OVER, 1],
                                                op0=ALU.add, op1=ALU.add))
            settle()
            for e in range(EXPERTS):
                done(nc.vector.tensor_tensor(starts[:, e + 1:e + 2], starts[:, e:e + 1], rt[:, TILES_OVER, 2, e:e + 1], ALU.add))
                settle()
            slots = [P, MAX_JOBS + 1, EXPERTS]
            starts_wide = starts[:, 0:EXPERTS].rearrange("p (o e) -> p o e", o=1).broadcast_to(slots)
            done(nc.vector.tensor_tensor(job_hit[:, :, :], starts_wide,
                                         job_no[:, :].rearrange("p (j o) -> p j o", o=1).broadcast_to(slots), ALU.is_le))
            settle()
            done(nc.vector.tensor_reduce(job_base[:, :], job_hit[:, :, :], AX.X, ALU.add))
            settle()
            done(nc.vector.tensor_scalar(job_expert[0:1, :], job_base[0:1, :], -1.0, None, ALU.add))
            done(nc.vector.tensor_scalar(last_job_no[0:1, 0:1], starts[0:1, EXPERTS:EXPERTS + 1], -1.0, None, ALU.add))
            done(nc.vector.tensor_tensor(job_hit[:, :, :], job_hit[:, :, :], starts_wide, ALU.mult))
            settle()
            done(nc.vector.tensor_reduce(job_base[:, :], job_hit[:, :, :], AX.X, ALU.max))
            settle()
            done(nc.vector.tensor_tensor(job_base[:, :], job_no[:, :], job_base[:, :], ALU.subtract))
            settle()
            nc.vector.tensor_scalar(job_base[:, :], job_base[:, :], float(SLOT), None, ALU.mult).then_inc(jobs_ready, 1)
            dve.wait_ge(jobs_ready, 1)

            def hot_rows(dst, job, e):
                for n, (t0, rows) in enumerate(TILES):
                    nc.vector.tensor_scalar(dst[0:rows, n, :], slot_id[0:rows, 0:SLOT], job_base[0:rows, bass.ds(job, 1)],
                                            place[0:rows, n, bass.ds(e, 1)], ALU.add, ALU.is_equal).then_inc(spread_ready, 1)

            def low_chunk(at, half, in_turn=False):
                s, buf = chunk_at(at, half)
                dve.wait_ge(rounded, turns.chunk(2 * at + half + 1, in_turn))
                nc.vector.tensor_tensor(w_lo[buf][:, :], expert_ring[s][:, half * CHUNK_W:(half + 1) * CHUNK_W],
                                        w_hi[buf][:, :].bitcast(f32), ALU.subtract).then_inc(split, 1)

            def silu_times_g(u):
                dve.wait_ge(silu_ready, turns.value(KB * DENSE_UNITS + UNIT_AT[u] + 1, UNITS, 2 if u in ("odd", "next") else 0))
                nc.vector.tensor_tensor(e_hid, e_silu, psum[:, GROUP[("ag", u)][0], UNIT:2 * UNIT], ALU.mult).then_inc(hid_ready, 1)

            def hid_low(u):
                dve.wait_ge(hid_hi_ready, turns.value(UNIT_AT[u] + 1, UNITS, 2 if u in ("odd", "next") else 0))
                nc.vector.tensor_tensor(hid_lo[:, :, :].rearrange("p a b -> p (a b)"), bank(("tr", u), P, KB * SLOT),
                                        hid_hi[:, :, :].bitcast(f32).rearrange("p a b -> p (a b)"), ALU.subtract).then_inc(hid_ready, 1)

            def gathered_low(name, value):
                dve.wait_ge(he_hi_ready, value)
                tiles = slice(4 * name[1], 4 * name[1] + 4)
                nc.vector.tensor_tensor(he_lo[:, tiles, :].rearrange("p a b -> p (a b)"), bank(name, P, 512),
                                        he_hi[:, tiles, :].bitcast(f32).rearrange("p a b -> p (a b)"), ALU.subtract
                                        ).then_inc(he_ready, 1)

            hot_rows(spread, 0, 0)
            def next_chunks(first, end):
                turns.ahead = True
                for c in range(first, end):
                    low_chunk(c // 2, c % 2)
                turns.ahead = False

            def job_units(job, is_last):
                e = dve.value_load(job_expert[0:1, bass.ds(job, 1)], min_val=0, max_val=EXPERTS - 1)
                e_next = dve.value_load(job_expert[0:1, bass.ds(job + 1, 1)], min_val=0, max_val=EXPERTS - 1)
                low_chunk(2, 0)
                low_chunk(2, 1)
                low_chunk(3, 0)
                silu_times_g("first")
                low_chunk(3, 1)
                hid_low("first")
                hot_rows(spread, job + 1, e_next)
                hot_rows(wspread, job, e)
                dve.wait_ge(spread_ready, job * 9 + 9)
                for n, (t0, rows) in enumerate(TILES):
                    nc.vector.tensor_scalar(wspread[0:rows, n, :], wspread[0:rows, n, :], weight[0:rows, n, bass.ds(e, 1)],
                                            None, ALU.mult).then_inc(spread_ready, 1)
                with dve.Fori(0, TURNS) as i:
                    turns.i = i
                    for first, u in ((4, "odd"), (7, "next")):
                        low_chunk(first, 0, True)
                        low_chunk(first, 1, True)
                        low_chunk(first + 1, 0, True)
                        silu_times_g(u)
                        low_chunk(first + 1, 1, True)
                        if u == "odd":
                            low_chunk(first + 2, 0, True)
                            low_chunk(first + 2, 1, True)
                            hid_low(u)
                    low_chunk(9, 0, True)
                    low_chunk(9, 1, True)
                    hid_low("next")
                    turns.i = None
                low_chunk(JOB_MATRICES - 2, 0)
                low_chunk(JOB_MATRICES - 2, 1)
                low_chunk(JOB_MATRICES - 1, 0)
                silu_times_g("last")
                low_chunk(JOB_MATRICES - 1, 1)
                hid_low("last")
                if not is_last:
                    next_chunks(0, 3)
                full(("dwt", 0))
                nc.vector.tensor_copy(wspread_t, bank(("dwt", 0))).then_inc(spread_t_ready, 1)
                if not is_last:
                    next_chunks(3, 4)
                for hf in range(2):
                    gathered_low(("gather", hf), job * 2 + (hf + 3))
                dve.wait_ge(x_ready, job * DT + MIXER_SUMS)
                for j in range(DT):
                    full(("scatter", j))
                    nc.vector.tensor_tensor(x[:, j, :], x[:, j, :], bank(("scatter", j)), ALU.add).then_inc(x_ready, 1)

            for c in range(4):
                low_chunk(c // 2, c % 2)
            for hf in range(2):
                gathered_low(("gather0", hf), hf + 1)
            last_job = dve.value_load(last_job_no[0:1, 0:1], min_val=EXPERTS - 1, max_val=MAX_JOBS - 1)
            with dve.Fori(0, last_job) as job:
                turns.job = job
                job_units(job, False)
            turns.job = last_job
            job_units(last_job, True)
            dve.wait_ge(x_ready, last_job * DT + (MIXER_SUMS + DT))
            norm(4, VEC_FIN, y_out)

        @block.tensor
        def _(pe):
            turns = Turns()

            def take(name):
                for n, when in GROUP[name][2]:
                    ready, value, per_job, per_turn = reader(n)
                    if when == "last_turn":
                        value -= per_turn
                    if when == "end_of_turns":
                        value += (TURNS - 1) * per_turn
                    if when == "last_job":
                        value -= per_job
                    pe.wait_ge(ready, turns.value(value, per_job, 0 if when == "end_of_turns" else per_turn))

            def give(ins):
                ins.then_inc(bank_full, 1)

            def loaded(i):
                pe.wait_ge(slot_loaded[slot_of(i)], 16 * loads_of(i))

            def slab(s, c=256):
                return ring[s][:, :].rearrange("p (k c) -> p k c", c=c)

            def mean(n):
                take(("norm", n))
                for k in range(DT):
                    pe.wait_ge(squared, DT * n + k + 1)
                    ins = nc.tensor.matmul(bank(("norm", n)), mean_w[:, :], sq[:, k, :], start=(k == 0), stop=(k == DT - 1))
                give(ins)

            def rows_of(seg, l):
                for hf in range(2):
                    i = STREAM[(seg, l, hf)]
                    loaded(i)
                    w = slab(slot_of(i))
                    for n, (t0, rows) in enumerate(TILES):
                        take((seg, l, hf, n))
                        for k in range(DT):
                            if seg == "v" and hf + n == 0:
                                pe.wait_ge(h_ready, 2 * DT * l + k + 1)
                            ins = nc.tensor.matmul(bank((seg, l, hf, n), rows, 256), h[:, k, t0:t0 + rows], w[:, k, :],
                                                   start=(k == 0), stop=(k == DT - 1))
                        give(ins)

            def scores(l):
                pe.wait_ge(qk_ready, 8 * (l + 1))
                pe.wait_ge(layer_in[3], 16 * (l + 1))
                for hd in range(HEADS):
                    r0, j = DH * (hd % 2), hd // 2
                    q, k = q_t[r0:r0 + DH, j, :], key_t[r0:r0 + DH, j, :]
                    take(("s", l, hd))
                    p = bank(("s", l, hd), P, 384)
                    nc.tensor.matmul(p[:, 0:128], q[:, 0:128], k[:, 0:128], start=True, stop=True)
                    give(nc.tensor.matmul(p[:, 128:384], q[:, 128:256], k[:, 0:256], start=True, stop=True))
                for r in range(2):
                    take(("s2", l, r))
                    for j in range(4):
                        p = bank(("s2", l, r), DEC, TOK, 32 * j)
                        q = q_t[DH * r:DH * r + DH, j, SEQ:TOK]
                        nc.tensor.matmul(p[:, 0:PAST], q, ck_t[DH * r:DH * r + DH, j, :], start=True, stop=True,
                                         tile_position=(DH * r, 32 * j))
                        ins = nc.tensor.matmul(p[:, PAST:TOK], q, key_t[DH * r:DH * r + DH, j, SEQ:TOK], start=True, stop=True,
                                               tile_position=(DH * r, 32 * j))
                    give(ins)

            def mixed(l):
                pe.wait_ge(vn_ready, 3 * (l + 1))
                pe.wait_ge(mix_masked, l + 1)
                for j in range(BT):
                    take(("mixed", l, j))
                    for n, (t0, rows) in enumerate(TILES):
                        ins = nc.tensor.matmul(bank(("mixed", l, j))[:, t0:t0 + rows], vg[0:rows, n, j * P:(j + 1) * P],
                                               wst[0:rows, j, 0:rows], start=True, stop=True)
                    give(ins)

            def attention(l):
                pe.wait_ge(prob_ready, 9 * l + 1)
                for r in range(2):
                    take(("pt2", l, r))
                    for n, rows in enumerate((P, P, DEC)):
                        ins = nc.tensor.transpose(bank(("pt2", l, r), rows, 384)[:, n * P:(n + 1) * P],
                                                  prob2[:, r, n * P:n * P + rows], ident[:, :])
                    give(ins)
                for b in range(BT):
                    for hd in (2 * b, 2 * b + 1):
                        pe.wait_ge(prob_ready, 9 * l + hd + 2)
                        take(("pt", l, hd))
                        p = bank(("pt", l, hd), P, 384)
                        for n in range(3):
                            ins = nc.tensor.transpose(p[:, n * P:(n + 1) * P], prob[:, hd, n * P:(n + 1) * P], ident[:, :])
                        give(ins)
                    take(("pv", l, b))
                    if b == 0:
                        pe.wait_ge(v_ready, 6 * (l + 1))
                        pe.wait_ge(layer_in[4], 16 * (l + 1))
                        pe.wait_ge(pt2_ready, 2 * (l + 1))
                    for hd in (2 * b, 2 * b + 1):
                        pe.wait_ge(pt_ready, 8 * l + hd + 1)
                        p = bank(("pv", l, b), DH, TOK, DH * (hd % 2))
                        t, c = pt[:, hd % 2, :], slice(DH * hd, DH * hd + DH)
                        nc.tensor.matmul(p[:, 0:128], v_tok[:, 0, c], t[:, 0:128], start=True, stop=True)
                        nc.tensor.matmul(p[:, 128:256], v_tok[:, 0, c], t[:, 128:256], start=True, stop=False)
                        nc.tensor.matmul(p[:, 128:256], v_tok[:, 1, c], t[:, 256:384], start=False, stop=True)
                        r, j = hd % 2, hd // 2
                        q = slice(32 * j, 32 * j + 32)
                        nc.tensor.matmul(p[:, 256:288], cv[:, 0, c], pt2[:, r, 0, q], start=True, stop=False)
                        nc.tensor.matmul(p[:, 256:288], cv[:, 1, c], pt2[:, r, 1, q], start=False, stop=False)
                        ins = nc.tensor.matmul(p[:, 256:288], v_tok[0:DEC, 2, c], pt2[0:DEC, r, 2, q], start=False, stop=True)
                    give(ins)

            def features(seg, l):
                for j in range(BT):
                    lead_chunk(CHUNK_OF[(seg, l, j)])

            def branches(l):
                for hf in range(2):
                    for b, (src, ready) in enumerate(((a_t, a_ready), (b_t, b_ready), (c_t, c_ready))):
                        for j in range(4):
                            lead_chunk(CHUNK_OF[("gate", l, 12 * hf + 4 * b + j)])
                        i = STREAM[("branch", l, hf, b)]
                        loaded(i)
                        w = slab(slot_of(i), 512)
                        pe.wait_ge(ready, BT * (l + 1))
                        for j in range(4):
                            take(("branch", l, hf, b, j))
                            for k in range(BT):
                                ins = nc.tensor.matmul(bank(("branch", l, hf, b, j)), w[:, k, j * P:(j + 1) * P], src[:, k, :],
                                                       start=(k == 0), stop=(k == BT - 1))
                            give(ins)

            def project_out(l):
                for j in range(DT):
                    i = STREAM[("out", l, j // 2)]
                    loaded(i)
                    w = slab(slot_of(i))
                    take(("out", l, j))
                    for k in range(DT):
                        if j == 0:
                            pe.wait_ge(m_ready, DT * l + k + 1)
                        ins = nc.tensor.matmul(bank(("out", l, j)), w[:, k, (j % 2) * P:(j % 2 + 1) * P], m_t[k // 4][:, k % 4, :],
                                               start=(k == 0), stop=(k == DT - 1))
                    give(ins)

            def lead_chunk(c):
                matrix, part = LEAD_ORDER[c]
                pe.wait_ge(split, c + 1)
                hi, _ = chunk_views(matrix, w_hi[lead_buffer(c)], 0, part)
                lo, _ = chunk_views(matrix, w_lo[lead_buffer(c)], 0, part)
                w, src = matrix[0], (h_hi, h_lo)
                if w == "w2":
                    pe.wait_ge(hidden_split, matrix[1] + 1)
                    src = hd_hi, hd_lo
                norms = [n for n in FIRST_CHUNK if FIRST_CHUNK[n] == c]
                names = chunk_results(matrix, part)
                for q, name in enumerate(names):
                    take(name)
                    tiles = KB if w == "w2" else DT
                    for k in range(tiles):
                        for n in norms:
                            pe.wait_ge(h_low_ready, DT * n + k + 1)
                        high, low = hi[:, k, q * P:(q + 1) * P], lo[:, k, q * P:(q + 1) * P]
                        nc.tensor.matmul(bank(name), high, src[0][:, k, :], start=(k == 0), stop=False)
                        nc.tensor.matmul(bank(name), high, src[1][:, k, :], start=False, stop=False)
                        ins = nc.tensor.matmul(bank(name), low, src[0][:, k, :], start=False, stop=(k == tiles - 1))
                ins.then_inc(chunk_used, 1)

            pe.wait_ge(zeroed, 3)
            pe.wait_ge(made, 5)
            for l in range(2):
                mean(NORM_OF_LAYER[l])
                rows_of("v", l)
                features("q", l)
                features("k", l)
                features("ua", l)
                rows_of("va", l)
                scores(l)
                features("cin", l)
                features("gc", l)
                features("gb", l)
                mixed(l)
                attention(l)
                branches(l)
                project_out(l)
                mean(2 * l + 1)
                if l == 0:
                    for c in range(FIRST_CHUNK[1], FIRST_CHUNK[1] + 6 * DENSE_UNITS):
                        lead_chunk(c)

            pe.wait_ge(h_ready, DT * 4)
            pe.wait_ge(layer_in[5], 32)
            take(("logits",))
            for n, (t0, rows) in enumerate(TILES):
                for k in range(DT):
                    ins = nc.tensor.matmul(bank(("logits",), rows, 24)[:, 8 * n:8 * n + 8], h[:, k, t0:t0 + rows], rw[:, k, :],
                                           start=(k == 0), stop=(k == DT - 1))
            give(ins)

            def place_tokens():
                pe.wait_ge(mask_ready, 1)
                take(("counts",))
                p = bank(("counts",), P, 32)
                for n in range(3):
                    for k in range(n + 1):
                        nc.tensor.matmul(p[:, 8 * n:8 * n + 8], before[:, :] if k == n else ones[:, :], rt[:, 5, k],
                                         start=(k == 0), stop=(k == n))
                for k in range(3):
                    ins = nc.tensor.matmul(p[:, 24:32], ones[:, :], rt[:, 5, k], start=(k == 0), stop=(k == 2))
                give(ins)

            place_tokens()
            for n, (t0, rows) in enumerate(TILES):
                for hf in range(2):
                    take(("htok", n, hf))
                    for k in range(4):
                        ins = nc.tensor.transpose(bank(("htok", n, hf), rows, 512)[:, k * P:(k + 1) * P],
                                                  h[:, 4 * hf + k, t0:t0 + rows], ident[:, :])
                    give(ins)
            pe.wait_ge(htok_ready, 6)
            pe.wait_ge(count_ready, 1)

            def gather(kind, tiles=4):
                for hf in range(2):
                    take((kind, hf))
                    for j in range(tiles):
                        at = (4 * hf + j) * P
                        for n, (t0, rows) in enumerate(TILES):
                            ins = nc.tensor.matmul(bank((kind, hf), P, 512)[:, j * P:(j + 1) * P], h_tok[0:rows, n, at:at + P],
                                                   spread[0:rows, n, :], start=(n == 0), stop=(n == 2))
                    give(ins)

            def split_chunk(at, half, in_turn):
                c = 2 * at + half
                pe.wait_ge(split, turns.chunk(c + 1, in_turn))
                return w_hi[c % CHUNKS], w_lo[c % CHUNKS]

            def unit_rows(u, at):
                in_turn = u in ("odd", "next")
                take(("ag", u))
                out = bank(("ag", u), P, 2 * UNIT)
                for m in range(2):
                    p = out[:, m * UNIT:(m + 1) * UNIT]
                    for half in range(2):
                        hi, lo = split_chunk(at + m, half, in_turn)
                        for q in range(4):
                            k = 4 * half + q
                            w_high, w_low = hi[:, q * UNIT:(q + 1) * UNIT], lo[:, q * UNIT:(q + 1) * UNIT]
                            nc.tensor.matmul(p, he_hi[:, k, :], w_high, start=(k == 0), stop=False)
                            nc.tensor.matmul(p, he_hi[:, k, :], w_low, start=False, stop=False)
                            ins = nc.tensor.matmul(p, he_lo[:, k, :], w_high, start=False, stop=(k == DT - 1))
                        ins.then_inc(chunk_used, 1)

            def transpose_hidden(u):
                take(("tr", u))
                _, value, per_job, per_turn = reader(("ag", u))
                pe.wait_ge(hid_ready, turns.value(value, per_job, per_turn))
                for b in range(KB):
                    ins = nc.tensor.transpose(bank(("tr", u), P, 512)[:, b * P:(b + 1) * P], e_hid[:, b * P:(b + 1) * P], ident[:, :])
                give(ins)

            def unit_down(u, at):
                _, value, per_job, per_turn = reader(("tr", u))
                if (u, at) == ("next", JOB_MATRICES - 2):
                    value += (TURNS - 1) * per_turn
                before_turn = u == "next" and at == 4
                in_turn = at in (4, 7)
                pe.wait_ge(hid_ready, turns.value(value - (per_turn if before_turn else 0), per_job, per_turn if in_turn else 0))
                for b in range(KB):
                    hi, lo = split_chunk(at, b, in_turn)
                    last = u == "last" and b == KB - 1
                    for h_part, w_part in ((hid_hi, hi), (hid_hi, lo), (hid_lo, hi)):
                        for hf in range(2):
                            ins = nc.tensor.matmul(psum[:, 6 + hf, :], h_part[:, b, :], w_part[:, hf * 512:(hf + 1) * 512],
                                                   start=False, stop=(last and h_part is hid_lo))
                    ins.then_inc(chunk_used, 1)

            pe.wait_ge(spread_ready, 3)
            gather("gather0")
            pe.wait_ge(jobs_ready, 1)
            last_job = pe.value_load(last_job_no[0:1, 0:1], min_val=EXPERTS - 1, max_val=MAX_JOBS - 1)

            def job_units(job, is_last):
                pe.wait_ge(he_ready, job * 2 + 2)
                for hf in range(2):
                    nc.tensor.matmul(psum[:, 6 + hf, :], zero_row[:, 0:P], zero_row, start=True, stop=False)
                unit_rows("first", 0)
                transpose_hidden("first")
                with pe.Fori(0, TURNS) as i:
                    turns.i = i
                    unit_rows("odd", 2)
                    unit_down("next", 4)
                    transpose_hidden("odd")
                    unit_rows("next", 5)
                    unit_down("odd", 7)
                    transpose_hidden("next")
                    turns.i = None
                unit_rows("last", JOB_MATRICES - 4)
                unit_down("next", JOB_MATRICES - 2)
                transpose_hidden("last")
                unit_down("last", JOB_MATRICES - 1)
                pe.wait_ge(spread_ready, job * 9 + 12)
                take(("dwt", 0))
                for n, (t0, rows) in enumerate(TILES):
                    ins = nc.tensor.transpose(bank(("dwt", 0))[:, t0:t0 + rows], wspread[0:rows, n, :], ident[0:rows, 0:rows])
                give(ins)
                gather("gather", 1 if is_last else 4)
                pe.wait_ge(ytok_ready, job * 2 + 2)
                pe.wait_ge(spread_t_ready, job + 1)
                for j in range(DT):
                    take(("scatter", j))
                    give(nc.tensor.matmul(bank(("scatter", j)), y_tok[:, j * P:(j + 1) * P], wspread_t, start=True, stop=True))

            with pe.Fori(0, last_job) as job:
                turns.job = job
                job_units(job, False)
            turns.job = last_job
            job_units(last_job, True)
            turns.ahead = True
            mean(4)


def kernel(**inputs):
    import concourse.bacc as _bacc
    from concourse.bass_utils import run_bass_kernel_spmd as _run

    a = {k: np.asarray(v) for k, v in inputs.items()}

    def columns(v):
        return v.reshape(-1, P).T

    vecs = np.concatenate([
        columns(a["norm_mix_g"]), columns(a["norm_ffn_g"]), columns(a["final_norm_g"]),
        columns(a["conv_w"]),
        a["state_conv"].reshape(2, 2, BT, P).transpose(3, 0, 2, 1).reshape(P, 16)], axis=1)
    arrays = {
        "x_t": np.concatenate([a["x_prompt"][0], a["x_sample"][0]], axis=0).T,
        "vecs": vecs,
        "w_in": a["w_in"],
        "cache_k_t": a["cache_attn_k"].reshape(2, PAST, HALF).transpose(0, 2, 1),
        "cache_v": a["cache_attn_v"].reshape(2, PAST, HALF),
        "ws_t": a["gmlp_ws"].transpose(0, 3, 1, 2),
        "bs": a["gmlp_bs"].reshape(2, HALF),
        "g_v": a["gmlp_norm_g"],
        "bias_rev": a["attn_rel_bias"][:, :, ::-1],
        "w_branch": a["w_branch"],
        "w_out": a["w_out"],
        "w1": a["ffn_w1"][0], "w3": a["ffn_w3"][0], "w2": a["ffn_w2"][0],
        "router": a["moe_router"][0], "router_b": a["moe_router_b"],
        "e_w1": a["moe_w1"][0], "e_w3": a["moe_w3"][0], "e_w2": a["moe_w2"][0],
    }
    outs = {"y_t": (D, TOK), "k_t": (2, HALF, TOK), "v_rows": (2, TOK, HALF), "z_state": (2, P, BT, 4),
            "vn_rows": (2, DEC, HALF)}
    nc = _bacc.Bacc("TRN2", target_bir_lowering=False, num_devices=1)
    feed, args = {}, {}
    for name, v in arrays.items():
        v = np.ascontiguousarray(v)
        feed[f"in_{name}"] = v
        args[name] = nc.dram_tensor(f"in_{name}", v.shape, mybir.dt.from_np(v.dtype), kind="ExternalInput").ap()
    for name, shape in outs.items():
        args[name] = nc.dram_tensor(f"out_{name}", shape, mybir.dt.float32, kind="ExternalOutput").ap()
    encoder(nc, **args)
    r = _run(nc, [feed], core_ids=[0]).results[0]
    y, kt, vr = r["out_y_t"].T, r["out_k_t"].transpose(0, 2, 1), r["out_v_rows"]
    zs = r["out_z_state"].transpose(0, 3, 2, 1).reshape(2, 4, HALF)
    k5, v5 = (t.reshape(2, 1, TOK, HEADS, DH) for t in (kt, vr))
    c = np.ascontiguousarray
    return (c(y[None, :SEQ]), c(y[None, SEQ:]), c(k5[:, :, :SEQ]), c(v5[:, :, :SEQ]), c(zs[:, None, 0:2]),
            c(k5[:, :, SEQ:]), c(v5[:, :, SEQ:]), c(zs[:, None, 2:4]), c(r["out_vn_rows"][:, None]))
```
